# Optimizing a Trainium2 kernel written in Bass

```python
import math
import jax
import jax.numpy as jnp
from jax import lax
import numpy as np

D_MODEL = 1024
BATCH = 1
SEQ = 256
DEPTH = 2

N_MIXERS = 4
NORM_EPS = 1e-6
Q_BLOCK = 128
ROPE_THETA = 10000.0
FFN_HIDDEN = -(-(8 * D_MODEL // 3) // 256) * 256

HEAD_DIM = 64
NSA_HEADS = D_MODEL // HEAD_DIM
NSA_GROUPS = 4
NSA_CMP_STRIDE = 16
NSA_CMP_LEN = 2 * NSA_CMP_STRIDE
NSA_CMP_HIDDEN = 4 * HEAD_DIM
NSA_SEL_LEN = 64
NSA_N_SEL = 16
NSA_N_LOCAL = 2
NSA_WINDOW = 512
NSA_IN = NSA_HEADS * HEAD_DIM + 6 * NSA_GROUPS * HEAD_DIM + 3 * NSA_HEADS

MLA_HEADS = D_MODEL // 64
MLA_Q_LORA = 3 * D_MODEL // 8
MLA_KV_LORA = D_MODEL // 4
MLA_NOPE = 64
MLA_ROPE = 32
MLA_V = 64
MLA_IN = MLA_Q_LORA + MLA_KV_LORA + MLA_ROPE

RET_HEADS = D_MODEL // 256
RET_QK = 256
RET_V = 2 * RET_QK
RET_CHUNK = 128
RET_IN = 2 * RET_HEADS * RET_QK + 2 * RET_HEADS * RET_V

SSD_INNER = 2 * D_MODEL
SSD_HEADDIM = 64
SSD_HEADS = SSD_INNER // SSD_HEADDIM
SSD_GROUPS = 4
SSD_STATE = 128
SSD_CONV = 4
SSD_CHUNK = 128
SSD_CONV_CH = SSD_INNER + 2 * SSD_GROUPS * SSD_STATE
SSD_IN = SSD_INNER + SSD_CONV_CH + SSD_HEADS

kernel_name = 'hybrid_nsa_mla_retnet_ssd_trunk'

def _n_kind(m):
    return (DEPTH - m + N_MIXERS - 1) // N_MIXERS

def _rms(x, g, eps=NORM_EPS):
    xf = x.astype(jnp.float32)
    y = xf * lax.rsqrt(jnp.mean(jnp.square(xf), axis=-1, keepdims=True) + eps)
    return (y * g.astype(jnp.float32)).astype(x.dtype)

def _masked_softmax(s, mask):
    s = jnp.where(mask, s.astype(jnp.float32), -jnp.inf)
    m = jnp.max(s, axis=-1, keepdims=True)
    m = jnp.where(jnp.isfinite(m), m, 0.0)
    p = jnp.exp(s - m)
    return p / jnp.maximum(jnp.sum(p, axis=-1, keepdims=True), 1e-30)

def _rope(x, pos):
    d = x.shape[-1]
    inv = ROPE_THETA ** (-jnp.arange(0, d, 2, dtype=jnp.float32) / d)
    ang = pos.astype(jnp.float32)[..., None] * inv
    cos = jnp.cos(ang)[:, :, None, :]
    sin = jnp.sin(ang)[:, :, None, :]
    xf = x.astype(jnp.float32)
    x1, x2 = xf[..., : d // 2], xf[..., d // 2:]
    return jnp.concatenate([x1 * cos - x2 * sin, x1 * sin + x2 * cos], axis=-1).astype(x.dtype)

def _nsa_mixer(h, w_in, q_norm, k_norm, cmp_pe, cmp_w1, cmp_w2, w_out):
    B, S, _ = h.shape
    H, G, Dh = NSA_HEADS, NSA_GROUPS, HEAD_DIM
    R = H // G
    kvw = G * Dh
    parts = jnp.split(h @ w_in, np.cumsum([H * Dh] + [kvw] * 6).tolist(), axis=-1)
    q, k_c, v_c, k_s, v_s, k_w, v_w, gate = parts
    q = _rms(q.reshape(B, S, G, R, Dh), q_norm)
    k_c, v_c, k_s, v_s, k_w, v_w = (t.reshape(B, S, G, Dh) for t in (k_c, v_c, k_s, v_s, k_w, v_w))
    gate = jax.nn.sigmoid(gate.astype(jnp.float32)).reshape(B, S, G, R, 3)

    n_cmp = S // NSA_CMP_STRIDE - 1

    def compress(t, pe, w1, w2):
        ch = t.reshape(B, S // NSA_CMP_STRIDE, NSA_CMP_STRIDE, G, Dh)
        blk = jnp.concatenate([ch[:, :-1], ch[:, 1:]], axis=2) + pe[:, None, :]
        flat = jnp.swapaxes(blk, 2, 3).reshape(B, n_cmp, G, NSA_CMP_LEN * Dh)
        return jax.nn.silu(flat @ w1) @ w2

    k_cmp = _rms(compress(k_c, cmp_pe[0], cmp_w1[0], cmp_w2[0]), k_norm[0])
    v_cmp = compress(v_c, cmp_pe[1], cmp_w1[1], cmp_w2[1])
    cmp_end = jnp.arange(n_cmp) * NSA_CMP_STRIDE + NSA_CMP_LEN - 1

    n_blk = S // NSA_SEL_LEN
    top = min(NSA_N_SEL, n_blk)
    ratio = NSA_SEL_LEN // NSA_CMP_STRIDE
    k_sel = _rms(k_s, k_norm[1]).reshape(B, n_blk, NSA_SEL_LEN, G, Dh).transpose(0, 3, 1, 2, 4)
    v_sel = v_s.reshape(B, n_blk, NSA_SEL_LEN, G, Dh).transpose(0, 3, 1, 2, 4)
    blk_ids = jnp.arange(n_blk)
    bi = jnp.arange(B)[:, None, None, None]
    gi = jnp.arange(G)[None, :, None, None]

    pad = ((0, 0), (NSA_WINDOW, 0), (0, 0), (0, 0))
    k_win = jnp.pad(_rms(k_w, k_norm[2]), pad)
    v_win = jnp.pad(v_w, pad)
    scale = Dh ** -0.5

    def block(qb):
        q0 = qb * Q_BLOCK
        tpos = q0 + jnp.arange(Q_BLOCK)
        qi = lax.dynamic_slice_in_dim(q, q0, Q_BLOCK, axis=1)
        gb = lax.dynamic_slice_in_dim(gate, q0, Q_BLOCK, axis=1)
        s = jnp.einsum('bqgrd,bcgd->bgrqc', qi, k_cmp) * scale
        p_cmp = _masked_softmax(s, cmp_end[None, :] <= tpos[:, None])
        o_cmp = jnp.einsum('bgrqc,bcgd->bqgrd', p_cmp.astype(v_cmp.dtype), v_cmp)
        imp = jnp.pad(p_cmp.sum(axis=2), ((0, 0), (0, 0), (0, 0), (1, 1)))
        imp = imp[..., : ratio * n_blk].reshape(B, G, Q_BLOCK, n_blk, ratio).sum(-1) + imp[..., ratio::ratio]
        cur = tpos // NSA_SEL_LEN
        causal_blk = blk_ids[None, :] <= cur[:, None]
        forced = causal_blk & ((blk_ids[None, :] == 0) | (blk_ids[None, :] > cur[:, None] - NSA_N_LOCAL))
        score = jnp.where(forced, jnp.inf, jnp.where(causal_blk, imp, -jnp.inf))
        _, idx = lax.top_k(score, top)
        ks_g = k_sel[bi, gi, idx]
        vs_g = v_sel[bi, gi, idx]
        tok = idx[..., None] * NSA_SEL_LEN + jnp.arange(NSA_SEL_LEN)
        smask = (tok <= tpos[None, None, :, None, None]).reshape(B, G, 1, Q_BLOCK, top * NSA_SEL_LEN)
        s = jnp.einsum('bqgrd,bgqnld->bgrqnl', qi, ks_g).reshape(B, G, R, Q_BLOCK, top * NSA_SEL_LEN) * scale
        p = _masked_softmax(s, smask).reshape(B, G, R, Q_BLOCK, top, NSA_SEL_LEN)
        o_sel = jnp.einsum('bgrqnl,bgqnld->bqgrd', p.astype(vs_g.dtype), vs_g)
        kwi = lax.dynamic_slice_in_dim(k_win, q0, Q_BLOCK + NSA_WINDOW, axis=1)
        vwi = lax.dynamic_slice_in_dim(v_win, q0, Q_BLOCK + NSA_WINDOW, axis=1)
        kpos = q0 - NSA_WINDOW + jnp.arange(Q_BLOCK + NSA_WINDOW)
        wmask = (kpos[None, :] <= tpos[:, None]) & (kpos[None, :] > tpos[:, None] - NSA_WINDOW) & (kpos[None, :] >= 0)
        s = jnp.einsum('bqgrd,bkgd->bgrqk', qi, kwi) * scale
        p = _masked_softmax(s, wmask)
        o_win = jnp.einsum('bgrqk,bkgd->bqgrd', p.astype(vwi.dtype), vwi)
        o = gb[..., 0:1] * o_cmp + gb[..., 1:2] * o_sel + gb[..., 2:3] * o_win
        return o.reshape(B, Q_BLOCK, H * Dh).astype(h.dtype)

    o = lax.map(block, jnp.arange(S // Q_BLOCK))
    o = jnp.moveaxis(o, 0, 1).reshape(B, S, H * Dh)
    return o @ w_out

def _mla_mixer(h, pos, w_in, q_a_norm, kv_a_norm, w_q_b, w_kv_b, q_norm, k_norm, w_out):
    B, S, _ = h.shape
    H, dq = MLA_HEADS, MLA_NOPE + MLA_ROPE
    cq, ckv, k_rot = jnp.split(h @ w_in, [MLA_Q_LORA, MLA_Q_LORA + MLA_KV_LORA], axis=-1)
    q = _rms((_rms(cq, q_a_norm) @ w_q_b).reshape(B, S, H, dq), q_norm)
    kv = (_rms(ckv, kv_a_norm) @ w_kv_b).reshape(B, S, H, MLA_NOPE + MLA_V)
    k_nope = _rms(kv[..., :MLA_NOPE], k_norm[:MLA_NOPE])
    v = kv[..., MLA_NOPE:]
    k_rot = _rope(_rms(k_rot, k_norm[MLA_NOPE:])[:, :, None, :], pos)
    q = jnp.concatenate([q[..., :MLA_NOPE], _rope(q[..., MLA_NOPE:], pos)], axis=-1)
    k = jnp.concatenate([k_nope, jnp.broadcast_to(k_rot, (B, S, H, MLA_ROPE))], axis=-1)
    scale = dq ** -0.5
    key_pos = jnp.arange(S)

    def block(qb):
        q0 = qb * Q_BLOCK
        qi = lax.dynamic_slice_in_dim(q, q0, Q_BLOCK, axis=1)
        s = jnp.einsum('bqhd,bkhd->bhqk', qi, k) * scale
        p = _masked_softmax(s, key_pos[None, :] <= (q0 + jnp.arange(Q_BLOCK))[:, None])
        return jnp.einsum('bhqk,bkhd->bqhd', p.astype(v.dtype), v)

    o = lax.map(block, jnp.arange(S // Q_BLOCK))
    o = jnp.moveaxis(o, 0, 1).reshape(B, S, H * MLA_V)
    return o @ w_out

def _retention_mixer(h, pos, w_in, gn_w, w_out):
    B, S, _ = h.shape
    H, dk, dv, C = RET_HEADS, RET_QK, RET_V, RET_CHUNK
    q, k, v, g = jnp.split(h @ w_in, np.cumsum([H * dk, H * dk, H * dv]).tolist(), axis=-1)
    q = _rope(q.reshape(B, S, H, dk), pos)
    k = _rope(k.reshape(B, S, H, dk), pos) * (dk ** -0.5)
    v = v.reshape(B, S, H, dv)
    n_ch = S // C

    def chunks(t):
        return t.astype(jnp.float32).reshape(B, n_ch, C, H, t.shape[-1]).transpose(1, 0, 3, 2, 4)

    log_gamma = jnp.log1p(-(2.0 ** (-5.0 - jnp.arange(H, dtype=jnp.float32))))
    n = jnp.arange(C, dtype=jnp.float32)
    rel = n[:, None] - n[None, :]
    decay_in = jnp.where(rel >= 0, jnp.exp(jnp.maximum(rel, 0.0)[None] * log_gamma[:, None, None]), 0.0)
    xi = jnp.exp((n + 1.0)[None] * log_gamma[:, None])
    zeta = jnp.exp((C - 1.0 - n)[None] * log_gamma[:, None])
    gamma_c = jnp.exp(C * log_gamma)

    def step(state, inp):
        qc, kc, vc = inp
        inner = jnp.einsum('bhqk,bhke->bhqe', jnp.einsum('bhqd,bhkd->bhqk', qc, kc) * decay_in, vc)
        cross = jnp.einsum('bhqd,bhde->bhqe', qc, state) * xi[None, :, :, None]
        state = gamma_c[None, :, None, None] * state + jnp.einsum('bhkd,bhke->bhde', kc * zeta[None, :, :, None], vc)
        return state, inner + cross

    state0 = jnp.zeros((B, H, dk, dv), jnp.float32)
    _, y = lax.scan(step, state0, (chunks(q), chunks(k), chunks(v)))
    y = y.transpose(1, 0, 3, 2, 4).reshape(B, S, H, dv)
    mu = jnp.mean(y, axis=-1, keepdims=True)
    var = jnp.mean(jnp.square(y - mu), axis=-1, keepdims=True)
    y = ((y - mu) * lax.rsqrt(var + NORM_EPS)).reshape(B, S, H * dv) * gn_w.astype(jnp.float32)
    return (jax.nn.silu(g.astype(jnp.float32)) * y).astype(h.dtype) @ w_out

def _ssd_mixer(h, w_in, conv_w, conv_b, dt_bias, a_log, d_skip, norm_w, w_out):
    B, S, _ = h.shape
    H, P, G, N, C = SSD_HEADS, SSD_HEADDIM, SSD_GROUPS, SSD_STATE, SSD_CHUNK
    R = H // G
    z, xbc, dt = jnp.split(h @ w_in, [SSD_INNER, SSD_INNER + SSD_CONV_CH], axis=-1)
    xbc = lax.conv_general_dilated(xbc, conv_w[:, None, :], window_strides=(1,), padding=[(SSD_CONV - 1, 0)],
                                   dimension_numbers=('NWC', 'WIO', 'NWC'), feature_group_count=SSD_CONV_CH)
    xbc = jax.nn.silu(xbc + conv_b)
    xs, bm, cm = jnp.split(xbc, [SSD_INNER, SSD_INNER + G * N], axis=-1)
    xs = xs.reshape(B, S, H, P)
    dt = jax.nn.softplus(dt.astype(jnp.float32) + dt_bias.astype(jnp.float32))
    a = -jnp.exp(a_log.astype(jnp.float32))
    n_ch = S // C

    def chunks(t):
        return t.astype(jnp.float32).reshape((B, n_ch, C) + t.shape[2:]).swapaxes(0, 1)

    tril = jnp.tril(jnp.ones((C, C), dtype=bool))

    def step(state, inp):
        xc, dtc, bc, cc = inp
        cum = jnp.cumsum(dtc * a, axis=1)
        seg = jnp.where(tril[None, :, :, None], cum[:, :, None, :] - cum[:, None, :, :], -jnp.inf)
        w = jnp.exp(seg).reshape(B, C, C, G, R) * jnp.einsum('btgn,bsgn->btsg', cc, bc)[..., None] \
            * dtc.reshape(B, 1, C, G, R)
        xg = xc.reshape(B, C, G, R, P)
        y = jnp.einsum('btsgr,bsgrp->btgrp', w, xg)
        y = y + jnp.einsum('btgn,bgrpn->btgrp', cc, state) * jnp.exp(cum).reshape(B, C, G, R)[..., None]
        w_end = (jnp.exp(cum[:, -1:, :] - cum) * dtc).reshape(B, C, G, R)
        state = jnp.exp(cum[:, -1, :]).reshape(B, G, R)[..., None, None] * state \
            + jnp.einsum('bsgn,bsgr,bsgrp->bgrpn', bc, w_end, xg)
        return state, y

    state0 = jnp.zeros((B, G, R, P, N), jnp.float32)
    _, y = lax.scan(step, state0, (chunks(xs), chunks(dt), chunks(bm.reshape(B, S, G, N)), chunks(cm.reshape(B, S, G, N))))
    y = y.swapaxes(0, 1).reshape(B, S, H, P) + d_skip.astype(jnp.float32)[:, None] * xs.astype(jnp.float32)
    yg = (y.reshape(B, S, SSD_INNER) * jax.nn.silu(z.astype(jnp.float32))).reshape(B, S, G, SSD_INNER // G)
    y = _rms(yg, norm_w.reshape(G, SSD_INNER // G)).reshape(B, S, SSD_INNER)
    return y.astype(h.dtype) @ w_out

def _swiglu(h, w_in, w_out):
    a, b = jnp.split(h @ w_in, 2, axis=-1)
    return (jax.nn.silu(a) * b) @ w_out

def setup_inputs(seed: int = 0) -> dict:
    key = jax.random.key(seed)
    ks = iter(jax.random.split(key, 64))
    f32 = jnp.float32

    def nrm(shape, scale):
        return jax.random.normal(next(ks), shape, f32) * scale

    def gain(shape):
        return 1.0 + nrm(shape, 0.05)

    la, lb, lc, ld = (_n_kind(m) for m in range(N_MIXERS))
    D = D_MODEL
    positions = jax.random.randint(next(ks), (BATCH, 1), 0, 4096, jnp.int32) + jnp.arange(SEQ, dtype=jnp.int32)[None, :]
    dt0 = jnp.exp(jax.random.uniform(next(ks), (ld, SSD_HEADS), f32, math.log(1e-3), math.log(1e-1)))
    return {
        'x': nrm((BATCH, SEQ, D), 1.0),
        'c': nrm((BATCH, D), 1.0),
        'positions': positions,
        'ada_w': nrm((DEPTH, D, 6 * D), 0.5 * D ** -0.5),
        'ada_b': nrm((DEPTH, 6 * D), 0.02),
        'norm_mix': gain((DEPTH, D)),
        'norm_ffn': gain((DEPTH, D)),
        'ffn_w_in': nrm((DEPTH, D, 2 * FFN_HIDDEN), D ** -0.5),
        'ffn_w_out': nrm((DEPTH, FFN_HIDDEN, D), FFN_HIDDEN ** -0.5),
        'nsa_w_in': nrm((la, D, NSA_IN), D ** -0.5),
        'nsa_q_norm': gain((la, HEAD_DIM)),
        'nsa_k_norm': gain((la, 3, HEAD_DIM)),
        'nsa_cmp_pe': nrm((la, 2, NSA_CMP_LEN, HEAD_DIM), 0.1),
        'nsa_cmp_w1': nrm((la, 2, NSA_CMP_LEN * HEAD_DIM, NSA_CMP_HIDDEN), (NSA_CMP_LEN * HEAD_DIM) ** -0.5),
        'nsa_cmp_w2': nrm((la, 2, NSA_CMP_HIDDEN, HEAD_DIM), NSA_CMP_HIDDEN ** -0.5),
        'nsa_w_out': nrm((la, NSA_HEADS * HEAD_DIM, D), (NSA_HEADS * HEAD_DIM) ** -0.5),
        'mla_w_in': nrm((lb, D, MLA_IN), D ** -0.5),
        'mla_q_a_norm': gain((lb, MLA_Q_LORA)),
        'mla_kv_a_norm': gain((lb, MLA_KV_LORA)),
        'mla_w_q_b': nrm((lb, MLA_Q_LORA, MLA_HEADS * (MLA_NOPE + MLA_ROPE)), MLA_Q_LORA ** -0.5),
        'mla_w_kv_b': nrm((lb, MLA_KV_LORA, MLA_HEADS * (MLA_NOPE + MLA_V)), MLA_KV_LORA ** -0.5),
        'mla_q_norm': gain((lb, MLA_NOPE + MLA_ROPE)),
        'mla_k_norm': gain((lb, MLA_NOPE + MLA_ROPE)),
        'mla_w_out': nrm((lb, MLA_HEADS * MLA_V, D), (MLA_HEADS * MLA_V) ** -0.5),
        'ret_w_in': nrm((lc, D, RET_IN), D ** -0.5),
        'ret_gn_w': gain((lc, RET_HEADS * RET_V)),
        'ret_w_out': nrm((lc, RET_HEADS * RET_V, D), (RET_HEADS * RET_V) ** -0.5),
        'ssd_w_in': nrm((ld, D, SSD_IN), D ** -0.5),
        'ssd_conv_w': nrm((ld, SSD_CONV, SSD_CONV_CH), SSD_CONV ** -0.5),
        'ssd_conv_b': nrm((ld, SSD_CONV_CH), 0.02),
        'ssd_dt_bias': dt0 + jnp.log(-jnp.expm1(-dt0)),
        'ssd_a_log': jnp.log(jax.random.uniform(next(ks), (ld, SSD_HEADS), f32, 1.0, 16.0)),
        'ssd_d': 1.0 + nrm((ld, SSD_HEADS), 0.1),
        'ssd_norm': gain((ld, SSD_INNER)),
        'ssd_w_out': nrm((ld, SSD_INNER, D), SSD_INNER ** -0.5),
    }

def reference(x, c, positions, ada_w, ada_b, norm_mix, norm_ffn, ffn_w_in, ffn_w_out,
              nsa_w_in, nsa_q_norm, nsa_k_norm, nsa_cmp_pe, nsa_cmp_w1, nsa_cmp_w2, nsa_w_out,
              mla_w_in, mla_q_a_norm, mla_kv_a_norm, mla_w_q_b, mla_w_kv_b, mla_q_norm, mla_k_norm, mla_w_out,
              ret_w_in, ret_gn_w, ret_w_out,
              ssd_w_in, ssd_conv_w, ssd_conv_b, ssd_dt_bias, ssd_a_log, ssd_d, ssd_norm, ssd_w_out):
    cond = jax.nn.silu(c)
    for i in range(DEPTH):
        mod = cond @ ada_w[i] + ada_b[i]
        sh_m, sc_m, g_m, sh_f, sc_f, g_f = [t[:, None, :] for t in jnp.split(mod, 6, axis=-1)]
        hm = _rms(x, norm_mix[i]) * (1.0 + sc_m) + sh_m
        kind, j = i % N_MIXERS, i // N_MIXERS
        if kind == 0:
            y = _nsa_mixer(hm, nsa_w_in[j], nsa_q_norm[j], nsa_k_norm[j], nsa_cmp_pe[j],
                           nsa_cmp_w1[j], nsa_cmp_w2[j], nsa_w_out[j])
        elif kind == 1:
            y = _mla_mixer(hm, positions, mla_w_in[j], mla_q_a_norm[j], mla_kv_a_norm[j], mla_w_q_b[j],
                           mla_w_kv_b[j], mla_q_norm[j], mla_k_norm[j], mla_w_out[j])
        elif kind == 2:
            y = _retention_mixer(hm, positions, ret_w_in[j], ret_gn_w[j], ret_w_out[j])
        else:
            y = _ssd_mixer(hm, ssd_w_in[j], ssd_conv_w[j], ssd_conv_b[j], ssd_dt_bias[j], ssd_a_log[j],
                           ssd_d[j], ssd_norm[j], ssd_w_out[j])
        x = x + g_m * y.astype(x.dtype)
        hf = _rms(x, norm_ffn[i]) * (1.0 + sc_f) + sh_f
        x = x + g_f * _swiglu(hf, ffn_w_in[i], ffn_w_out[i])
    return x


_drawn_inputs = setup_inputs


def setup_inputs(seed=0):
    import zlib

    import numpy as np

    out = dict(_drawn_inputs(seed))
    spreads = {}
    factors = {'norm_mix': 7.445,
     'norm_ffn': 2.845,
     'nsa_q_norm': 8.0,
     'nsa_k_norm': 8.0,
     'nsa_cmp_pe': 8.0,
     'mla_q_a_norm': 8.0,
     'mla_kv_a_norm': 8.0,
     'mla_q_norm': 8.0,
     'mla_k_norm': 8.0}
    for name, (base, spread) in spreads.items():
        noise = np.random.default_rng([zlib.crc32(name.encode()), seed]).standard_normal(out[name].shape)
        drawn = base * np.exp(spread * noise) if base else spread * noise
        out[name] = jnp.asarray(drawn.astype(out[name].dtype))
    for name, factor in factors.items():
        out[name] = (out[name] * factor).astype(out[name].dtype)
    return out
```

```python
from contextlib import ExitStack

import numpy as np

import concourse.bass as bass
from concourse import mybir

F32 = mybir.dt.float32
F32R = mybir.dt.float32r
BF16 = mybir.dt.bfloat16
I32 = mybir.dt.int32
ACT = mybir.ActivationFunctionType
ALU = mybir.AluOpType
X = mybir.AxisListType.X

P = 128
S = 256
T = S // P
D = 1024
KD = D // P
EPS = 1e-6
MASKED = -1e30
FLOOR = -1e29
TINY = 1e-30
H = 16
DH = 64
G = 4
R = H // G
STRIDE = 16
CLEN = 32
NCMP = S // STRIDE - 1
CP = 32
CM = CLEN * DH // P
CH = 256
NSA_IN = H * DH + 6 * G * DH + 3 * H
QL, KVL, ROT, NOPE = 384, 256, 32, 64
DQ = NOPE + ROT
MLA_IN = QL + KVL + ROT
FH = 2816
HU = 256
FU = FH // HU
FK = FH // P
NSEG = 12
RING = 4
ARING = 3
HALF = 1024
LAST_UP = FU - 1

IN0 = 0
GATE0 = IN0 + 20
CMP0 = GATE0 + 2
OUT0 = CMP0 + 8
UP0 = OUT0 + 8
DOWN0 = UP0 + 4 * FU
IN1 = DOWN0 + FK
INB1 = IN1 + 4
QB1 = INB1 + 2
KVB1 = QB1 + 6
OUT1 = KVB1 + 4
UP1 = OUT1 + 8
DOWN1 = UP1 + 4 * FU
END = DOWN1 + FK

UNIT_EMPTIED = ["act"] * 8 + ["dve"] * (2 + FU + 2) + ["act"] * 9 + ["dve"] * (2 + FU + 2)
U_IN0, U_CMP0, U_OUT0, U_UP0 = 0, 6, 8, 10
U_DOWN0 = U_UP0 + FU
U_IN1 = U_DOWN0 + 2
U_QB1 = U_IN1 + 2
U_KVB1 = U_QB1 + 3
U_OUT1 = U_KVB1 + 4
U_UP1 = U_OUT1 + 2
U_DOWN1 = U_UP1 + FU

TP_EMPTIED = []


def _batches(n, who):
    TP_EMPTIED.extend([who] * n)
    return len(TP_EMPTIED) - n


T_H0 = _batches(4, "dve")
T_KVC = _batches(2, "act")
T_Q = _batches(4, "dve")
T_K = _batches(4, "dve")
T_SC = _batches(1, "act")
T_KC = _batches(1, "dve")
T_PC = _batches(2, "act")
T_P0 = _batches(2 * H, "act")
T_O0 = _batches(4, "dve")
T_HF0 = _batches(4, "dve")
T_HID0 = _batches(FU, "dve")
T_H1 = _batches(4, "dve")
T_CQ = _batches(3, "dve")
T_Q1 = _batches(8, "act")
T_K1 = _batches(8, "dve")
T_P1 = _batches(H, "act")
T_O1 = _batches(4, "dve")
T_HF1 = _batches(4, "dve")
T_HID1 = _batches(FU, "dve")

ST_H0, ST_O0, ST_HF0, ST_HID0 = 0, 4, 8, 12
ST_H1 = ST_HID0 + FU
ST_CQ = ST_H1 + 4
ST_O1 = ST_CQ + 3
ST_HF1 = ST_O1 + 4
ST_HID1 = ST_HF1 + 4


def count_before(owners, n, who):
    return sum(o == who for o in owners[:n])


def trunk(nc, x_in, c_in, positions, ada_w, ada_b, norm_mix, norm_ffn, ffn_w_in, ffn_w_out,
          nsa_w_in, nsa_q_norm, nsa_k_norm, nsa_cmp_pe, nsa_cmp_w1, nsa_cmp_w2, nsa_w_out,
          mla_w_in, mla_q_a_norm, mla_kv_a_norm, mla_w_q_b, mla_w_kv_b, mla_q_norm, mla_k_norm,
          mla_w_out, out):
    ctx = ExitStack()
    with ctx:
        def sb(name, shape, dt, stack=ctx):
            return stack.enter_context(nc.sbuf_tensor(name, shape, dt))

        def sem(name):
            return ctx.enter_context(nc.semaphore(name))

        raw = sb("raw", [P, RING, 2 * HALF], F32)
        w_hi = sb("w_hi", [P, RING, HALF], F32R)
        w_lo = sb("w_lo", [P, RING, HALF], F32R)
        ada_ring = sb("ada_ring", [P, ARING, D], F32)
        ada_acc = sb("ada_acc", [P, 2, D], F32)
        x = sb("x", [P, T, D], F32)
        st_hi = sb("st_hi", [P, KD, S], F32R)
        st_lo = sb("st_lo", [P, KD, S], F32R)
        gate_rows = sb("gate_rows", [P, 2, D], F32)
        scratch = sb("scratch", [P, 2 * D], F32)
        tfull = sb("tfull", [P, 2, 512], F32)
        ident = sb("ident", [P, P], F32)
        ident_b = sb("ident_b", [P, P], BF16)
        ones = sb("ones", [P, P], F32)
        tri = sb("tri", [P, 3, P], BF16)
        cmp_mask = sb("cmp_mask", [P, T, H // 2 * CP], BF16)
        cond = sb("cond", [P, KD], F32)
        gain_cols = sb("gain_cols", [P, 4, KD], F32)
        ada_cols = sb("ada_cols", [P, NSEG, KD], F32)
        scale_cols = sb("scale_cols", [P, 4, KD], F32)
        nsa_gains = sb("nsa_gains", [P, 4], F32)
        pe_cols = sb("pe_cols", [P, 2, CM], F32)
        w2 = sb("w2", [P, 2, CH // P, DH], F32)
        lat_gains = sb("lat_gains", [P, 5], F32)
        q_gain_row = sb("q_gain_row", [P, DQ], F32)
        k_gain_row = sb("k_gain_row", [P, DQ], F32)
        pos_i = sb("pos_i", [P, T], I32)
        inv = sb("inv", [P, ROT // 2], F32)
        cs = sb("cs", [P, 2, T, ROT // 2], F32)
        trig = sb("trig", [P, 3, T * ROT // 2], F32)
        stat = sb("stat", [P, 8, 32], F32)
        nmax = sb("nmax", [P, 4, 2], F32)
        sums = sb("sums", [P, 2, T * R], F32)
        coef = sb("coef", [P, 3, T * R], F32)

        lin = [ctx.enter_context(nc.psum_tensor(f"lin{n}", [P, 512], F32)) for n in range(4)]
        tp = [ctx.enter_context(nc.psum_tensor(f"tp{n}", [P, 512], F32)) for n in range(2)]
        sc = [ctx.enter_context(nc.psum_tensor(f"sc{n}", [P, 512], F32)) for n in range(2)]

        nsa = ExitStack()
        with nsa:
            proj = sb("proj", [P, T, NSA_IN], F32, nsa)
            kdup_o = sb("kdup_o", [P, 2, T * G * 2 * DH], F32, nsa)
            q_t = sb("q_t", [P, H // 2, S], F32, nsa)
            k_t = sb("k_t", [P, 2, G, S], F32, nsa)
            z = sb("z", [P, 2, G, S], F32, nsa)
            a_hi = sb("a_hi", [P, CM, G * CP], F32R, nsa)
            a_lo = sb("a_lo", [P, CM, G * CP], F32R, nsa)
            kc_t = sb("kc_t", [P, P], F32, nsa)
            gates = sb("gates", [P, T, 3 * H], F32, nsa)
            v_cmp = sb("v_cmp", [P, G, DH], F32, nsa)
            cstat = sb("cstat", [P, 3, H], F32, nsa)
        prob = z[:, 0, :, :].rearrange("p g s -> p (g s)").rearrange("p (b n) -> p b n", b=2)
        prob_t = z[:, 1, :, :].rearrange("p g s -> p (g s)").rearrange("p (b n) -> p b n", b=2)
        kv_t = k_t[:, :, 0:2, :].rearrange("p b g s -> p b (g s)")
        ffn = ExitStack()
        with ffn:
            hid_hi = sb("hid_hi", [P, FK * S], F32R, ffn)
            hid_lo = sb("hid_lo", [P, FK * S], F32R, ffn)
            silu_a = sb("silu_a", [P, 2, T, HU], F32, ffn)
            hid = sb("hid", [P, 2, T, HU], F32, ffn)
        mla = ExitStack()
        with mla:
            proj1 = sb("proj1", [P, T, MLA_IN], F32, mla)
            q_tok = sb("q_tok", [P, T, H * DQ], F32, mla)
            k_tok = sb("k_tok", [P, T, H, DQ], F32, mla)
            v_tok = sb("v_tok", [P, T, H, DH], F32, mla)
            q1_t = sb("q1_t", [DQ, H, S], F32, mla)
            k1_t = sb("k1_t", [DQ, H, S], F32, mla)
        o0 = kdup_o[:, :, :].rearrange("p t n -> p (t n)").rearrange("p (t n) -> p t n", t=T)
        q_tok_flat = q_tok[:, :, :].rearrange("p t n -> p (t n)")
        k_tok_flat = k_tok[:, :, :, :].rearrange("p t h d -> p (t h d)")
        o1 = q_tok_flat[:, 0:T * D].rearrange("p (t n) -> p t n", t=T)
        prob1 = k_tok_flat[:, 0:1024].rearrange("p (b n) -> p b n", b=2)
        prob1_t = k_tok_flat[:, 1024:2048].rearrange("p (b n) -> p b n", b=2)

        small_in = sem("small_in")
        x_in_done = sem("x_in_done")
        landed = [sem(f"landed{n}") for n in range(RING)]
        hi_ready = sem("hi_ready")
        lo_ready = sem("lo_ready")
        slot_used = sem("slot_used")
        unit_empty_act = sem("unit_empty_act")
        unit_empty_dve = sem("unit_empty_dve")
        unit_empty = {"act": unit_empty_act, "dve": unit_empty_dve}
        tp_filled = sem("tp_filled")
        tp_empty_act = sem("tp_empty_act")
        tp_empty_dve = sem("tp_empty_dve")
        tp_empty = {"act": tp_empty_act, "dve": tp_empty_dve}
        t_scaled = sem("t_scaled")
        st_high = sem("st_high")
        st_ready = sem("st_ready")
        ada_landed = [sem(f"ada_landed{n}") for n in range(ARING)]
        ada_bias = [sem(f"ada_bias{n}") for n in range(2)]
        ada_used = sem("ada_used")
        acc_zero = sem("acc_zero")
        acc_dve = sem("acc_dve")
        acc_pool = sem("acc_pool")
        ada_red = sem("ada_red")
        ada_out = sem("ada_out")
        consts = sem("consts")
        squares = sem("squares")
        var_ready = sem("var_ready")
        root = sem("root")
        xn_ready = sem("xn_ready")
        cond_landed = sem("cond_landed")
        cond_ready = sem("cond_ready")
        trig_arg = sem("trig_arg")
        trig_done = sem("trig_done")
        resid = sem("resid")
        z_done = sem("z_done")
        a_full = sem("a_full")
        a_high = sem("a_high")
        a_ready = sem("a_ready")
        s_copied = sem("s_copied")
        cmp_out = sem("cmp_out")
        gate_exp = sem("gate_exp")
        scored = sem("scored")
        maxed = sem("maxed")
        exped = sem("exped")
        p_copied = sem("p_copied")
        pv_done = sem("pv_done")
        pv_empty = sem("pv_empty")
        o_steps = sem("o_steps")
        silu_ready = sem("silu_ready")
        act_step = sem("act_step")
        dve_step = sem("dve_step")
        pool_step = sem("pool_step")
        stored = sem("stored")

        block = ctx.enter_context(nc.Block())

        def at(i, first, stride):
            return first if i is None else i * stride + first

        def half(buf, s):
            return buf[:, s % RING, :]

        def raw_half(s):
            return raw[:, (s // 2) % RING, (s % 2) * HALF:(s % 2 + 1) * HALF]

        def split_sizes(s):
            if GATE0 <= s < CMP0:
                return 4 * 48
            if INB1 <= s < QB1:
                return 4 * 160
            if QB1 <= s < KVB1:
                return 1024 if (s - QB1) % 2 == 0 else 512
            return HALF

        def raw_part(s):
            n = split_sizes(s)
            slot = raw[:, (s // 2) % RING, :]
            if KVB1 <= s < OUT1:
                v = slot.rearrange("p (k c) -> p k c", k=2)
                return v[:, :, (s % 2) * 512:(s % 2 + 1) * 512]
            first = 0 if s % 2 == 0 else (split_sizes(s - 1))
            return slot[:, first:first + n]

        def part_of(buf, s):
            n = split_sizes(s)
            v = buf[:, s % RING, 0:n]
            if KVB1 <= s < OUT1:
                return v.rearrange("p (k c) -> p k c", k=2)
            return v

        up_view = ffn_w_in.rearrange("l (k p) (two c) -> l p k two c", p=P, two=2)

        def weight_slot(b):
            s = 2 * b
            slot = raw[:, b % RING, :]

            def cut(k, c):
                return slot[:, 0:k * c].rearrange("p (k c) -> p k c", k=k)

            def columns(w, k0, k, c0, c):
                return w.rearrange("(k p) n -> p k n", p=P)[:, k0:k0 + k, c0:c0 + c]

            if s < GATE0:
                u, h = divmod(s - IN0, 4)
                return columns(nsa_w_in[0], 2 * h, 4, 512 * u, 512), cut(4, 512)
            if s < CMP0:
                return columns(nsa_w_in[0], 0, KD, 2560, 48), cut(KD, 48)
            if s < OUT0:
                which, q = divmod(s - CMP0, 4)
                return columns(nsa_cmp_w1[0, which], 4 * q, 8, 0, CH), cut(8, CH)
            for first, w in ((OUT0, nsa_w_out), (OUT1, mla_w_out)):
                if first <= s < first + 8:
                    u, h = divmod(s - first, 4)
                    return columns(w[0], 2 * h, 4, 512 * u, 512), cut(4, 512)
            for layer, first in ((0, DOWN0), (1, DOWN1)):
                if first <= s < first + FK:
                    return columns(ffn_w_out[layer], s - first, 2, 0, D), cut(2, D)
            if s < INB1:
                return columns(mla_w_in[0], 2 * (s - IN1), 4, 0, 512), cut(4, 512)
            if s < QB1:
                return columns(mla_w_in[0], 0, KD, 512, 160), cut(KD, 160)
            if s < KVB1:
                return columns(mla_w_q_b[0], 0, 3, 512 * ((s - QB1) // 2), 512), cut(3, 512)
            return columns(mla_w_kv_b[0], 0, 2, 512 * (s - KVB1), D), cut(2, D)

        LANDED = []
        count = [0] * RING
        for b in range(END // 2):
            is_up = UP0 <= 2 * b < DOWN0 or UP1 <= 2 * b < DOWN1
            count[b % RING] += 32 if is_up else 16
            LANDED.append(count[b % RING])

        N_SMALL = 0

        @block.sync
        def _(sp):
            nonlocal N_SMALL
            sp.dma_start(x[:], x_in[0].rearrange("(t p) n -> p t n", p=P)).then_inc(x_in_done, 16)
            with nc.allow_non_contiguous_dma(reason="vectors laid out over partitions"):
                smalls = [(gain_cols[:, 2 * layer + j, :], g[layer].rearrange("(k p) -> p k", p=P))
                          for layer in range(2) for j, g in enumerate((norm_mix, norm_ffn))]
                smalls += [(pe_cols[:, b, :], nsa_cmp_pe[0, b].rearrange("(m u) d -> (u d) m", u=2))
                           for b in range(2)]
                smalls += [
                    (nsa_gains[0:64, 0:1], nsa_q_norm.rearrange("l p -> p l")),
                    (nsa_gains[64:128, 0:1], nsa_q_norm.rearrange("l p -> p l")),
                    (nsa_gains[0:64, 1:4], nsa_k_norm[0].rearrange("b p -> p b")),
                    (nsa_gains[64:128, 1:4], nsa_k_norm[0].rearrange("b p -> p b")),
                    (lat_gains[:, 0:3], mla_q_a_norm[0].rearrange("(k p) -> p k", p=P)),
                    (lat_gains[:, 3:5], mla_kv_a_norm[0].rearrange("(k p) -> p k", p=P)),
                ]
                for dst, src in smalls:
                    sp.dma_start(dst, src).then_inc(small_in, 16)
            for b in range(2):
                sp.dma_start(w2[:, b], nsa_cmp_w2[0, b].rearrange("(k p) d -> p k d", p=P)).then_inc(small_in, 16)
            sp.dma_start(q_gain_row[:], mla_q_norm[0].partition_broadcast(P)).then_inc(small_in, 16)
            sp.dma_start(k_gain_row[:], mla_k_norm[0].partition_broadcast(P)).then_inc(small_in, 16)
            N_SMALL = 16 * (len(smalls) + 4)
            sp.wait_ge(ada_used, 12)

            def load(b, i=None):
                if b >= RING or i is not None:
                    sp.wait_ge(lo_ready, at(i, 2 * (b - RING) + 2, 8))

            def load_up(layer, first, b, i):
                load(b, i)
                j = b - first
                k0 = 4 * (j % 2)
                slot = raw[:, b % RING, :].rearrange("p (k two c) -> p k two c", k=4, two=2)
                for side in range(2):
                    c0 = at(i, HU * (j // 2), 2 * HU)
                    src = up_view[layer][:, k0:k0 + 4, side, bass.ds(c0, HU)]
                    sp.dma_start(slot[:, :, side, :], src).then_inc(landed[b % RING], 16)

            b = 0
            while b < END // 2:
                layer = 0 if b < UP1 // 2 else 1
                first = (UP0, UP1)[layer] // 2
                if b == first:
                    for q in range(2):
                        load_up(layer, first, first + q, None)
                    with sp.Fori(0, (FU - 1) // 2) as i:
                        for q in range(4):
                            load_up(layer, first, first + 2 + q, i)
                    b = first + 2 * FU
                    continue
                src, dst = weight_slot(b)
                load(b)
                sp.dma_start(dst, src).then_inc(landed[b % RING], 16)
                b += 1
            y = out[0].rearrange("(t p) n -> p t n", p=P)
            for n in range(2):
                sp.wait_ge(resid, 12 + 2 * n + 2)
                sp.dma_start(y[:, :, 512 * n:512 * n + 512], x[:, :, 512 * n:512 * n + 512]).then_inc(stored, 16)
            sp.wait_ge(stored, 32)

        def ada_source(a):
            seg, kt = divmod(a, KD)
            layer, s6 = divmod(seg, 6)
            return ada_w[layer, kt * P:(kt + 1) * P, s6 * D:(s6 + 1) * D]

        @block.gpsimd
        def _(pool):
            steps = [0]

            def link(ins):
                steps[0] += 1
                ins.then_inc(pool_step, 1)
                pool.wait_ge(pool_step, steps[0])

            with nc.allow_non_contiguous_dma(reason="vectors laid out over partitions"):
                pool.dma_start(pos_i[:], positions[0].rearrange("(t p) -> p t", p=P)).then_inc(cond_landed, 16)
                pool.dma_start(cond[:], c_in[0].rearrange("(k p) -> p k", p=P)).then_inc(cond_landed, 16)

            def issue(a):
                pool.dma_start(ada_ring[:, a % ARING, :], ada_source(a)).then_inc(ada_landed[a % ARING], 16)

            def issue_bias(seg):
                layer, s6 = divmod(seg, 6)
                pool.dma_start(ada_acc[0:1, seg % 2, :],
                               ada_b[layer:layer + 1, s6 * D:(s6 + 1) * D]).then_inc(ada_bias[seg % 2], 16)

            for a in range(ARING):
                issue(a)
            link(nc.gpsimd.memset(ada_acc[:], 0.0))
            issue_bias(0)
            issue_bias(1)
            for n in range(ROT // 2):
                f = float(np.float32(np.float64(10000.0) ** (-2.0 * n / ROT)))
                nc.gpsimd.memset(inv[:, n:n + 1], f)
            nc.gpsimd.memset(ones[:], 1.0)
            nc.gpsimd.memset(ident[:], 0.0)
            nc.gpsimd.memset(ident_b[:], 0.0)
            nc.gpsimd.memset(tri[:], 0.0)
            nc.gpsimd.memset(v_cmp[:], 0.0)
            link(nc.gpsimd.memset(cmp_mask[:], 0.0))
            for t in (ident, ident_b):
                nc.gpsimd.affine_select(out=t[:], in_=t[:], compare_op=ALU.not_equal, fill=1.0, base=0,
                                        pattern=[[-1, P]], channel_multiplier=1)
            for n in (0, 2):
                nc.gpsimd.affine_select(out=tri[:, n, :], in_=tri[:, n, :], compare_op=ALU.is_ge, fill=MASKED,
                                        base=0, pattern=[[-1, P]], channel_multiplier=1)
            for t in range(T):
                last = nc.gpsimd.affine_select(
                    out=cmp_mask[:, t, :], in_=cmp_mask[:, t, :], compare_op=ALU.is_ge, fill=MASKED,
                    base=t * P - CLEN + 1, pattern=[[0, H // 2], [-STRIDE, CP]], channel_multiplier=1)
            last.then_inc(consts, 1)
            for a in range(ARING, 2 * KD + ARING):
                pool.wait_ge(ada_used, a - ARING + 1)
                issue(a)
            for seg in range(2, NSEG):
                acc = ada_acc[:, seg % 2, :]
                pool.wait_ge(ada_red, seg - 1)
                link(nc.gpsimd.memset(acc, 0.0))
                issue_bias(seg)
                pool.wait_ge(ada_bias[seg % 2], 16 * (seg // 2 + 1))
                for kt in range(KD):
                    a = seg * KD + kt
                    chunk = ada_ring[:, a % ARING, :]
                    pool.wait_ge(ada_landed[a % ARING], 16 * (a // ARING + 1))
                    link(nc.gpsimd.tensor_scalar(chunk, chunk, cond[:, kt:kt + 1], 0.0, ALU.mult, ALU.add))
                    add = nc.gpsimd.tensor_tensor(acc, acc, chunk, ALU.add)
                    link(add)
                    if a + ARING < NSEG * KD:
                        issue(a + ARING)
                pool.sem_inc(acc_pool, 1)

        @block.scalar
        def _(act):
            steps = [0]
            made = [0]
            n_root = [0]

            def link(ins):
                steps[0] += 1
                ins.then_inc(act_step, 1)
                act.wait_ge(act_step, steps[0])

            def high(s, i=None, landed_at=None):
                if s % 2 == 0:
                    b = s // 2
                    act.wait_ge(landed[b % RING], LANDED[b] if landed_at is None else landed_at)
                if s >= RING or i is not None:
                    act.wait_ge(slot_used, at(i, s - RING + 1, 8))
                nc.scalar.activation(part_of(w_hi, s), raw_part(s), ACT.Copy).then_inc(hi_ready, 1)

            def high_to(n):
                while made[0] < n:
                    high(made[0])
                    made[0] += 1

            def unit_done(s_end):
                act.wait_ge(slot_used, s_end)

            def squares_of_x(update):
                for t in range(T):
                    if update == 0:
                        act.wait_ge(x_in_done, 16)
                    else:
                        act.wait_ge(resid, update)
                    nc.scalar.activation(scratch[:, t * D:(t + 1) * D], x[:, t, :], ACT.Square,
                                         accum_out=stat[:, 0, t:t + 1]).then_inc(squares, 1)

            def roots(n):
                n_root[0] += 1
                act.wait_ge(var_ready, n_root[0])
                nc.scalar.activation(stat[:, 2, 0:n], stat[:, 1, 0:n], ACT.Sqrt).then_inc(root, 1)

            def high_from_tfull(k0, nk, n_scaled):
                act.wait_ge(t_scaled, n_scaled + 1)
                nc.scalar.activation(st_hi[:, k0:k0 + nk, :], tfull[:, n_scaled % 2, 0:nk * S].rearrange(
                    "p (k s) -> p k s", k=nk), ACT.Copy).then_inc(st_high, 1)

            def high_from_tp(batch, dst):
                act.wait_ge(tp_filled, batch + 1)
                nc.scalar.activation(dst, tp[batch % 2][:], ACT.Copy).then_inc(st_high, 1)

            def attention(n_items, item0, tp0, scale_exp, prob_b, prob_tb):
                for n in range(n_items + 1):
                    if n < n_items:
                        m = item0 + n
                        step, r = divmod(n, R)
                        act.wait_ge(maxed, m + 1)
                        if n >= 2:
                            act.wait_ge(tp_filled, tp0 + n - 1)
                        for t in range(T):
                            w = (t + 1) * P
                            c0 = t * P
                            e = nc.scalar.activation(
                                prob_b[:, n % 2, c0:c0 + w], sc[m % 2][:, c0:c0 + w], ACT.Exp,
                                bias=nmax[:, m % 4, t:t + 1],
                                accum_out=sums[:, step % 2, t * R + r:t * R + r + 1])
                        e.then_inc(exped, 1)
                    if n >= 1:
                        b = tp0 + n - 1
                        act.wait_ge(tp_filled, b + 1)
                        nc.scalar.activation(prob_tb[:, (n - 1) % 2, 0:3 * P], tp[b % 2][:, 0:3 * P],
                                             ACT.Copy).then_inc(tp_empty_act, 1)

            def feed_forward(up, down, unit0, tp0):
                def unit(u, i=None):
                    for q in range(4):
                        s = up + 4 * u + 4 + q
                        b = s // 2
                        if q == 1 and (u > 0 or i is not None):
                            batch = tp0 + u - 1
                            act.wait_ge(tp_filled, at(i, batch + 1, 2))
                            nc.scalar.activation(hid_hi[:, bass.ds(at(i, (u - 1) * 512, 1024), 512)],
                                                 tp[batch % 2][:], ACT.Copy).then_inc(st_high, 1)
                        stride = 32
                        if i is not None or s < down:
                            lv = at(i, LANDED[b], stride)
                        else:
                            lv = LANDED[b]
                        high(s, i, lv)
                    act.wait_ge(slot_used, at(i, up + 4 * u + 4, 8))
                    for t in range(T):
                        nc.scalar.activation(silu_a[:, u % 2, t, :], lin[2 * ((unit0 + u) % 2) + t][:, 0:HU],
                                             ACT.Silu).then_inc(silu_ready, 1)

                unit(0)
                with act.Fori(0, (FU - 3) // 2) as i:
                    unit(1, i)
                    unit(2, i)
                unit(FU - 2)
                unit(FU - 1)
                made[0] = down + 4
                high_to(down + 5)
                high_from_tp(tp0 + FU - 1, hid_hi[:, (FU - 1) * 512:FU * 512])
                high_to(min(down + FK + 4, END))

            act.wait_ge(cond_landed, 32)
            nc.scalar.activation(cond[:], cond[:], ACT.Silu).then_inc(cond_ready, 1)
            act.wait_ge(trig_arg, 2)
            nc.scalar.activation(cs[:].rearrange("p a t n -> p (a t n)"),
                                 trig[:, 0:2, :].rearrange("p a n -> p (a n)"), ACT.Sin).then_inc(trig_done, 1)
            squares_of_x(0)
            roots(2)
            for m in range(4):
                high_from_tfull(2 * m, 2, m)
            high_to(4)
            for u in range(6):
                s_end = IN0 + 4 * (u + 1) if u < 5 else CMP0
                high_to(s_end + 4)
                unit_done(s_end)
                n = 512 if u < 5 else 48
                for t in range(T):
                    ev = nc.scalar.activation(proj[:, t, 512 * u:512 * u + n], lin[2 * (u % 2) + t][:, 0:n],
                                              ACT.Copy)
                ev.then_inc(unit_empty_act, 1)
                if u == 2:
                    roots(T * H)
                if u == 4:
                    roots(T * G)
                    roots(T * G)
                if u == 3:
                    for b in range(2):
                        act.wait_ge(tp_filled, T_KVC + b + 1)
                        link_ins = nc.scalar.activation(kv_t[:, b, :], tp[(T_KVC + b) % 2][:], ACT.Copy)
                        link_ins.then_inc(tp_empty_act, 1)
                        act.wait_ge(tp_empty_act, b + 1)
                        for odd in range(2):
                            src = kv_t[64 * odd:64 * odd + 64, b, :].rearrange("p (j s) -> p j s", j=2)
                            act.dma_start(z[0:64, b, odd::2, :], src).then_inc(z_done, 16)
                            act.dma_start(z[64:128, b, odd::2, 0:S - 1], src[:, :, 1:S]).then_inc(z_done, 16)
                if u == 5:
                    act.wait_ge(unit_empty_act, 6)
                    nc.scalar.activation(gates[:], proj[:, :, 2560:2608], ACT.Exp, scale=-1.0).then_inc(gate_exp, 1)
            for b in range(2):
                act.wait_ge(a_full, b + 1)
                if b == 1:
                    act.wait_ge(slot_used, CMP0 + 4)
                nc.scalar.activation(a_hi[:].rearrange("p m c -> p (m c)"), scratch[:], ACT.Copy).then_inc(a_high, 1)
                if b == 0:
                    high_to(CMP0 + 4 + 4)
                    unit_done(CMP0 + 4)
                else:
                    high_to(CMP0 + 8 + 4)
                    unit_done(CMP0 + 8)
                nc.scalar.activation(tfull[:, 0, b * CH:(b + 1) * CH], lin[2 * ((U_CMP0 + b) % 2)][:, 0:CH],
                                     ACT.Silu).then_inc(unit_empty_act, 1)
            act.wait_ge(tp_filled, T_SC + 1)
            nc.scalar.activation(prob_t[:, 1, :], tp[T_SC % 2][:], ACT.Copy).then_inc(tp_empty_act, 1)
            roots(1)
            for t in range(T):
                act.wait_ge(maxed, t + 1)
                nc.scalar.activation(prob[:, t, :], prob[:, t, :], ACT.Exp).then_inc(exped, 1)
            for t in range(T):
                act.wait_ge(tp_filled, T_PC + t + 1)
                nc.scalar.activation(prob_t[:, t, :], tp[(T_PC + t) % 2][:], ACT.Copy).then_inc(tp_empty_act, 1)
            attention(2 * H, T, T_P0, 1.0, prob, prob_t)
            for m in range(4):
                high_from_tp(T_O0 + m, st_hi[:, 2 * m:2 * m + 2, :].rearrange("p k s -> p (k s)"))
            high_to(OUT0 + 8 + 4)
            squares_of_x(4)
            roots(2)
            for m in range(4):
                high_from_tfull(2 * m, 2, 4 + m)
            feed_forward(UP0, DOWN0, U_UP0, T_HID0)

            squares_of_x(8)
            roots(2)
            for m in range(4):
                high_from_tfull(2 * m, 2, 8 + m)
            for u in range(2):
                s_end = (INB1, QB1)[u]
                high_to(s_end + 4)
                unit_done(s_end)
                n = (512, 160)[u]
                for t in range(T):
                    ev = nc.scalar.activation(proj1[:, t, 512 * u:512 * u + n],
                                              lin[2 * ((U_IN1 + u) % 2) + t][:, 0:n], ACT.Copy)
                ev.then_inc(unit_empty_act, 1)
            act.wait_ge(unit_empty_act, count_before(UNIT_EMPTIED, U_IN1 + 2, "act"))
            for n, (c0, w) in enumerate(((0, QL), (QL, KVL), (QL + KVL, ROT))):
                for t in range(T):
                    at0 = (2 * n + t) * QL if n < 2 else 4 * QL + t * ROT
                    nc.scalar.activation(scratch[:, at0:at0 + w],
                                         proj1[:, t, c0:c0 + w], ACT.Square,
                                         accum_out=stat[:, 0, 2 * n + t:2 * n + t + 1]).then_inc(squares, 1)
            roots(6)
            for m, (k0, nk) in enumerate(((0, 2), (2, 1), (3, 2))):
                high_from_tfull(k0, nk, 12 + m)
            for u in range(3):
                high_to(QB1 + 2 * u + 2 + 4)
                unit_done(QB1 + 2 * u + 2)
                for t in range(T):
                    ev = nc.scalar.activation(q_tok[:, t, 512 * u:512 * u + 512],
                                              lin[2 * ((U_QB1 + u) % 2) + t][:], ACT.Copy)
                ev.then_inc(unit_empty_act, 1)
            for u in range(4):
                high_to(KVB1 + u + 1 + 4)
                unit_done(KVB1 + u + 1)
                for t in range(T):
                    kv = lin[2 * ((U_KVB1 + u) % 2) + t][:].rearrange("p (h d) -> p h d", d=2 * DH)
                    nc.scalar.activation(k_tok[:, t, 4 * u:4 * u + 4, 0:NOPE], kv[:, :, 0:NOPE], ACT.Copy)
                    ev = nc.scalar.activation(v_tok[:, t, 4 * u:4 * u + 4, :], kv[:, :, NOPE:], ACT.Copy)
                ev.then_inc(unit_empty_act, 1)
            roots(32)
            roots(32)
            for j in range(8):
                act.wait_ge(tp_filled, T_Q1 + j + 1)
                nc.scalar.activation(q1_t[:, 2 * j:2 * j + 2, :].rearrange("p h s -> p (h s)"),
                                     tp[(T_Q1 + j) % 2][0:DQ, :], ACT.Copy,
                                     scale=float(DQ ** -0.5)).then_inc(tp_empty_act, 1)
            act.wait_ge(tp_filled, T_P1)
            attention(H, T + 2 * H, T_P1, 1.0, prob1, prob1_t)
            for m in range(4):
                high_from_tp(T_O1 + m, st_hi[:, 2 * m:2 * m + 2, :].rearrange("p k s -> p (k s)"))
            high_to(OUT1 + 8 + 4)
            squares_of_x(12)
            roots(2)
            for m in range(4):
                high_from_tfull(2 * m, 2, 15 + m)
            feed_forward(UP1, DOWN1, U_UP1, T_HID1)

        @block.vector
        def _(dve):
            steps = [0]
            made = [0]
            counts = {"scaled": 0, "st": 0, "root": 0, "squares": 0, "resid": 0, "red": 0, "item": 0,
                      "step": 0}

            def link(ins):
                steps[0] += 1
                ins.then_inc(dve_step, 1)
                dve.wait_ge(dve_step, steps[0])

            def low(s, i=None):
                dve.wait_ge(hi_ready, at(i, s + 1, 8))
                nc.vector.tensor_tensor(part_of(w_lo, s), raw_part(s), part_of(w_hi, s).bitcast(F32),
                                        ALU.subtract).then_inc(lo_ready, 1)

            def low_to(n):
                while made[0] < n:
                    low(made[0])
                    made[0] += 1

            def reciprocal_roots(n, widths):
                c0 = 0
                for cnt, width in widths:
                    ins = nc.vector.tensor_scalar(stat[:, 1, c0:c0 + cnt], stat[:, 0, c0:c0 + cnt],
                                                  1.0 / width, EPS, ALU.mult, ALU.add)
                    c0 += cnt
                ins.then_inc(var_ready, 1)
                counts["root"] += 1
                dve.wait_ge(root, counts["root"])
                r, a = stat[:, 3, 0:n], stat[:, 4, 0:n]
                link(nc.vector.reciprocal(r, stat[:, 2, 0:n]))
                link(nc.vector.tensor_tensor(a, r, r, ALU.mult))
                link(nc.vector.tensor_tensor(a, a, stat[:, 1, 0:n], ALU.mult))
                link(nc.vector.tensor_scalar(a, a, -0.5, 1.5, ALU.mult, ALU.add))
                link(nc.vector.tensor_tensor(r, r, a, ALU.mult))

            def normalise_x():
                counts["squares"] += T
                dve.wait_ge(squares, counts["squares"])
                reciprocal_roots(T, [(T, D)])
                for t in range(T):
                    nc.vector.tensor_scalar(scratch[:, t * D:(t + 1) * D], x[:, t, :], stat[:, 3, t:t + 1],
                                            None, ALU.mult).then_inc(xn_ready, 1)

            def scale_and_split(batch, k0, nk, scale, shift):
                m = counts["scaled"]
                counts["scaled"] += 1
                dve.wait_ge(tp_filled, batch + 1)
                for k in range(nk):
                    src = tp[batch % 2][:, k * S:(k + 1) * S]
                    dst = tfull[:, m % 2, k * S:(k + 1) * S]
                    if shift is None:
                        ins = nc.vector.tensor_scalar(dst, src, scale[:, k:k + 1], None, ALU.mult)
                    else:
                        ins = nc.vector.tensor_scalar(dst, src, scale[:, k:k + 1], shift[:, k:k + 1],
                                                      ALU.mult, ALU.add)
                ins.then_inc(t_scaled, 1)
                counts["st"] += 1
                dve.wait_ge(st_high, counts["st"])
                nc.vector.tensor_tensor(
                    st_lo[:, k0:k0 + nk, :], tfull[:, m % 2, 0:nk * S].rearrange("p (k s) -> p k s", k=nk),
                    st_hi[:, k0:k0 + nk, :].bitcast(F32), ALU.subtract).then_inc(st_ready, 1)

            def modulated(norm, batch0, shift_seg):
                for m in range(4):
                    scale_and_split(batch0 + m, 2 * m, 2, scale_cols[:, norm, 2 * m:2 * m + 2],
                                    ada_cols[:, shift_seg, 2 * m:2 * m + 2])

            def low_from_tp(batch, hi, lo, i=None):
                counts["st"] += 1
                dve.wait_ge(st_high, at(i, counts["st"], 2))
                nc.vector.tensor_tensor(lo, tp[batch % 2][:], hi.bitcast(F32), ALU.subtract).then_inc(st_ready, 1)

            def ada_columns(seg):
                counts["red"] += 1
                dve.wait_ge(ada_red, seg + 1)
                nc.vector.tensor_copy(ada_cols[:, seg, :], sc[seg % 2][:, 0:KD]).then_inc(ada_out, 1)

            def ada_row(seg, row):
                dve.wait_ge(ada_red, seg + 1)
                nc.vector.tensor_copy(gate_rows[:, row, 0:512], sc[0][:])
                nc.vector.tensor_copy(gate_rows[:, row, 512:D], sc[1][:]).then_inc(ada_out, 1)

            def modulation(norm, scale_seg):
                dve.wait_ge(ada_out, scale_seg + 1)
                link(nc.vector.tensor_scalar(scale_cols[:, norm, :], ada_cols[:, scale_seg, :], 1.0, None,
                                             ALU.add))
                link(nc.vector.tensor_tensor(scale_cols[:, norm, :], scale_cols[:, norm, :],
                                             gain_cols[:, norm, :], ALU.mult))

            def update_x(unit, s_end, row, n):
                dve.wait_ge(slot_used, s_end)
                for t in range(T):
                    bank = lin[2 * (unit % 2) + t]
                    tmp = scratch[:, (2 * n + t) * 512:(2 * n + t + 1) * 512]
                    xs = x[:, t, 512 * n:512 * n + 512]
                    ins = nc.vector.tensor_tensor(tmp, bank[:], gate_rows[:, row, 512 * n:512 * n + 512],
                                                  ALU.mult)
                    if t == T - 1:
                        ins.then_inc(unit_empty_dve, 1)
                    else:
                        link(ins)
                dve.wait_ge(unit_empty_dve, count_before(UNIT_EMPTIED, unit + 1, "dve"))
                for t in range(T):
                    tmp = scratch[:, (2 * n + t) * 512:(2 * n + t + 1) * 512]
                    xs = x[:, t, 512 * n:512 * n + 512]
                    nc.vector.tensor_tensor(xs, xs, tmp, ALU.add).then_inc(resid, 1)

            def group_norm(src, n_cols, groups, width, squares_buf):
                link(nc.vector.tensor_tensor(squares_buf, src, src, ALU.mult))
                return nc.vector.tensor_reduce(stat[:, 0, n_cols:n_cols + groups], squares_buf, X, ALU.add)

            def attention(n_items, tp0, step0, emit_step):
                for n in range(n_items + 2):
                    if n < n_items:
                        m = counts["item"]
                        counts["item"] += 1
                        dve.wait_ge(scored, m + 1)
                        nc.vector.tensor_reduce(nmax[:, m % 4, 0:1], sc[m % 2][:, 0:P], X, ALU.max, negate=True)
                        nc.vector.tensor_reduce(nmax[:, m % 4, 1:2], sc[m % 2][:, P:3 * P], X, ALU.max,
                                                negate=True).then_inc(maxed, 1)
                    if n >= R + 1 and n % R == 1:
                        emit_step((n - R - 1) // R)

            def feed_forward(up, down, unit0, tp0):
                st0 = counts["st"]

                def unit(u, i=None):
                    for q in range(4):
                        s = up + 4 * u + 4 + q
                        if q == 1 and (u > 0 or i is not None):
                            batch = tp0 + u - 1
                            dve.wait_ge(st_high, at(i, st0 + u, 2))
                            cols = bass.ds(at(i, (u - 1) * 512, 1024), 512)
                            nc.vector.tensor_tensor(hid_lo[:, cols], tp[batch % 2][:],
                                                    hid_hi[:, cols].bitcast(F32),
                                                    ALU.subtract).then_inc(st_ready, 1)
                        low(s, i)
                    for t in range(T):
                        dve.wait_ge(silu_ready, at(i, silu0 + T * u + t + 1, 2 * T))
                        ins = nc.vector.tensor_tensor(hid[:, u % 2, t, :], silu_a[:, u % 2, t, :],
                                                      lin[2 * ((unit0 + u) % 2) + t][:, HU:2 * HU], ALU.mult)
                    ins.then_inc(unit_empty_dve, 1)

                silu0 = counts["silu"] if "silu" in counts else 0
                unit(0)
                with dve.Fori(0, (FU - 3) // 2) as i:
                    unit(1, i)
                    unit(2, i)
                unit(FU - 2)
                unit(FU - 1)
                counts["silu"] = silu0 + T * FU
                made[0] = down + 4
                low_to(down + 5)
                counts["st"] = st0 + FU - 1
                low_from_tp(tp0 + FU - 1, hid_hi[:, (FU - 1) * 512:FU * 512], hid_lo[:, (FU - 1) * 512:FU * 512])

            dve.wait_ge(cond_landed, 32)
            dve.wait_ge(consts, 1)
            two_pi = 2 * np.pi
            pieces, left = [], two_pi
            for bits in (7, 8, 8):
                scale = 2.0 ** (bits - 1 - np.floor(np.log2(left)))
                piece = float(np.floor(left * scale) / scale)
                pieces.append(piece)
                left -= piece
            pieces.append(float(np.float32(left)))
            ang = trig[:, 2, :]
            pos_f = stat[:, 5, 0:T]
            link(nc.vector.tensor_copy(pos_f, pos_i[:]))
            half_w = ROT // 2
            for t in range(T):
                ins = nc.vector.tensor_scalar(ang[:, t * half_w:(t + 1) * half_w], inv[:], pos_f[:, t:t + 1],
                                              None, ALU.mult)
            link(ins)
            magic = float(1.5 * 2 ** 23)
            for j in range(2):
                turns = stat[:, 6, :]
                arg = trig[:, j, :]
                link(nc.vector.tensor_scalar(turns, ang, 1.0 / two_pi, 0.25 * j, ALU.mult, ALU.add))
                link(nc.vector.tensor_scalar(turns, turns, magic, None, ALU.add))
                link(nc.vector.tensor_scalar(turns, turns, -magic, None, ALU.add))
                src = ang
                for piece in pieces:
                    link(nc.vector.scalar_tensor_tensor(arg, turns, -piece, src, ALU.mult, ALU.add))
                    src = arg
                link(nc.vector.tensor_scalar(arg, arg, float(j * np.pi / 2), None, ALU.add))
                nc.vector.tensor_scalar(arg, arg, -3.1415925, 3.1415925, ALU.max, ALU.min).then_inc(trig_arg, 1)
            dve.wait_ge(cond_ready, 1)
            for a in range(2 * KD):
                seg, kt = divmod(a, KD)
                if kt == 0:
                    dve.wait_ge(ada_bias[seg], 16)
                dve.wait_ge(ada_landed[a % ARING], 16 * (a // ARING + 1))
                if a > 0:
                    dve.wait_ge(ada_used, a)
                nc.vector.scalar_tensor_tensor(ada_acc[:, seg, :], ada_ring[:, a % ARING, :], cond[:, kt:kt + 1],
                                               ada_acc[:, seg, :], ALU.mult, ALU.add).then_inc(ada_used, 1)
            dve.wait_ge(small_in, N_SMALL)
            link(nc.vector.tensor_scalar(nsa_gains[:, 0:1], nsa_gains[:, 0:1], float(DH ** -0.5), None, ALU.mult))
            normalise_x()
            ada_columns(0)
            ada_columns(1)
            modulation(0, 1)
            modulated(0, T_H0, 0)
            low_to(4)

            def normed_keys(b, c0):
                for t in range(T):
                    src = proj[:, t, c0:c0 + G * DH].rearrange("p (g d) -> p g d", g=G)
                    sq = scratch[:, t * 256:(t + 1) * 256].rearrange("p (g d) -> p g d", g=G)
                    link(group_norm(src, t * G, G, DH, sq))
                reciprocal_roots(T * G, [(T * G, DH)])
                for t in range(T):
                    for u in range(2):
                        src = proj[:, t, c0:c0 + G * DH].rearrange("p (g d) -> p g d", g=G)
                        dst = kdup_o[:, b, t * 512:(t + 1) * 512].rearrange("p (g u d) -> p g u d", g=G, u=2)
                        ins = nc.vector.tensor_tensor(
                            dst[:, :, u, :], src,
                            stat[:, 3, t * G:(t + 1) * G].unsqueeze(2).broadcast_to([P, G, DH]), ALU.mult)
                ins.then_inc(xn_ready, 1)

            def blocks(b):
                a_view = scratch[:].rearrange("p (m g c) -> p m g c", m=CM, g=G)
                dve.wait_ge(z_done, 16 * 4 * 2)
                if b == 1:
                    dve.wait_ge(a_ready, 1)
                for g in range(G):
                    zg = z[:, b, g, :].rearrange("p (c m u) -> p u m c", u=2, m=CM // 2)
                    for hm in range(2):
                        src = zg[:, 0, :, hm:hm + NCMP]
                        pe = pe_cols[:, b, hm * 8:hm * 8 + 8].unsqueeze(2).broadcast_to([P, 8, NCMP])
                        ins = nc.vector.tensor_tensor(a_view[:, hm * 8:hm * 8 + 8, g, 0:NCMP], src, pe, ALU.add)
                ins.then_inc(a_full, 1)

            def blocks_low():
                b = counts.setdefault("blocks", 0)
                counts["blocks"] = b + 1
                dve.wait_ge(a_high, b + 1)
                nc.vector.tensor_tensor(a_lo[:].rearrange("p m c -> p (m c)"), scratch[:],
                                        a_hi[:].rearrange("p m c -> p (m c)").bitcast(F32),
                                        ALU.subtract).then_inc(a_ready, 1)

            def scaled_copy(batch, dst, gain):
                dve.wait_ge(tp_filled, batch + 1)
                nc.vector.tensor_scalar(dst, tp[batch % 2][:], gain, None, ALU.mult).then_inc(tp_empty_dve, 1)

            low_to(8)
            low_to(12)
            low_to(16)
            dve.wait_ge(unit_empty_act, 2)
            for t in range(T):
                src = proj[:, t, 0:D].rearrange("p (h d) -> p h d", h=H)
                link(group_norm(src, t * H, H, DH, scratch[:, t * D:(t + 1) * D].rearrange(
                    "p (h d) -> p h d", h=H)))
            reciprocal_roots(T * H, [(T * H, DH)])
            for t in range(T):
                src = proj[:, t, 0:D].rearrange("p (h d) -> p h d", h=H)
                ins = nc.vector.tensor_tensor(
                    src, src, stat[:, 3, t * H:(t + 1) * H].unsqueeze(2).broadcast_to([P, H, DH]), ALU.mult)
            ins.then_inc(xn_ready, 1)
            low_to(20)
            low_to(24)
            dve.wait_ge(unit_empty_act, 5)
            for b in range(2):
                for u in range(4 if b == 0 else 0):
                    batch = T_Q + u
                    scaled_copy(batch, q_t[:, 2 * u:2 * u + 2, :].rearrange("p k s -> p (k s)"),
                                nsa_gains[:, 0:1])
                normed_keys(b, 1536 + 512 * b)
            link(nc.vector.memset(scratch[:], 0.0))
            low_to(26)
            blocks(0)
            blocks_low()
            for b in range(2):
                for u in range(2):
                    scaled_copy(T_K + 2 * b + u, k_t[:, b, 2 * u:2 * u + 2, :].rearrange("p g s -> p (g s)"),
                                nsa_gains[:, 2 + b:3 + b])
            ada_row(2, 0)
            ada_columns(3)
            dve.wait_ge(gate_exp, 1)
            link(nc.vector.tensor_scalar(gates[:], gates[:], 1.0, None, ALU.add))
            link(nc.vector.reciprocal(gates[:], gates[:]))
            low_to(30)
            blocks(1)
            blocks_low()
            low_to(34)
            dve.wait_ge(cmp_out, 1)
            kc = scratch[:, 0:DH]
            link(nc.vector.tensor_copy(kc, sc[0][:, 0:DH]))
            link(group_norm(kc.unsqueeze(1), 0, 1, DH, scratch[:, DH:2 * DH].unsqueeze(1)))
            reciprocal_roots(1, [(1, DH)])
            for u in range(2):
                ins = nc.vector.tensor_scalar(scratch[:, (2 + u) * DH:(3 + u) * DH], kc, stat[:, 3, 0:1], None,
                                              ALU.mult)
            for g in range(G):
                link(nc.vector.tensor_copy(v_cmp[CP * g:CP * g + CP, g, :],
                                           sc[0][CP * g:CP * g + CP, DH:2 * DH]))
            nc.vector.tensor_copy(stat[:, 7, 0:1], stat[:, 3, 0:1]).then_inc(xn_ready, 1)
            dve.wait_ge(tp_filled, T_KC + 1)
            nc.vector.tensor_scalar(kc_t[:], tp[T_KC % 2][:, 0:P], nsa_gains[:, 1:2], None,
                                    ALU.mult).then_inc(tp_empty_dve, 1)
            gate_view = gates[:].rearrange("p t (g r u b) -> p t r g u b", g=G, u=2, b=3)
            for t in range(T):
                counts["item"] += 1
                dve.wait_ge(scored, t + 1)
                s4 = sc[t][:].rearrange("p (h c) -> p h c", c=CP)
                mx = cstat[:, t, :]
                link(nc.vector.tensor_reduce(mx, s4, X, ALU.max))
                link(nc.vector.tensor_scalar(mx, mx, FLOOR, None, ALU.max))
                nc.vector.tensor_tensor(prob[:, t, :].rearrange("p (h c) -> p h c", c=CP), s4,
                                        mx.unsqueeze(2).broadcast_to([P, H, CP]), ALU.subtract).then_inc(maxed, 1)
            for t in range(T):
                dve.wait_ge(exped, t + 1)
                cf = cstat[:, t, :]
                link(nc.vector.tensor_reduce(cf, prob[:, t, :].rearrange("p (h c) -> p h c", c=CP), X, ALU.add))
                link(nc.vector.tensor_scalar(cf, cf, TINY, None, ALU.max))
                link(nc.vector.reciprocal(cf, cf))
                for tile in range(T):
                    cf3 = cf[:, tile * 8:tile * 8 + 8].rearrange("p (r g) -> p r g", g=G)
                    link(nc.vector.tensor_tensor(cf3, cf3, gate_view[:, tile, :, :, t, 0], ALU.mult))
            for odd in range(2):
                dve.wait_ge(pv_done, odd + 1)
                for j in range(4):
                    t, pair = divmod(j, 2)
                    cf = cstat[:, odd, j * G:(j + 1) * G]
                    dst = o0[:, t, :].rearrange("p (g r d) -> p g r d", g=G, r=R)[:, :, 2 * pair + odd, :]
                    src = lin[2 * t + odd][:, pair * 256:(pair + 1) * 256].rearrange(
                        "p (g d) -> p g d", g=G)
                    ins = nc.vector.tensor_tensor(dst, src, cf.unsqueeze(2).broadcast_to([P, G, DH]), ALU.mult)
                ins.then_inc(pv_empty, 1)
            dve.wait_ge(pv_empty, T)

            def nsa_step(k):
                b, g = divmod(k, G)
                cf = coef[:, 0, :]
                dve.wait_ge(pv_done, T + k + 1)
                link(nc.vector.tensor_scalar(cf, sums[:, k % 2, :], TINY, None, ALU.max))
                link(nc.vector.reciprocal(cf, cf))
                gv = gates[:].rearrange("p t (h b) -> p t h b", b=3)[:, :, R * g:R * g + R, 1 + b]
                cf3 = cf.rearrange("p (t r) -> p t r", t=T)
                link(nc.vector.tensor_tensor(cf3, cf3, gv, ALU.mult))
                tmp = scratch[:, 512 * (k % 2):512 * (k % 2) + 512]
                nc.vector.tensor_tensor(tmp.rearrange("p (h d) -> p h d", d=DH),
                                        lin[k % 4][:].rearrange("p (h d) -> p h d", d=DH),
                                        cf.unsqueeze(2).broadcast_to([P, T * R, DH]),
                                        ALU.mult).then_inc(pv_empty, 1)
                dve.wait_ge(pv_empty, T + k + 1)
                og = o0[:, :, 256 * g:256 * g + 256]
                ins = nc.vector.tensor_tensor(og, og, tmp.rearrange("p (t n) -> p t n", t=T), ALU.add)
                ins.then_inc(o_steps, 1)

            attention(2 * H, T_P0, T, nsa_step)

            def output_low(batch0):
                for m in range(4):
                    low_from_tp(batch0 + m, st_hi[:, 2 * m:2 * m + 2, :].rearrange("p k s -> p (k s)"),
                                st_lo[:, 2 * m:2 * m + 2, :].rearrange("p k s -> p (k s)"))

            output_low(T_O0)
            low_to(OUT0 + 8)
            update_x(U_OUT0, OUT0 + 4, 0, 0)
            low_to(OUT0 + 12)
            update_x(U_OUT0 + 1, OUT0 + 8, 0, 1)
            ada_columns(4)
            ada_row(5, 1)
            normalise_x()
            modulation(1, 4)
            modulated(1, T_HF0, 3)
            feed_forward(UP0, DOWN0, U_UP0, T_HID0)
            ada_columns(6)
            ada_columns(7)
            low_to(DOWN0 + FK + 4)
            for n in range(2):
                update_x(U_DOWN0 + n, DOWN0 + FK, 1, n)

            normalise_x()
            modulation(2, 7)
            modulated(2, T_H1, 6)
            low_to(QB1)
            ada_row(8, 0)
            ada_columns(9)
            counts["squares"] += 6
            dve.wait_ge(squares, counts["squares"])
            reciprocal_roots(6, [(2, QL), (2, KVL), (2, ROT)])
            for n, (c0, w) in enumerate(((0, QL), (QL, KVL), (QL + KVL, ROT))):
                for t in range(T):
                    src = proj1[:, t, c0:c0 + w]
                    ins = nc.vector.tensor_scalar(src, src, stat[:, 3, 2 * n + t:2 * n + t + 1], None, ALU.mult)
            ins.then_inc(xn_ready, 1)
            scale_and_split(T_CQ, 0, 2, lat_gains[:, 0:2], None)
            scale_and_split(T_CQ + 1, 2, 1, lat_gains[:, 2:3], None)
            scale_and_split(T_CQ + 2, 3, 2, lat_gains[:, 3:5], None)
            low_to(QB1 + 4)
            dve.wait_ge(trig_done, 1)
            sin, cos = cs[:, 0], cs[:, 1]
            hw = ROT // 2

            def rotate(v, t, heads):
                def bc(a):
                    return a[:, t, :].unsqueeze(1).broadcast_to([P, heads, hw])
                n = heads * hw
                p = [scratch[:, j * 256:j * 256 + n].rearrange("p (h d) -> p h d", h=heads) for j in range(4)]
                x1, x2 = v[:, :, 0:hw], v[:, :, hw:ROT]
                nc.vector.tensor_tensor(p[0], x1, bc(cos), ALU.mult)
                nc.vector.tensor_tensor(p[1], x2, bc(sin), ALU.mult)
                nc.vector.tensor_tensor(p[2], x1, bc(sin), ALU.mult)
                link(nc.vector.tensor_tensor(p[3], x2, bc(cos), ALU.mult))
                link(nc.vector.tensor_tensor(x1, p[0], p[1], ALU.subtract))
                return nc.vector.tensor_tensor(x2, p[2], p[3], ALU.add)

            for t in range(T):
                kr = proj1[:, t, QL + KVL:MLA_IN]
                link(nc.vector.tensor_tensor(kr, kr, k_gain_row[:, NOPE:DQ], ALU.mult))
                link(rotate(kr.unsqueeze(1), t, 1))
                link(nc.vector.tensor_copy(k_tok[:, t, :, NOPE:DQ], kr.unsqueeze(1).broadcast_to([P, H, ROT])))
            low_to(QB1 + 6)
            low_to(KVB1 + 4)
            low_to(OUT1)
            dve.wait_ge(unit_empty_act, count_before(UNIT_EMPTIED, U_KVB1, "act"))
            for t in range(T):
                src = q_tok[:, t, :].rearrange("p (h d) -> p h d", h=H)
                link(group_norm(src, t * H, H, DQ, scratch[:, 0:H * DQ].rearrange("p (h d) -> p h d", h=H)))
            reciprocal_roots(T * H, [(T * H, DQ)])
            for t in range(T):
                src = q_tok[:, t, :].rearrange("p (h d) -> p h d", h=H)
                link(nc.vector.tensor_tensor(
                    src, src, stat[:, 3, t * H:(t + 1) * H].unsqueeze(2).broadcast_to([P, H, DQ]), ALU.mult))
                link(nc.vector.tensor_tensor(
                    src, src, q_gain_row[:].unsqueeze(1).broadcast_to([P, H, DQ]), ALU.mult))
                link(rotate(src[:, :, NOPE:DQ], t, H))
            dve.sem_inc(xn_ready, 1)
            low_to(OUT1 + 4)
            dve.wait_ge(unit_empty_act, count_before(UNIT_EMPTIED, U_OUT1, "act"))
            for t in range(T):
                link(group_norm(k_tok[:, t, :, 0:NOPE], t * H, H, NOPE,
                                scratch[:, 0:H * NOPE].rearrange("p (h d) -> p h d", h=H)))
            reciprocal_roots(T * H, [(T * H, NOPE)])
            for t in range(T):
                src = k_tok[:, t, :, 0:NOPE]
                link(nc.vector.tensor_tensor(
                    src, src, stat[:, 3, t * H:(t + 1) * H].unsqueeze(2).broadcast_to([P, H, NOPE]), ALU.mult))
                ins = nc.vector.tensor_tensor(
                    src, src, k_gain_row[:, 0:NOPE].unsqueeze(1).broadcast_to([P, H, NOPE]), ALU.mult)
            ins.then_inc(xn_ready, 1)
            for j in range(8):
                dve.wait_ge(tp_filled, T_K1 + j + 1)
                nc.vector.tensor_copy(k1_t[:, 2 * j:2 * j + 2, :].rearrange("p h s -> p (h s)"),
                                      tp[(T_K1 + j) % 2][0:DQ, :]).then_inc(tp_empty_dve, 1)

            def mla_step(k):
                cf = coef[:, 0, :]
                dve.wait_ge(pv_done, T + 8 + k + 1)
                link(nc.vector.tensor_scalar(cf, sums[:, k % 2, :], TINY, None, ALU.max))
                link(nc.vector.reciprocal(cf, cf))
                og = o1[:, :, 256 * k:256 * k + 256].rearrange("p t (r d) -> p t r d", d=DH)
                ps = lin[k % 4][:].rearrange("p (t r d) -> p t r d", t=T, d=DH)
                for t in range(T):
                    ins = nc.vector.tensor_tensor(og[:, t], ps[:, t], cf[:, t * R:(t + 1) * R].unsqueeze(
                        2).broadcast_to([P, R, DH]), ALU.mult)
                ins.then_inc(o_steps, 1)

            attention(H, T_P1, T + 8, mla_step)
            output_low(T_O1)
            low_to(OUT1 + 8)
            update_x(U_OUT1, OUT1 + 4, 0, 0)
            low_to(OUT1 + 12)
            update_x(U_OUT1 + 1, OUT1 + 8, 0, 1)
            ada_columns(10)
            ada_row(11, 1)
            normalise_x()
            modulation(3, 10)
            modulated(3, T_HF1, 9)
            feed_forward(UP1, DOWN1, U_UP1, T_HID1)
            low_to(END)
            for n in range(2):
                update_x(U_DOWN1 + n, END, 1, n)

        @block.tensor
        def _(pe):
            xn = [0]

            def three(bank, a_h, a_l, w_h, w_l, first, last):
                nc.tensor.matmul(bank, a_h, w_h, start=first, stop=False)
                nc.tensor.matmul(bank, a_h, w_l, start=False, stop=False)
                return nc.tensor.matmul(bank, a_l, w_h, start=False, stop=last)

            def wait_unit(unit, i=None):
                if unit < 2 and i is None:
                    return
                who = UNIT_EMPTIED[unit - 2]
                pe.wait_ge(unit_empty[who], at(i, count_before(UNIT_EMPTIED, unit - 1, who), 2))

            def wait_tp(batch, i=None):
                if batch < 2 and i is None:
                    return
                who = TP_EMPTIED[batch - 2]
                if who == "act":
                    pe.wait_ge(tp_empty["act"], count_before(TP_EMPTIED, batch - 1, who))
                else:
                    pe.wait_ge(*dve_emptied(batch - 2, i))

            def dve_emptied(batch, i=None):
                for first, n, st in ((T_H0, 4, ST_H0), (T_O0, 4, ST_O0), (T_HF0, 4, ST_HF0),
                                     (T_HID0, FU, ST_HID0), (T_H1, 4, ST_H1), (T_CQ, 3, ST_CQ),
                                     (T_O1, 4, ST_O1), (T_HF1, 4, ST_HF1), (T_HID1, FU, ST_HID1)):
                    if first <= batch < first + n:
                        return st_ready, at(i, st + batch - first + 1, 2)
                alone = 0
                for first, n in ((T_Q, 4), (T_K, 4), (T_KC, 1), (T_K1, 8)):
                    if first <= batch < first + n:
                        return tp_empty_dve, alone + batch - first + 1
                    alone += n

            def transposes(batch, pieces, rows=P):
                wait_tp(batch)
                for n, src in enumerate(pieces):
                    ins = nc.tensor.transpose(tp[batch % 2][0:rows, n * P:(n + 1) * P], src, ident[:])
                ins.then_inc(tp_filled, 1)

            def unit(unit, s0, slots, n, lhs, wait_st=None):
                wait_unit(unit)
                total = sum(len(k) for k in slots)
                done = 0
                for q, kts in enumerate(slots):
                    s = s0 + q
                    pe.wait_ge(lo_ready, s + 1)
                    wh = w_hi[:, s % RING, 0:len(kts) * n].rearrange("p (k c) -> p k c", c=n)
                    wl = w_lo[:, s % RING, 0:len(kts) * n].rearrange("p (k c) -> p k c", c=n)
                    for j, k in enumerate(kts):
                        if wait_st is not None:
                            wait_st(k)
                        for t, (ah, al) in enumerate(lhs(k)):
                            ins = three(lin[2 * (unit % 2) + t][:, 0:n], ah, al, wh[:, j], wl[:, j],
                                        done == 0, done == total - 1)
                        done += 1
                    ins.then_inc(slot_used, 1)

            def stationary(k):
                return [(st_hi[:, k, t * P:(t + 1) * P], st_lo[:, k, t * P:(t + 1) * P]) for t in range(T)]

            def st_wait(first):
                def wait(k):
                    if k % 2 == 0:
                        pe.wait_ge(st_ready, first + k // 2 + 1)
                return wait

            FOUR = [[0, 1], [2, 3], [4, 5], [6, 7]]

            def transposed_x(batch0):
                xn[0] += T
                pe.wait_ge(xn_ready, xn[0])
                for m in range(4):
                    transposes(batch0 + m, [scratch[:, t * D + k * P:t * D + (k + 1) * P]
                                            for k in (2 * m, 2 * m + 1) for t in range(T)])

            def transposed_o(batch0, o, steps):
                pe.wait_ge(o_steps, steps)
                for m in range(4):
                    transposes(batch0 + m, [o[:, t, k * P:(k + 1) * P] for k in (2 * m, 2 * m + 1)
                                            for t in range(T)])

            def wait_acc(seg):
                if seg < 2:
                    pe.wait_ge(ada_used, KD * (seg + 1))
                else:
                    pe.wait_ge(acc_pool, seg - 1)
                if seg > 0:
                    pe.wait_ge(ada_out, seg)

            def reduce_columns(seg):
                wait_acc(seg)
                for k in range(KD):
                    ins = nc.tensor.matmul(sc[seg % 2][:, k:k + 1], ada_acc[:, seg % 2, k * P:(k + 1) * P],
                                           ones[:, 0:1], start=True, stop=True)
                ins.then_inc(ada_red, 1)

            def reduce_row(seg):
                wait_acc(seg)
                for n in range(2):
                    ins = nc.tensor.matmul(sc[n][:], ones[:], ada_acc[:, seg % 2, 512 * n:512 * n + 512],
                                           start=True, stop=True)
                ins.then_inc(ada_red, 1)

            def attention(n_items, item0, tp0, step0, q_of, k_of, v_of, prob_b, prob_tb):
                for n in range(n_items + 2):
                    if n < n_items:
                        m = item0 + n
                        if n >= 1:
                            pe.wait_ge(exped, m - 1)
                        bank = sc[m % 2]
                        nc.tensor.matmul(bank[:, 0:3 * P], ident_b[:], tri[:].rearrange("p a b -> p (a b)"),
                                         start=True, stop=False)
                        nc.tensor.matmul(bank[:, 0:P], q_of(n, 0), k_of(n, 1), start=False, stop=False)
                        nc.tensor.matmul(bank[:, P:3 * P], q_of(n, 1), k_of(n, 2), start=False,
                                         stop=True).then_inc(scored, 1)
                    if 1 <= n <= n_items:
                        i = n - 1
                        pe.wait_ge(exped, item0 + i + 1)
                        transposes(tp0 + i, [prob_b[:, i % 2, j * P:(j + 1) * P] for j in range(3)])
                    if n >= 2:
                        i = n - 2
                        step, r = divmod(i, R)
                        who, cnt = "act", count_before(TP_EMPTIED, tp0 + i + 1, "act")
                        pe.wait_ge(tp_empty[who], cnt)
                        if r == 0 and step0 + step >= step0 + 4:
                            pe.wait_ge(pv_empty, step0 + step - 3)
                        bank = lin[step % 4]
                        pt = prob_tb[:, i % 2, :]
                        nc.tensor.matmul(bank[:, r * DH:(r + 1) * DH], pt[:, 0:P], v_of(i, 0),
                                         start=True, stop=True)
                        lo = (R + r) * DH
                        nc.tensor.matmul(bank[:, lo:lo + DH], pt[:, P:2 * P], v_of(i, 0), start=True, stop=False)
                        ins = nc.tensor.matmul(bank[:, lo:lo + DH], pt[:, 2 * P:3 * P], v_of(i, 1),
                                               start=False, stop=True)
                        if r == R - 1:
                            ins.then_inc(pv_done, 1)

            def feed_forward(up, down, unit0, tp0, st_h, hid0, up_reduce):
                def one(u, i=None):
                    wait_unit(unit0 + u, i)
                    for q in range(4):
                        s = up + 4 * u + q
                        pe.wait_ge(lo_ready, at(i, s + 1, 8))
                        for j in range(2):
                            k = 2 * q + j
                            if j == 0 and u == 0 and i is None:
                                pe.wait_ge(st_ready, st_h + q + 1)
                            for t, (ah, al) in enumerate(stationary(k)):
                                ins = three(lin[2 * ((unit0 + u) % 2) + t][:], ah, al,
                                            w_hi[:, s % RING, 512 * j:512 * j + 512],
                                            w_lo[:, s % RING, 512 * j:512 * j + 512], k == 0, k == KD - 1)
                        ins.then_inc(slot_used, 1)
                        if q == 0 and (u > 0 or i is not None):
                            hidden(u - 1, i)

                def hidden(u, i=None):
                    batch = tp0 + u
                    pe.wait_ge(unit_empty_dve, at(i, count_before(UNIT_EMPTIED, unit0 + u + 1, "dve"), 2))
                    sem_, value = dve_emptied(batch - 2, None)
                    pe.wait_ge(sem_, at(i, value, 2))
                    for n in range(4):
                        k, t = divmod(n, 2)
                        ins = nc.tensor.transpose(tp[batch % 2][:, n * P:(n + 1) * P],
                                                  hid[:, u % 2, t, k * P:(k + 1) * P], ident[:])
                    ins.then_inc(tp_filled, 1)

                one(0)
                with pe.Fori(0, (FU - 3) // 2) as i:
                    one(1, i)
                    one(2, i)
                one(FU - 2)
                one(FU - 1)
                for n in range(2):
                    wait_unit(unit0 + FU + n)
                for k in range(FK):
                    s = down + k
                    pe.wait_ge(lo_ready, s + 1)
                    pe.wait_ge(st_ready, hid0 + k // 2 + 1)
                    for t in range(T):
                        c0 = k * S + t * P
                        for n in range(2):
                            ins = three(lin[2 * ((unit0 + FU + n) % 2) + t][:], hid_hi[:, c0:c0 + P],
                                        hid_lo[:, c0:c0 + P], w_hi[:, s % RING, 512 * n:512 * n + 512],
                                        w_lo[:, s % RING, 512 * n:512 * n + 512], k == 0, k == FK - 1)
                    ins.then_inc(slot_used, 1)
                    if k == 0:
                        hidden(FU - 1)
                        for seg in up_reduce:
                            reduce_columns(seg)

            pe.wait_ge(consts, 1)
            reduce_columns(0)
            reduce_columns(1)
            transposed_x(T_H0)
            for u in range(4):
                unit(u, IN0 + 4 * u, FOUR, 512, stationary, st_wait(ST_H0) if u == 0 else None)
            for b in range(2):
                c0 = 1024 + 256 * b
                pe.wait_ge(unit_empty_act, 3)
                transposes(T_KVC + b, [proj[:, t, c0 + P * j:c0 + P * (j + 1)] for j in range(2) for t in range(T)])
            unit(4, IN0 + 16, FOUR, 512, stationary)
            xn[0] += 1
            pe.wait_ge(xn_ready, xn[0])
            for m in range(4):
                transposes(T_Q + m, [proj[:, t, k * P:(k + 1) * P] for k in (2 * m, 2 * m + 1) for t in range(T)])
            unit(5, GATE0, [[0, 1, 2, 3], [4, 5, 6, 7]], 48, stationary)
            for b in range(2):
                xn[0] += 1
                pe.wait_ge(xn_ready, xn[0])
                for m in range(2):
                    transposes(T_K + 2 * b + m, [kdup_o[:, b, t * 512 + g * P:t * 512 + (g + 1) * P]
                                                 for g in (2 * m, 2 * m + 1) for t in range(T)])
            reduce_row(2)
            reduce_columns(3)
            for b in range(2):
                pe.wait_ge(a_ready, b + 1)
                unit(U_CMP0 + b, CMP0 + 4 * b, [[0, 1, 2, 3], [4, 5, 6, 7], [8, 9, 10, 11], [12, 13, 14, 15]], CH,
                     lambda k: [(a_hi[:, k, :], a_lo[:, k, :])])
            pe.wait_ge(unit_empty_act, 8)
            transposes(T_SC, [tfull[:, 0, j * P:(j + 1) * P] for j in range(4)])
            pe.wait_ge(tp_empty_act, count_before(TP_EMPTIED, T_SC + 1, "act"))
            pe.wait_ge(ada_out, 4)
            for b in range(2):
                for k in range(2):
                    ins = nc.tensor.matmul(sc[0][:, b * DH:(b + 1) * DH],
                                           prob_t[:, 1, (2 * b + k) * P:(2 * b + k + 1) * P], w2[:, b, k, :],
                                           start=(k == 0), stop=(k == 1))
            ins.then_inc(cmp_out, 1)
            xn[0] += 1
            pe.wait_ge(xn_ready, xn[0])
            transposes(T_KC, [scratch[:, 2 * DH:4 * DH]])
            pe.wait_ge(tp_empty_dve, 9)
            for odd in range(2):
                nc.tensor.matmul(sc[odd][:], ident_b[:], cmp_mask[:].rearrange("p t c -> p (t c)"),
                                 start=True, stop=False)
                for t in range(T):
                    for pair in range(R // 2):
                        for g in range(G):
                            c0 = ((t * 2 + pair) * G + g) * CP
                            ins = nc.tensor.matmul(
                                sc[odd][:, c0:c0 + CP],
                                q_t[64 * odd:64 * odd + 64, 2 * g + pair, t * P:(t + 1) * P],
                                kc_t[64 * odd:64 * odd + 64, g * CP:(g + 1) * CP], start=False,
                                stop=(c0 == 512 - CP))
                ins.then_inc(scored, 1)
            for odd in range(2):
                pe.wait_ge(exped, odd + 1)
                transposes(T_PC + odd, [prob[:, odd, j * P:(j + 1) * P] for j in range(4)])
            for odd in range(2):
                pe.wait_ge(tp_empty_act, count_before(TP_EMPTIED, T_PC + odd + 1, "act"))
                for j in range(4):
                    t, pair = divmod(j, 2)
                    ins = nc.tensor.matmul(lin[2 * t + odd][:, pair * 256:(pair + 1) * 256],
                                           prob_t[:, odd, j * P:(j + 1) * P],
                                           v_cmp[:].rearrange("p g d -> p (g d)"), start=True, stop=True)
                ins.then_inc(pv_done, 1)
            pe.wait_ge(pv_empty, 2)

            def nsa_q(n, t):
                h = n % H
                p0 = 64 * (h % 2)
                return q_t[p0:p0 + 64, h // 2, t * P:(t + 1) * P]

            def nsa_k(n, tiles):
                b, h = divmod(n, H)
                p0 = 64 * (h % 2)
                return k_t[p0:p0 + 64, b, h // R, 0:tiles * P]

            def nsa_v(n, t):
                b, h = divmod(n, H)
                c0 = 1792 + 512 * b + (h // R) * DH
                return proj[:, t, c0:c0 + DH]

            attention(2 * H, T, T_P0, T, nsa_q, nsa_k, nsa_v, prob, prob_t)
            transposed_o(T_O0, o0, 2 * G)
            unit(U_OUT0, OUT0, FOUR, 512, stationary, st_wait(ST_O0))
            unit(U_OUT0 + 1, OUT0 + 4, FOUR, 512, stationary)
            reduce_columns(4)
            reduce_row(5)
            transposed_x(T_HF0)
            feed_forward(UP0, DOWN0, U_UP0, T_HID0, ST_HF0, ST_HID0, (6, 7))

            transposed_x(T_H1)
            unit(U_IN1, IN1, FOUR, 512, stationary, st_wait(ST_H1))
            unit(U_IN1 + 1, INB1, [[0, 1, 2, 3], [4, 5, 6, 7]], 160, stationary)
            reduce_row(8)
            reduce_columns(9)
            xn[0] += 1
            pe.wait_ge(xn_ready, xn[0])
            transposes(T_CQ, [proj1[:, t, k * P:(k + 1) * P] for k in (0, 1) for t in range(T)])
            transposes(T_CQ + 1, [proj1[:, t, 2 * P:3 * P] for t in range(T)])
            transposes(T_CQ + 2, [proj1[:, t, k * P:(k + 1) * P] for k in (3, 4) for t in range(T)])
            pe.wait_ge(st_ready, ST_CQ + 2)
            for u in range(3):
                unit(U_QB1 + u, QB1 + 2 * u, [[0, 1], [2]], 512, stationary)
            pe.wait_ge(st_ready, ST_CQ + 3)
            for u in range(4):
                unit(U_KVB1 + u, KVB1 + u, [[3, 4]], 512, stationary)
            for which, batch0 in ((0, T_Q1), (1, T_K1)):
                xn[0] += 1
                pe.wait_ge(xn_ready, xn[0])
                for j in range(8):
                    def head(t, h):
                        if which == 0:
                            return q_tok[:, t, h * DQ:(h + 1) * DQ]
                        return k_tok[:, t, h, :]
                    transposes(batch0 + j, [head(t, h) for h in (2 * j, 2 * j + 1) for t in range(T)], DQ)
            pe.wait_ge(tp_empty_act, count_before(TP_EMPTIED, T_K1, "act"))
            pe.wait_ge(tp_empty_dve, 17)
            pe.wait_ge(ada_out, 10)
            attention(H, T + 2 * H, T_P1, T + 8,
                      lambda n, t: q1_t[:, n, t * P:(t + 1) * P],
                      lambda n, tiles: k1_t[:, n, 0:tiles * P],
                      lambda n, t: v_tok[:, t, n, :], prob1, prob1_t)
            transposed_o(T_O1, o1, 3 * G)
            unit(U_OUT1, OUT1, FOUR, 512, stationary, st_wait(ST_O1))
            unit(U_OUT1 + 1, OUT1 + 4, FOUR, 512, stationary)
            reduce_columns(10)
            reduce_row(11)
            transposed_x(T_HF1)
            feed_forward(UP1, DOWN1, U_UP1, T_HID1, ST_HF1, ST_HID1, ())


_INS = ['x', 'c', 'positions', 'ada_w', 'ada_b', 'norm_mix', 'norm_ffn', 'ffn_w_in', 'ffn_w_out',
        'nsa_w_in', 'nsa_q_norm', 'nsa_k_norm', 'nsa_cmp_pe', 'nsa_cmp_w1', 'nsa_cmp_w2', 'nsa_w_out',
        'mla_w_in', 'mla_q_a_norm', 'mla_kv_a_norm', 'mla_w_q_b', 'mla_w_kv_b', 'mla_q_norm',
        'mla_k_norm', 'mla_w_out']


def kernel(**inputs):
    import concourse.bacc as bacc
    from concourse.bass_utils import run_bass_kernel_spmd

    nc = bacc.Bacc("TRN2", target_bir_lowering=False, num_devices=1)
    arrays, args = {}, []
    for name in _INS:
        a = np.ascontiguousarray(inputs[name])
        arrays[f"in_{name}_dram"] = a
        args.append(nc.dram_tensor(f"in_{name}_dram", a.shape, mybir.dt.from_np(a.dtype),
                                   kind="ExternalInput").ap())
    args.append(nc.dram_tensor("out_0_dram", (1, S, D), F32, kind="ExternalOutput").ap())
    trunk(nc, *args)
    r = run_bass_kernel_spmd(nc, [arrays], core_ids=[0])
    return r.results[0]["out_0_dram"]
```

```python
from contextlib import ExitStack

import numpy as np

import concourse.bass as bass
from concourse import mybir

F32 = mybir.dt.float32
F32R = mybir.dt.float32r
BF16 = mybir.dt.bfloat16
I32 = mybir.dt.int32
ACT = mybir.ActivationFunctionType
ALU = mybir.AluOpType
X = mybir.AxisListType.X

P = 128
S = 256
T = S // P
D = 1024
KD = D // P
EPS = 1e-6
MASKED = -1e30
FLOOR = -1e29
TINY = 1e-30
H = 16
DH = 64
G = 4
R = H // G
STRIDE = 16
CLEN = 32
NCMP = S // STRIDE - 1
CP = 32
CM = CLEN * DH // P
CH = 256
NSA_IN = H * DH + 6 * G * DH + 3 * H
QL, KVL, ROT, NOPE = 384, 256, 32, 64
DQ = NOPE + ROT
QU = R * DQ
MLA_IN = QL + KVL + ROT
FH = 2816
HU = 256
FU = FH // HU
FK = FH // P
NSEG = 12
RING = 4
ARING = 3
HALF = 1024
LAST_UP = FU - 1

KVC0 = 0
KVS0 = KVC0 + 4
KVW0 = KVS0 + 4
CMPK0 = KVW0 + 4
QA0 = CMPK0 + 4
CMPV0 = QA0 + 4
QB0 = CMPV0 + 4
GATE0 = QB0 + 4
OUT0 = GATE0 + 2
UP0 = OUT0 + 8
DOWN0 = UP0 + 4 * FU
IN1 = DOWN0 + FK
INB1 = IN1 + 4
KVB1 = INB1 + 2
QB1 = KVB1 + 4
OUT1 = QB1 + 8
UP1 = OUT1 + 8
DOWN1 = UP1 + 4 * FU
END = DOWN1 + FK
NSA_UNITS = {KVC0: 1024, KVS0: 1536, KVW0: 2048, QA0: 0, QB0: 512}

UNIT_EMPTIED = ["act"] * 8 + ["dve"] * (2 + FU + 2) + ["act"] * 10 + ["dve"] * (2 + FU + 2)
U_KVC, U_KVS, U_KVW, U_CMPK, U_QA, U_CMPV, U_QB, U_GATE = range(8)
U_OUT0, U_UP0 = 8, 10
U_DOWN0 = U_UP0 + FU
U_IN1 = U_DOWN0 + 2
U_KVB1 = U_IN1 + 2
U_QB1 = U_KVB1 + 4
U_OUT1 = U_QB1 + 4
U_UP1 = U_OUT1 + 2
U_DOWN1 = U_UP1 + FU

TP_EMPTIED = []


def _batches(n, *who):
    TP_EMPTIED.extend(who[i % len(who)] for i in range(n))
    return len(TP_EMPTIED) - n


T_H0 = _batches(4, "st")
T_KVC = _batches(2, "act")
T_SC = _batches(1, "act")
T_K = _batches(4, "act")
T_Q = _batches(4, "dve")
T_KC = _batches(1, "dve")
T_PC = _batches(2, "act")
T_P0 = _batches(2 * H, "act", "dve")
T_O0 = _batches(4, "st")
T_HF0 = _batches(4, "st")
T_HID0 = _batches(FU, "st")
T_H1 = _batches(4, "st")
T_CQ = _batches(3, "st")
T_K1 = _batches(8, "act")
T_Q1 = _batches(8, "act", "dve")
T_P1 = _batches(H, "act", "dve")
T_O1 = _batches(4, "st")
T_HF1 = _batches(4, "st")
T_HID1 = _batches(FU, "st")


def count_before(owners, n, who):
    return sum(o == who for o in owners[:n])


def stationary_number(batch):
    return count_before(TP_EMPTIED, batch, "st")


def trunk(nc, x_in, c_in, positions, ada_w, ada_b, norm_mix, norm_ffn, ffn_w_in, ffn_w_out,
          nsa_w_in, nsa_q_norm, nsa_k_norm, nsa_cmp_pe, nsa_cmp_w1, nsa_cmp_w2, nsa_w_out,
          mla_w_in, mla_q_a_norm, mla_kv_a_norm, mla_w_q_b, mla_w_kv_b, mla_q_norm, mla_k_norm,
          mla_w_out, out):
    ctx = ExitStack()
    with ctx:
        def sb(name, shape, dt, stack=ctx):
            return stack.enter_context(nc.sbuf_tensor(name, shape, dt))

        def sem(name):
            return ctx.enter_context(nc.semaphore(name))

        raw = sb("raw", [P, RING, 2 * HALF], F32)
        w_hi = sb("w_hi", [P, RING, HALF], F32R)
        w_lo = sb("w_lo", [P, RING, HALF], F32R)
        ada_ring = sb("ada_ring", [P, ARING, D], F32)
        ada_acc = sb("ada_acc", [P, 2, D], F32)
        x = sb("x", [P, T, D], F32)
        st_hi = sb("st_hi", [P, KD, S], F32R)
        st_lo = sb("st_lo", [P, KD, S], F32R)
        gate_rows = sb("gate_rows", [P, 2, D], F32)
        scratch = sb("scratch", [P, 2 * D], F32)
        tfull = sb("tfull", [P, 2, 512], F32)
        ident = sb("ident", [P, P], F32)
        ident_b = sb("ident_b", [P, P], BF16)
        ones = sb("ones", [P, P], F32)
        tri = sb("tri", [P, P], BF16)
        cmp_mask = sb("cmp_mask", [P, T, H // 2 * CP], BF16)
        cond = sb("cond", [P, KD], F32)
        gain_cols = sb("gain_cols", [P, 4, KD], F32)
        ada_cols = sb("ada_cols", [P, NSEG, KD], F32)
        scale_cols = sb("scale_cols", [P, 4, KD], F32)
        nsa_gains = sb("nsa_gains", [P, 4], F32)
        pe_cols = sb("pe_cols", [P, 2, CM], F32)
        w2 = sb("w2", [P, 2, CH // P, DH], F32)
        lat_gains = sb("lat_gains", [P, 5], F32)
        q_gain_row = sb("q_gain_row", [P, ROT], F32)
        k_gain_row = sb("k_gain_row", [P, ROT], F32)
        qk_gain_cols = sb("qk_gain_cols", [P, 2], F32)
        pos_i = sb("pos_i", [P, T], I32)
        inv = sb("inv", [P, ROT // 2], F32)
        cs = sb("cs", [P, 2, T, ROT // 2], F32)
        trig = sb("trig", [P, 3, T * ROT // 2], F32)
        stat = sb("stat", [P, 8, 32], F32)
        table_exp = sb("table_exp", [P, 1], F32)
        nmax = sb("nmax", [P, 4, 2], F32)
        sums = sb("sums", [P, 4, T * R], F32)
        coef = sb("coef", [P, 3, T * R], F32)

        lin = [ctx.enter_context(nc.psum_tensor(f"lin{n}", [P, 512], F32)) for n in range(4)]
        tp = [ctx.enter_context(nc.psum_tensor(f"tp{n}", [P, 512], F32)) for n in range(2)]
        sc = [ctx.enter_context(nc.psum_tensor(f"sc{n}", [P, 512], F32)) for n in range(2)]
        score = [sc[0], sc[1], lin[2], lin[3]]
        CMP_BANKS = [lin[2], lin[3], lin[0], lin[1]]

        nsa = ExitStack()
        with nsa:
            proj = sb("proj", [P, T, NSA_IN], F32, nsa)
            kdup_o = sb("kdup_o", [P, 2, T * G * 2 * DH], F32, nsa)
            q_t = sb("q_t", [P, H // 2, S], F32, nsa)
            k_even = sb("k_even", [P, 2, G, S], F32, nsa)
            z = sb("z", [P, 2, G, S], F32, nsa)
            a_lo = sb("a_lo", [P, CM, G * CP], F32R, nsa)
            kc_t = sb("kc_t", [P, 2, G, CP], F32, nsa)
            gates = sb("gates", [P, T, 3 * H], F32, nsa)
            v_cmp = sb("v_cmp", [P, G, DH], F32, nsa)
            cstat = sb("cstat", [P, 3, H], F32, nsa)
            compression = ExitStack()
            with compression:
                a_hi = sb("a_hi", [P, CM, G * CP], F32R, compression)
            k_odd = sb("k_odd", [P, 2, G, S], F32, nsa)
            k_t = [k_even, k_odd]
        z_flat = z[:].rearrange("p b g s -> p (b g s)")
        prob = z_flat[:, 0:9 * P].rearrange("p (b n) -> p b n", b=3)
        prob_t = z_flat[:, 9 * P:15 * P].rearrange("p (b n) -> p b n", b=2)
        probc_t = scratch[:, 0:2 * 512].rearrange("p (b n) -> p b n", b=2)
        sc_t = z_flat[:, 3 * 512:4 * 512]
        ffn = ExitStack()
        with ffn:
            hid_hi = sb("hid_hi", [P, FK * S], F32R, ffn)
            hid_lo = sb("hid_lo", [P, FK * S], F32R, ffn)
            silu_a = sb("silu_a", [P, 2, T, HU], F32, ffn)
            hid = sb("hid", [P, 2, T, HU], F32, ffn)
        mla = ExitStack()
        with mla:
            proj1 = sb("proj1", [P, T, MLA_IN], F32, mla)
            q_tok = sb("q_tok", [P, T, H * DQ], F32, mla)
            k_tok = sb("k_tok", [P, T, H, DQ], F32, mla)
            v_tok = sb("v_tok", [P, T, H, DH], F32, mla)
            q_sq = sb("q_sq", [P, T, QU], F32, mla)
            cs_q = sb("cs_q", [P, 4, T, ROT // 2], F32, mla)
            q1_t = sb("q1_t", [P, H, S], F32, mla)
            k1_t = sb("k1_t", [P, H, S], F32, mla)
        q_flat = q_t[:].rearrange("p k s -> p (k s)")
        qsq = q_flat[:, 0:1024]
        q_squares = [tfull[:].rearrange("p b n -> p (b n)")[:, 0:T * QU].rearrange("p (t n) -> p t n", t=T),
                     q_sq[:]]
        kv_t = q_flat[:, 1024:2048].rearrange("p (b n) -> p b n", b=2)
        o0 = kdup_o[:, :, :].rearrange("p t n -> p (t n)").rearrange("p (t n) -> p t n", t=T)
        q_tok_flat = q_tok[:, :, :].rearrange("p t n -> p (t n)")
        k_tok_flat = k_tok[:, :, :, :].rearrange("p t h d -> p (t h d)")
        o1 = q_tok_flat[:, 0:T * D].rearrange("p (t n) -> p t n", t=T)
        prob1 = k_tok_flat[:, 0:9 * P].rearrange("p (b n) -> p b n", b=3)
        prob1_t = k_tok_flat[:, 9 * P:15 * P].rearrange("p (b n) -> p b n", b=2)

        small_in = sem("small_in")
        x_in_done = sem("x_in_done")
        landed = [sem(f"landed{n}") for n in range(RING)]
        hi_ready = sem("hi_ready")
        lo_ready = sem("lo_ready")
        slot_used = sem("slot_used")
        unit_empty_act = sem("unit_empty_act")
        unit_empty_dve = sem("unit_empty_dve")
        unit_empty = {"act": unit_empty_act, "dve": unit_empty_dve}
        tp_filled = sem("tp_filled")
        tp_empty_act = sem("tp_empty_act")
        tp_empty_dve = sem("tp_empty_dve")
        tp_empty = {"act": tp_empty_act, "dve": tp_empty_dve}
        st_high = sem("st_high")
        st_ready = sem("st_ready")
        ada_landed = [sem(f"ada_landed{n}") for n in range(ARING)]
        ada_bias = [sem(f"ada_bias{n}") for n in range(2)]
        ada_used = sem("ada_used")
        acc_zero = sem("acc_zero")
        acc_dve = sem("acc_dve")
        acc_pool = sem("acc_pool")
        ada_red = sem("ada_red")
        ada_out = sem("ada_out")
        consts = sem("consts")
        inv_ready = sem("inv_ready")
        half_done = sem("half_done")
        scales_ready = sem("scales_ready")
        squares = sem("squares")
        xn_ready = sem("xn_ready")
        cond_landed = sem("cond_landed")
        cond_ready = sem("cond_ready")
        q_summed = sem("q_summed")
        q_scaled = sem("q_scaled")
        q_rotated = sem("q_rotated")
        trig_arg = sem("trig_arg")
        trig_done = sem("trig_done")
        resid = sem("resid")
        z_done = sem("z_done")
        a_full = sem("a_full")
        a_high = sem("a_high")
        a_ready = sem("a_ready")
        s_copied = sem("s_copied")
        cmp_out = sem("cmp_out")
        gate_exp = sem("gate_exp")
        scored = sem("scored")
        maxed = sem("maxed")
        cmp_scored = sem("cmp_scored")
        cmp_maxed = sem("cmp_maxed")
        cmp_exped = sem("cmp_exped")
        cmp_pv = sem("cmp_pv")
        cmp_added = sem("cmp_added")
        exped = sem("exped")
        p_copied = sem("p_copied")
        pv_done = sem("pv_done")
        pv_empty = sem("pv_empty")
        o_steps = sem("o_steps")
        silu_ready = sem("silu_ready")
        act_step = sem("act_step")
        dve_step = sem("dve_step")
        pool_step = sem("pool_step")
        stored = sem("stored")

        block = ctx.enter_context(nc.Block())

        def at(i, first, stride):
            return first if i is None else i * stride + first

        def half(buf, s):
            return buf[:, s % RING, :]

        def raw_half(s):
            return raw[:, (s // 2) % RING, (s % 2) * HALF:(s % 2 + 1) * HALF]

        def split_sizes(s):
            if GATE0 <= s < OUT0:
                return 4 * 48
            if INB1 <= s < KVB1:
                return 4 * 160
            if QB1 <= s < OUT1:
                return (2 if (s - QB1) % 2 == 0 else 1) * QU
            return HALF

        def raw_part(s):
            n = split_sizes(s)
            slot = raw[:, (s // 2) % RING, :]
            if KVB1 <= s < QB1:
                v = slot.rearrange("p (k c) -> p k c", k=2)
                return v[:, :, (s % 2) * 512:(s % 2 + 1) * 512]
            first = 0 if s % 2 == 0 else (split_sizes(s - 1))
            return slot[:, first:first + n]

        def part_of(buf, s):
            n = split_sizes(s)
            v = buf[:, s % RING, 0:n]
            if KVB1 <= s < QB1:
                return v.rearrange("p (k c) -> p k c", k=2)
            return v

        q_factors = [cs_q[:, n] for n in range(4)]

        def rotate(engine, link, temp, v, heads, factors):
            hw = ROT // 2
            n = T * heads * hw
            p = [temp[:, j * n:j * n + n].rearrange("p (t h d) -> p t h d", t=T, h=heads) for j in range(4)]
            x1, x2 = v[:, :, :, 0:hw], v[:, :, :, hw:ROT]
            for j, x12 in enumerate((x1, x2, x1, x2)):
                ins = engine.tensor_tensor(
                    p[j], x12, factors[j].unsqueeze(2).broadcast_to([P, T, heads, hw]), ALU.mult)
                if j == 3 or engine is nc.gpsimd:
                    link(ins)
            ins = engine.tensor_tensor(x1, p[0], p[1], ALU.subtract)
            if engine is nc.gpsimd:
                link(ins)
            return engine.tensor_tensor(x2, p[2], p[3], ALU.add)

        up_view = ffn_w_in.rearrange("l (k p) (two c) -> l p k two c", p=P, two=2)

        def weight_slot(b):
            s = 2 * b
            slot = raw[:, b % RING, :]

            def cut(k, c):
                return slot[:, 0:k * c].rearrange("p (k c) -> p k c", k=k)

            def columns(w, k0, k, c0, c):
                return w.rearrange("(k p) n -> p k n", p=P)[:, k0:k0 + k, c0:c0 + c]

            for which, first in ((0, CMPK0), (1, CMPV0)):
                if first <= s < first + 4:
                    return columns(nsa_cmp_w1[0, which], 4 * (s - first), 8, 0, CH), cut(8, CH)
            if s < GATE0:
                return columns(nsa_w_in[0], 2 * (s % 4), 4, NSA_UNITS[s - s % 4], 512), cut(4, 512)
            if s < OUT0:
                return columns(nsa_w_in[0], 0, KD, 2560, 48), cut(KD, 48)
            for first, w in ((OUT0, nsa_w_out), (OUT1, mla_w_out)):
                if first <= s < first + 8:
                    u, h = divmod(s - first, 4)
                    return columns(w[0], 2 * h, 4, 512 * u, 512), cut(4, 512)
            for layer, first in ((0, DOWN0), (1, DOWN1)):
                if first <= s < first + FK:
                    return columns(ffn_w_out[layer], s - first, 2, 0, D), cut(2, D)
            if s < INB1:
                return columns(mla_w_in[0], 2 * (s - IN1), 4, 0, 512), cut(4, 512)
            if s < KVB1:
                return columns(mla_w_in[0], 0, KD, 512, 160), cut(KD, 160)
            if s < QB1:
                return columns(mla_w_kv_b[0], 0, 2, 512 * (s - KVB1), D), cut(2, D)
            return columns(mla_w_q_b[0], 0, 3, QU * ((s - QB1) // 2), QU), cut(3, QU)

        LANDED = []
        count = [32] * RING
        for b in range(END // 2):
            is_up = UP0 <= 2 * b < DOWN0 or UP1 <= 2 * b < DOWN1
            count[b % RING] += 32 if is_up else 16
            LANDED.append(count[b % RING])

        smalls = [(gain_cols[:, 2 * layer + j, :], g[layer].rearrange("(k p) -> p k", p=P))
                  for layer in range(2) for j, g in enumerate((norm_mix, norm_ffn))]
        smalls += [(pe_cols[:, b, :], nsa_cmp_pe[0, b].rearrange("(m u) d -> (u d) m", u=2))
                   for b in range(2)]
        smalls += [
            (nsa_gains[0:64, 0:1], nsa_q_norm.rearrange("l p -> p l")),
            (nsa_gains[64:128, 0:1], nsa_q_norm.rearrange("l p -> p l")),
            (nsa_gains[0:64, 1:4], nsa_k_norm[0].rearrange("b p -> p b")),
            (nsa_gains[64:128, 1:4], nsa_k_norm[0].rearrange("b p -> p b")),
            (lat_gains[:, 0:3], mla_q_a_norm[0].rearrange("(k p) -> p k", p=P)),
            (lat_gains[:, 3:5], mla_kv_a_norm[0].rearrange("(k p) -> p k", p=P)),
            (qk_gain_cols[0:NOPE, 0:1], mla_q_norm[0:1, 0:NOPE].rearrange("l p -> p l")),
            (qk_gain_cols[0:NOPE, 1:2], mla_k_norm[0:1, 0:NOPE].rearrange("l p -> p l")),
            (q_gain_row[:], mla_q_norm[0, NOPE:DQ].partition_broadcast(P)),
            (k_gain_row[:], mla_k_norm[0, NOPE:DQ].partition_broadcast(P)),
        ]
        smalls += [(w2[:, b], nsa_cmp_w2[0, b].rearrange("(k p) d -> p k d", p=P)) for b in range(2)]
        N_SMALL = 16 * len(smalls)

        @block.sync
        def _(sp):
            for a in range(KD):
                if a >= RING:
                    sp.wait_ge(ada_used, 2 * (a - RING) + 2)
                seg, q = divmod(a, KD // 2)
                src = ada_w[0].rearrange("(k p) n -> p k n", p=P)[:, 2 * q:2 * q + 2, seg * D:(seg + 1) * D]
                sp.dma_start(raw[:, a % RING, :].rearrange("p (k n) -> p k n", k=2),
                             src).then_inc(landed[a % RING], 16)
                if a == 1:
                    sp.dma_start(x[:], x_in[0].rearrange("(t p) n -> p t n", p=P)).then_inc(x_in_done, 16)

            def load(b, i=None):
                if b >= RING or i is not None:
                    sp.wait_ge(lo_ready, at(i, 2 * (b - RING) + 2, 8))
                else:
                    sp.wait_ge(ada_used, 2 * (b + RING) + 2)

            def load_up(layer, first, b, i):
                load(b, i)
                j = b - first
                k0 = 4 * (j % 2)
                slot = raw[:, b % RING, :].rearrange("p (k two c) -> p k two c", k=4, two=2)
                for side in range(2):
                    c0 = at(i, HU * (j // 2), 2 * HU)
                    src = up_view[layer][:, k0:k0 + 4, side, bass.ds(c0, HU)]
                    sp.dma_start(slot[:, :, side, :], src).then_inc(landed[b % RING], 16)

            b = 0
            while b < END // 2:
                layer = 0 if b < UP1 // 2 else 1
                first = (UP0, UP1)[layer] // 2
                if b == first:
                    for q in range(2):
                        load_up(layer, first, first + q, None)
                    with sp.Fori(0, (FU - 1) // 2) as i:
                        for q in range(4):
                            load_up(layer, first, first + 2 + q, i)
                    b = first + 2 * FU
                    continue
                src, dst = weight_slot(b)
                load(b)
                sp.dma_start(dst, src).then_inc(landed[b % RING], 16)
                b += 1
            y = out[0].rearrange("(t p) n -> p t n", p=P)
            for n in range(2):
                sp.wait_ge(resid, 12 + 2 * n + 2)
                sp.dma_start(y[:, :, 512 * n:512 * n + 512], x[:, :, 512 * n:512 * n + 512]).then_inc(stored, 16)
            sp.wait_ge(stored, 32)

        def ada_source(a):
            seg, kt = divmod(a, KD)
            layer, s6 = divmod(seg, 6)
            return ada_w[layer, kt * P:(kt + 1) * P, s6 * D:(s6 + 1) * D]

        @block.gpsimd
        def _(pool):
            steps = [0]

            def link(ins):
                steps[0] += 1
                ins.then_inc(pool_step, 1)
                pool.wait_ge(pool_step, steps[0])

            def issue(a):
                n = a - 2 * KD
                pool.dma_start(ada_ring[:, n % ARING, :], ada_source(a)).then_inc(ada_landed[n % ARING], 16)

            def issue_bias(seg):
                layer, s6 = divmod(seg, 6)
                pool.dma_start(ada_acc[0:1, seg % 2, :],
                               ada_b[layer:layer + 1, s6 * D:(s6 + 1) * D]).then_inc(ada_bias[seg % 2], 16)

            link(nc.gpsimd.memset(ada_acc[:], 0.0))
            issue_bias(0)
            issue_bias(1)
            for n in range(ROT // 2):
                f = float(np.float32(np.float64(10000.0) ** (-2.0 * n / ROT)))
                ins = nc.gpsimd.memset(inv[:, n:n + 1], f)
            ins.then_inc(inv_ready, 1)
            nc.gpsimd.memset(ones[:], 1.0)
            nc.gpsimd.memset(ident[:], 0.0)
            nc.gpsimd.memset(ident_b[:], 0.0)
            nc.gpsimd.memset(tri[:], 0.0)
            nc.gpsimd.memset(v_cmp[:], 0.0)
            link(nc.gpsimd.memset(cmp_mask[:], 0.0))
            for t in (ident, ident_b):
                nc.gpsimd.affine_select(out=t[:], in_=t[:], compare_op=ALU.not_equal, fill=1.0, base=0,
                                        pattern=[[-1, P]], channel_multiplier=1)
            nc.gpsimd.affine_select(out=tri[:], in_=tri[:], compare_op=ALU.is_ge, fill=MASKED,
                                    base=0, pattern=[[-1, P]], channel_multiplier=1)
            for t in range(T):
                last = nc.gpsimd.affine_select(
                    out=cmp_mask[:, t, :], in_=cmp_mask[:, t, :], compare_op=ALU.is_ge, fill=MASKED,
                    base=t * P - CLEN + 1, pattern=[[0, H // 2], [-STRIDE, CP]], channel_multiplier=1)
            last.then_inc(consts, 1)
            pool.wait_ge(ada_used, 2 * KD - 4)
            for a in range(2 * KD, 2 * KD + ARING):
                issue(a)
            for seg in range(2, NSEG):
                acc = ada_acc[:, seg % 2, :]
                pool.wait_ge(ada_red, seg - 1)
                link(nc.gpsimd.memset(acc, 0.0))
                issue_bias(seg)
                pool.wait_ge(ada_bias[seg % 2], 16 * (seg // 2 + 1))
                for kt in range(KD):
                    a = seg * KD + kt
                    n = a - 2 * KD
                    chunk = ada_ring[:, n % ARING, :]
                    pool.wait_ge(ada_landed[n % ARING], 16 * (n // ARING + 1))
                    link(nc.gpsimd.tensor_scalar(chunk, chunk, cond[:, kt:kt + 1], 0.0, ALU.mult, ALU.add))
                    add = nc.gpsimd.tensor_tensor(acc, acc, chunk, ALU.add)
                    link(add)
                    if a + ARING < NSEG * KD:
                        issue(a + ARING)
                pool.sem_inc(acc_pool, 1)
            for u in (0, 2):
                pool.wait_ge(q_scaled, u + 1)
                v = q_tok[:, :, QU * u:QU * u + QU].rearrange("p t (h d) -> p t h d", h=R)
                link(rotate(nc.gpsimd, link, scratch[:, 512:1024], v[:, :, :, NOPE:DQ], R, q_factors))
                pool.sem_inc(q_rotated, 1)

        @block.scalar
        def _(act):
            steps = [0]
            made = [0]
            scaled_count = [0]

            def link(ins):
                steps[0] += 1
                ins.then_inc(act_step, 1)
                act.wait_ge(act_step, steps[0])

            def high(s, i=None, landed_at=None):
                if s % 2 == 0:
                    b = s // 2
                    act.wait_ge(landed[b % RING], LANDED[b] if landed_at is None else landed_at)
                if s >= RING or i is not None:
                    act.wait_ge(slot_used, at(i, s - RING + 1, 8))
                nc.scalar.activation(part_of(w_hi, s), raw_part(s), ACT.Copy).then_inc(hi_ready, 1)

            def high_to(n):
                while made[0] < n:
                    high(made[0])
                    made[0] += 1

            def unit_done(s_end):
                act.wait_ge(slot_used, s_end)

            def squares_of_x(k, n):
                for t in range(T):
                    if k == 0:
                        act.wait_ge(x_in_done, 16)
                    else:
                        act.wait_ge(resid, 4 * (k - 1) + 2 * n + t + 1)
                    nc.scalar.activation(scratch[:, (2 * n + t) * 512:(2 * n + t + 1) * 512],
                                         x[:, t, 512 * n:512 * n + 512], ACT.Square,
                                         accum_out=stat[:, 0, 2 * n + t:2 * n + t + 1]).then_inc(squares, 1)

            def scaled_high(batch, k0, nk, scale, shift=None):
                m = stationary_number(batch)
                parity = scaled_count[0] % 2
                scaled_count[0] += 1
                act.wait_ge(tp_filled, batch + 1)
                if m >= 2:
                    act.wait_ge(st_ready, m - 1)
                for k in range(nk):
                    src = tp[batch % 2][:, k * S:(k + 1) * S]
                    dst = tfull[:, parity, k * S:(k + 1) * S]
                    if shift is None:
                        ins = nc.scalar.activation(dst, src, ACT.Copy, scale=scale[:, k:k + 1])
                    else:
                        ins = nc.scalar.activation(dst, src, ACT.Identity, scale=scale[:, k:k + 1],
                                                   bias=shift[:, k:k + 1])
                link(ins)
                nc.scalar.activation(st_hi[:, k0:k0 + nk, :], tfull[:, parity, 0:nk * S].rearrange(
                    "p (k s) -> p k s", k=nk), ACT.Copy).then_inc(st_high, 1)

            def modulated(norm, batch0, shift_seg):
                act.wait_ge(scales_ready, norm + 1)
                for m in range(4):
                    scaled_high(batch0 + m, 2 * m, 2, scale_cols[:, norm, 2 * m:2 * m + 2],
                                ada_cols[:, shift_seg, 2 * m:2 * m + 2])

            def high_from_tp(batch, dst):
                act.wait_ge(tp_filled, batch + 1)
                nc.scalar.activation(dst, tp[batch % 2][:], ACT.Copy).then_inc(st_high, 1)

            def attention(n_items, item0, tp0, prob_b, prob_tb):
                for n in range(n_items + 2):
                    if n < n_items:
                        m = item0 + n
                        step, r = divmod(n, R)
                        act.wait_ge(maxed, m + 1)
                        if n >= 3:
                            act.wait_ge(tp_filled, tp0 + n - 2)
                        for t in range(T):
                            w = (t + 1) * P
                            c0 = t * P
                            e = nc.scalar.activation(
                                prob_b[:, n % 3, c0:c0 + w], score[n % 4][:, c0:c0 + w], ACT.Exp,
                                bias=nmax[:, n % 4, t:t + 1],
                                accum_out=sums[:, step % 4, t * R + r:t * R + r + 1])
                        e.then_inc(exped, 1)
                    if n >= 2 and TP_EMPTIED[tp0 + n - 2] == "act":
                        b = tp0 + n - 2
                        act.wait_ge(tp_filled, b + 1)
                        nc.scalar.activation(prob_tb[:, (n - 2) % 2, 0:3 * P], tp[b % 2][:, 0:3 * P],
                                             ACT.Copy).then_inc(tp_empty_act, 1)

            def feed_forward(up, down, unit0, tp0):
                def unit(u, i=None):
                    for q in range(4):
                        s = up + 4 * u + 4 + q
                        b = s // 2
                        if q == 2 and (u > 0 or i is not None):
                            batch = tp0 + u - 1
                            act.wait_ge(tp_filled, at(i, batch + 1, 2))
                            nc.scalar.activation(hid_hi[:, bass.ds(at(i, (u - 1) * 512, 1024), 512)],
                                                 tp[batch % 2][:], ACT.Copy).then_inc(st_high, 1)
                        stride = 32
                        if i is not None or s < down:
                            lv = at(i, LANDED[b], stride)
                        else:
                            lv = LANDED[b]
                        high(s, i, lv)
                    act.wait_ge(slot_used, at(i, up + 4 * u + 4, 8))
                    for t in range(T):
                        nc.scalar.activation(silu_a[:, u % 2, t, :], lin[2 * ((unit0 + u) % 2) + t][:, 0:HU],
                                             ACT.Silu).then_inc(silu_ready, 1)

                unit(0)
                with act.Fori(0, (FU - 3) // 2) as i:
                    unit(1, i)
                    unit(2, i)
                unit(FU - 2)
                unit(FU - 1)
                made[0] = down + 4
                high_to(down + 5)
                high_from_tp(tp0 + FU - 1, hid_hi[:, (FU - 1) * 512:FU * 512])
                high_to(down + FK)

            with nc.allow_non_contiguous_dma(reason="vectors laid out over partitions"):
                act.dma_start(cond[:], c_in[0].rearrange("(k p) -> p k", p=P)).then_inc(cond_landed, 16)
                act.dma_start(pos_i[:], positions[0].rearrange("(t p) -> p t", p=P)).then_inc(cond_landed, 16)
            act.wait_ge(cond_landed, 32)
            nc.scalar.activation(cond[:], cond[:], ACT.Silu).then_inc(cond_ready, 1)
            with nc.allow_non_contiguous_dma(reason="vectors laid out over partitions"):
                for dst, src in smalls:
                    act.dma_start(dst, src).then_inc(small_in, 16)
            squares_of_x(0, 0)
            squares_of_x(0, 1)
            act.wait_ge(trig_arg, 2)
            nc.scalar.activation(cs[:].rearrange("p a t n -> p (a t n)"),
                                 trig[:, 0:2, :].rearrange("p a n -> p (a n)"), ACT.Sin).then_inc(trig_done, 1)
            high_to(4)
            modulated(0, T_H0, 0)

            def empty_unit(unit, s_end, dst, c0, n):
                high_to(s_end + 4)
                unit_done(s_end)
                for t in range(T):
                    ev = nc.scalar.activation(dst[:, t, c0:c0 + n], lin[2 * (unit % 2) + t][:, 0:n], ACT.Copy)
                ev.then_inc(unit_empty_act, 1)

            def blocks_high(b):
                act.wait_ge(a_full, b + 1)
                nc.scalar.activation(a_hi[:].rearrange("p m c -> p (m c)"), scratch[:], ACT.Copy).then_inc(a_high, 1)

            def compressed_hidden(b, unit, s_end):
                high_to(s_end + 4)
                unit_done(s_end)
                nc.scalar.activation(tfull[:, 0, b * CH:(b + 1) * CH], lin[2 * (unit % 2)][:, 0:CH],
                                     ACT.Silu).then_inc(unit_empty_act, 1)

            def before_norm(s, k):
                high_to(s + 2)
                squares_of_x(k, 0)
                high_to(s + 4)
                squares_of_x(k, 1)

            empty_unit(U_KVC, KVC0 + 4, proj, 1024, 512)
            empty_unit(U_KVS, KVS0 + 4, proj, 1536, 512)
            for b in range(2):
                act.wait_ge(tp_filled, T_KVC + b + 1)
                nc.scalar.activation(kv_t[:, b, :], tp[(T_KVC + b) % 2][:], ACT.Copy).then_inc(tp_empty_act, 1)
                act.wait_ge(tp_empty_act, b + 1)
                for odd in range(2):
                    src = kv_t[64 * odd:64 * odd + 64, b, :].rearrange("p (j s) -> p j s", j=2)
                    act.dma_start(z[0:64, b, odd::2, :], src).then_inc(z_done, 16)
                    act.dma_start(z[64:128, b, odd::2, 0:S - 1], src[:, :, 1:S]).then_inc(z_done, 16)
            high_to(CMPK0)
            blocks_high(0)
            empty_unit(U_KVW, KVW0 + 4, proj, 2048, 512)
            compressed_hidden(0, U_CMPK, CMPK0 + 4)
            blocks_high(1)
            empty_unit(U_QA, QA0 + 4, proj, 0, 512)
            compressed_hidden(1, U_CMPV, CMPV0 + 4)
            empty_unit(U_QB, QB0 + 4, proj, 512, 512)
            act.wait_ge(tp_filled, T_SC + 1)
            nc.scalar.activation(sc_t, tp[T_SC % 2][:], ACT.Copy).then_inc(tp_empty_act, 1)
            empty_unit(U_GATE, GATE0 + 2, proj, 2560, 48)
            act.wait_ge(unit_empty_act, 8)
            nc.scalar.activation(gates[:], proj[:, :, 2560:2608], ACT.Exp, scale=-1.0).then_inc(gate_exp, 1)
            for b in range(2):
                for m in range(2):
                    batch = T_K + 2 * b + m
                    act.wait_ge(tp_filled, batch + 1)
                    for u in range(2):
                        half_p = slice(64 * u, 64 * u + 64)
                        ev = nc.scalar.activation(
                            k_t[u][half_p, b, 2 * m:2 * m + 2, :].rearrange("p g s -> p (g s)"),
                            tp[batch % 2][half_p, :], ACT.Copy, scale=nsa_gains[half_p, 2 + b:3 + b])
                    ev.then_inc(tp_empty_act, 1)
            for t in range(T):
                act.wait_ge(cmp_maxed, t + 1)
                nc.scalar.activation(tfull[:, t, :], tfull[:, t, :], ACT.Exp).then_inc(cmp_exped, 1)
            for t in range(T):
                act.wait_ge(tp_filled, T_PC + t + 1)
                nc.scalar.activation(probc_t[:, t, :], tp[(T_PC + t) % 2][:], ACT.Copy).then_inc(tp_empty_act, 1)
            attention(2 * H, 0, T_P0, prob, prob_t)
            for m in range(4):
                high_from_tp(T_O0 + m, st_hi[:, 2 * m:2 * m + 2, :].rearrange("p k s -> p (k s)"))
            before_norm(OUT0 + 8, 1)
            modulated(1, T_HF0, 3)
            feed_forward(UP0, DOWN0, U_UP0, T_HID0)

            before_norm(DOWN0 + FK, 2)
            modulated(2, T_H1, 6)
            for u in range(2):
                s_end = (INB1, KVB1)[u]
                high_to(s_end + 4)
                unit_done(s_end)
                n = (512, 160)[u]
                for t in range(T):
                    ev = nc.scalar.activation(proj1[:, t, 512 * u:512 * u + n],
                                              lin[2 * ((U_IN1 + u) % 2) + t][:, 0:n], ACT.Copy)
                ev.then_inc(unit_empty_act, 1)
            act.wait_ge(unit_empty_act, count_before(UNIT_EMPTIED, U_IN1 + 2, "act"))
            for n, (c0, w) in enumerate(((0, QL), (QL, KVL), (QL + KVL, ROT))):
                for t in range(T):
                    at0 = (2 * n + t) * QL if n < 2 else 4 * QL + t * ROT
                    nc.scalar.activation(scratch[:, at0:at0 + w],
                                         proj1[:, t, c0:c0 + w], ACT.Square,
                                         accum_out=stat[:, 0, 2 * n + t:2 * n + t + 1]).then_inc(squares, 1)
            for m, (k0, nk) in enumerate(((3, 2), (0, 2), (2, 1))):
                scaled_high(T_CQ + m, k0, nk, lat_gains[:, k0:k0 + nk])
            sq_view = scratch[:].rearrange("p (t h d) -> p t h d", t=T, h=H)
            for u in range(4):
                high_to(KVB1 + u + 1 + 4)
                unit_done(KVB1 + u + 1)
                for t in range(T):
                    kv = lin[2 * ((U_KVB1 + u) % 2) + t][:].rearrange("p (h d) -> p h d", d=2 * DH)
                    heads = slice(R * u, R * u + R)
                    nc.scalar.activation(k_tok[:, t, heads, 0:NOPE], kv[:, :, 0:NOPE], ACT.Copy)
                    nc.scalar.activation(sq_view[:, t, heads, :], kv[:, :, 0:NOPE], ACT.Square)
                    ev = nc.scalar.activation(v_tok[:, t, heads, :], kv[:, :, NOPE:], ACT.Copy)
                ev.then_inc(unit_empty_act, 1)

            def heads_copied(batch, j, dst, which):
                act.wait_ge(tp_filled, batch + 1)
                nc.scalar.activation(dst[0:DQ, 2 * j:2 * j + 2, :].rearrange("p h s -> p (h s)"),
                                     tp[batch % 2][0:DQ, :], ACT.Copy,
                                     scale=qk_gain_cols[0:DQ, which:which + 1]).then_inc(tp_empty_act, 1)

            for u in range(4):
                high_to(QB1 + 2 * u + 2 + 4)
                unit_done(QB1 + 2 * u + 2)
                for t in range(T):
                    bank = lin[2 * ((U_QB1 + u) % 2) + t][:, 0:QU]
                    if u >= 2 and t == 0:
                        act.wait_ge(q_summed, u - 1)
                    nc.scalar.activation(q_squares[u % 2][:, t, :], bank, ACT.Square)
                    ev = nc.scalar.activation(q_tok[:, t, QU * u:QU * u + QU], bank, ACT.Copy)
                ev.then_inc(unit_empty_act, 1)
                if u == 3:
                    for j in range(8):
                        heads_copied(T_K1 + j, j, k1_t, 1)
            for j in range(0, 8, 2):
                heads_copied(T_Q1 + j, j, q1_t, 0)
            nc.scalar.activation(table_exp[:], ones[:, 0:1], ACT.Exp)
            act.wait_ge(tp_filled, T_P1)
            attention(H, 2 * H, T_P1, prob1, prob1_t)
            for m in range(4):
                high_from_tp(T_O1 + m, st_hi[:, 2 * m:2 * m + 2, :].rearrange("p k s -> p (k s)"))
            before_norm(OUT1 + 8, 3)
            modulated(3, T_HF1, 9)
            feed_forward(UP1, DOWN1, U_UP1, T_HID1)

        @block.vector
        def _(dve):
            steps = [0]
            made = [0]
            counts = {"scaled": 0, "st": 0, "root": 0, "squares": 0, "resid": 0, "red": 0, "item": 0,
                      "step": 0}

            def link(ins):
                steps[0] += 1
                ins.then_inc(dve_step, 1)
                dve.wait_ge(dve_step, steps[0])

            def low(s, i=None):
                dve.wait_ge(hi_ready, at(i, s + 1, 8))
                nc.vector.tensor_tensor(part_of(w_lo, s), raw_part(s), part_of(w_hi, s).bitcast(F32),
                                        ALU.subtract).then_inc(lo_ready, 1)

            def low_to(n):
                while made[0] < n:
                    low(made[0])
                    made[0] += 1

            def reciprocal_roots(n, widths):
                c0 = 0
                for cnt, width in widths:
                    ins = nc.vector.tensor_scalar(stat[:, 1, c0:c0 + cnt], stat[:, 0, c0:c0 + cnt],
                                                  1.0 / width, EPS, ALU.mult, ALU.add)
                    c0 += cnt
                link(ins)
                v, y, a = stat[:, 1, 0:n], stat[:, 3, 0:n], stat[:, 4, 0:n]
                link(nc.vector.tensor_scalar(y.bitcast(I32), v.bitcast(I32), 1, None,
                                             ALU.logical_shift_right))
                link(nc.vector.tensor_scalar(y.bitcast(I32), y.bitcast(I32), -1.0, float(0x5F3759DF),
                                             ALU.mult, ALU.add))
                for _ in range(3):
                    link(nc.vector.scalar_tensor_tensor(a, y, -0.5, y, ALU.mult, ALU.mult))
                    link(nc.vector.tensor_tensor(a, a, v, ALU.mult))
                    link(nc.vector.scalar_tensor_tensor(y, a, 1.5, y, ALU.add, ALU.mult))

            def normalise_x():
                counts["squares"] += 2 * T
                dve.wait_ge(squares, counts["squares"])
                link(nc.vector.tensor_tensor(stat[:, 0, 0:T], stat[:, 0, 0:T], stat[:, 0, T:2 * T], ALU.add))
                reciprocal_roots(T, [(T, D)])
                for t in range(T):
                    nc.vector.tensor_scalar(scratch[:, t * D:(t + 1) * D], x[:, t, :], stat[:, 3, t:t + 1],
                                            None, ALU.mult).then_inc(xn_ready, 1)

            def scaled_low(k0, nk):
                m = counts["scaled"]
                counts["scaled"] += 1
                counts["st"] += 1
                dve.wait_ge(st_high, counts["st"])
                nc.vector.tensor_tensor(
                    st_lo[:, k0:k0 + nk, :], tfull[:, m % 2, 0:nk * S].rearrange("p (k s) -> p k s", k=nk),
                    st_hi[:, k0:k0 + nk, :].bitcast(F32), ALU.subtract).then_inc(st_ready, 1)

            def modulated(s):
                low_to(s + 2)
                for m in range(4):
                    scaled_low(2 * m, 2)
                    if m < 2:
                        low_to(s + 3 + m)

            def low_from_tp(batch, hi, lo, i=None):
                counts["st"] += 1
                dve.wait_ge(st_high, at(i, counts["st"], 2))
                nc.vector.tensor_tensor(lo, tp[batch % 2][:], hi.bitcast(F32), ALU.subtract).then_inc(st_ready, 1)

            def ada_columns(seg):
                counts["red"] += 1
                dve.wait_ge(ada_red, seg + 1)
                nc.vector.tensor_copy(ada_cols[:, seg, :], sc[seg % 2][:, 0:KD]).then_inc(ada_out, 1)

            def ada_row(seg, row):
                dve.wait_ge(ada_red, seg + 1)
                nc.vector.tensor_copy(gate_rows[:, row, 0:512], sc[0][:])
                nc.vector.tensor_copy(gate_rows[:, row, 512:D], sc[1][:]).then_inc(ada_out, 1)

            def modulation(norm, scale_seg):
                dve.wait_ge(ada_out, scale_seg + 1)
                link(nc.vector.tensor_scalar(scale_cols[:, norm, :], ada_cols[:, scale_seg, :], 1.0, None,
                                             ALU.add))
                nc.vector.tensor_tensor(scale_cols[:, norm, :], scale_cols[:, norm, :],
                                        gain_cols[:, norm, :], ALU.mult).then_inc(scales_ready, 1)

            def update_x(unit, row, n):
                for t in range(T):
                    tmp = scratch[:, (2 * n + t) * 512:(2 * n + t + 1) * 512]
                    ins = nc.vector.tensor_tensor(tmp, lin[2 * (unit % 2) + t][:],
                                                  gate_rows[:, row, 512 * n:512 * n + 512], ALU.mult)
                    if t == T - 1:
                        ins.then_inc(unit_empty_dve, 1)
                        dve.wait_ge(unit_empty_dve, count_before(UNIT_EMPTIED, unit + 1, "dve"))
                    else:
                        link(ins)
                    xs = x[:, t, 512 * n:512 * n + 512]
                    nc.vector.tensor_tensor(xs, xs, tmp, ALU.add).then_inc(resid, 1)

            def group_norm(src, n_cols, groups, width, squares_buf):
                link(nc.vector.tensor_tensor(squares_buf, src, src, ALU.mult))
                return nc.vector.tensor_reduce(stat[:, 0, n_cols:n_cols + groups], squares_buf, X, ALU.add)

            def attention(n_items, tp0, prob_tb, emit_step, finish_step=lambda k: None,
                          before=lambda n: None):
                for n in range(n_items + R + 3):
                    before(n)
                    if n < n_items:
                        m = counts["item"]
                        counts["item"] += 1
                        dve.wait_ge(scored, m + 1)
                        bank = score[n % 4]
                        nc.vector.tensor_reduce(nmax[:, n % 4, 0:1], bank[:, 0:P], X, ALU.max, negate=True)
                        nc.vector.tensor_reduce(nmax[:, n % 4, 1:2], bank[:, P:3 * P], X, ALU.max,
                                                negate=True).then_inc(maxed, 1)
                    if 2 <= n < n_items + 2 and TP_EMPTIED[tp0 + n - 2] == "dve":
                        b = tp0 + n - 2
                        dve.wait_ge(tp_filled, b + 1)
                        nc.vector.tensor_copy(prob_tb[:, (n - 2) % 2, 0:3 * P],
                                              tp[b % 2][:, 0:3 * P]).then_inc(tp_empty_dve, 1)
                    if n >= 2 * R and n % R == 0:
                        emit_step(n // R - 2)
                    if n >= 2 * R + 2 and n % R == 2:
                        finish_step(n // R - 2)

            def feed_forward(up, down, unit0, tp0, at_end=lambda: None):
                st0 = counts["st"]

                def unit(u, i=None):
                    for q in range(4):
                        s = up + 4 * u + 4 + q
                        if q == 2 and (u > 0 or i is not None):
                            batch = tp0 + u - 1
                            dve.wait_ge(st_high, at(i, st0 + u, 2))
                            cols = bass.ds(at(i, (u - 1) * 512, 1024), 512)
                            nc.vector.tensor_tensor(hid_lo[:, cols], tp[batch % 2][:],
                                                    hid_hi[:, cols].bitcast(F32),
                                                    ALU.subtract).then_inc(st_ready, 1)
                        low(s, i)
                    for t in range(T):
                        dve.wait_ge(silu_ready, at(i, silu0 + T * u + t + 1, 2 * T))
                        ins = nc.vector.tensor_tensor(hid[:, u % 2, t, :], silu_a[:, u % 2, t, :],
                                                      lin[2 * ((unit0 + u) % 2) + t][:, HU:2 * HU], ALU.mult)
                    ins.then_inc(unit_empty_dve, 1)

                silu0 = counts["silu"] if "silu" in counts else 0
                unit(0)
                with dve.Fori(0, (FU - 3) // 2) as i:
                    unit(1, i)
                    unit(2, i)
                at_end()
                unit(FU - 2)
                unit(FU - 1)
                counts["silu"] = silu0 + T * FU
                made[0] = down + 4
                low_to(down + 5)
                counts["st"] = st0 + FU - 1
                low_from_tp(tp0 + FU - 1, hid_hi[:, (FU - 1) * 512:FU * 512], hid_lo[:, (FU - 1) * 512:FU * 512])

            nc.vector.memset(qk_gain_cols[NOPE:P], 1.0)
            nc.vector.memset(k_even[64:128], 0.0)
            nc.vector.memset(kc_t[64:128, 0], 0.0)
            nc.vector.memset(kc_t[0:64, 1], 0.0)
            dve.wait_ge(cond_landed, 32)
            dve.wait_ge(inv_ready, 1)
            two_pi = 2 * np.pi
            pieces, left = [], two_pi
            for bits in (7, 8, 8):
                scale = 2.0 ** (bits - 1 - np.floor(np.log2(left)))
                piece = float(np.floor(left * scale) / scale)
                pieces.append(piece)
                left -= piece
            pieces.append(float(np.float32(left)))
            ang = trig[:, 2, :]
            pos_f = stat[:, 5, 0:T]
            link(nc.vector.tensor_copy(pos_f, pos_i[:]))
            half_w = ROT // 2
            for t in range(T):
                ins = nc.vector.tensor_scalar(ang[:, t * half_w:(t + 1) * half_w], inv[:], pos_f[:, t:t + 1],
                                              None, ALU.mult)
            link(ins)
            magic = float(1.5 * 2 ** 23)
            for j in range(2):
                turns = stat[:, 6, :]
                arg = trig[:, j, :]
                link(nc.vector.tensor_scalar(turns, ang, 1.0 / two_pi, 0.25 * j, ALU.mult, ALU.add))
                link(nc.vector.tensor_scalar(turns, turns, magic, None, ALU.add))
                link(nc.vector.tensor_scalar(turns, turns, -magic, None, ALU.add))
                src = ang
                for piece in pieces:
                    link(nc.vector.scalar_tensor_tensor(arg, turns, -piece, src, ALU.mult, ALU.add))
                    src = arg
                link(nc.vector.tensor_scalar(arg, arg, float(j * np.pi / 2), None, ALU.add))
                nc.vector.tensor_scalar(arg, arg, -3.1415925, 3.1415925, ALU.max, ALU.min).then_inc(trig_arg, 1)
            dve.wait_ge(cond_ready, 1)
            for a in range(2 * KD):
                seg, kt = divmod(a, KD)
                if kt == 0:
                    dve.wait_ge(ada_bias[seg], 16)
                b = a // 2
                dve.wait_ge(landed[b % RING], 16 * (b // RING + 1))
                if a > 0:
                    dve.wait_ge(ada_used, a)
                nc.vector.scalar_tensor_tensor(ada_acc[:, seg, :], raw_half(a), cond[:, kt:kt + 1],
                                               ada_acc[:, seg, :], ALU.mult, ALU.add).then_inc(ada_used, 1)
            dve.wait_ge(small_in, N_SMALL)
            link(nc.vector.tensor_scalar(nsa_gains[:, 0:1], nsa_gains[:, 0:1], float(DH ** -0.5), None, ALU.mult))
            normalise_x()
            ada_columns(0)
            ada_columns(1)
            modulation(0, 1)
            modulated(0)

            def normed_keys(b, c0):
                for t in range(T):
                    src = proj[:, t, c0:c0 + G * DH].rearrange("p (g d) -> p g d", g=G)
                    sq = qsq[:, t * 256:(t + 1) * 256].rearrange("p (g d) -> p g d", g=G)
                    link(group_norm(src, t * G, G, DH, sq))
                reciprocal_roots(T * G, [(T * G, DH)])
                for t in range(T):
                    for u in range(2):
                        src = proj[:, t, c0:c0 + G * DH].rearrange("p (g d) -> p g d", g=G)
                        dst = kdup_o[:, b, t * 512:(t + 1) * 512].rearrange("p (g u d) -> p g u d", g=G, u=2)
                        ins = nc.vector.tensor_tensor(
                            dst[:, :, u, :], src,
                            stat[:, 3, t * G:(t + 1) * G].unsqueeze(2).broadcast_to([P, G, DH]), ALU.mult)
                ins.then_inc(xn_ready, 1)

            def blocks(b):
                a_view = scratch[:].rearrange("p (m g c) -> p m g c", m=CM, g=G)
                dve.wait_ge(z_done, 16 * 4 * 2)
                if b == 1:
                    dve.wait_ge(a_ready, 1)
                for g in range(G):
                    zg = z[:, b, g, :].rearrange("p (c m u) -> p u m c", u=2, m=CM // 2)
                    for hm in range(2):
                        src = zg[:, 0, :, hm:hm + NCMP]
                        pe = pe_cols[:, b, hm * 8:hm * 8 + 8].unsqueeze(2).broadcast_to([P, 8, NCMP])
                        ins = nc.vector.tensor_tensor(a_view[:, hm * 8:hm * 8 + 8, g, 0:NCMP], src, pe, ALU.add)
                ins.then_inc(a_full, 1)

            def blocks_low():
                b = counts.setdefault("blocks", 0)
                counts["blocks"] = b + 1
                dve.wait_ge(a_high, b + 1)
                nc.vector.tensor_tensor(a_lo[:].rearrange("p m c -> p (m c)"), scratch[:],
                                        a_hi[:].rearrange("p m c -> p (m c)").bitcast(F32),
                                        ALU.subtract).then_inc(a_ready, 1)

            def scaled_copy(batch, dst, gain):
                dve.wait_ge(tp_filled, batch + 1)
                nc.vector.tensor_scalar(dst, tp[batch % 2][:], gain, None, ALU.mult).then_inc(tp_empty_dve, 1)

            def normed_queries(half_of):
                c0 = half_of * D // 2
                for t in range(T):
                    src = proj[:, t, c0:c0 + D // 2].rearrange("p (h d) -> p h d", d=DH)
                    link(group_norm(src, t * 8, 8, DH, qsq[:, t * 512:(t + 1) * 512].rearrange(
                        "p (h d) -> p h d", d=DH)))
                reciprocal_roots(T * 8, [(T * 8, DH)])
                for t in range(T):
                    src = proj[:, t, c0:c0 + D // 2].rearrange("p (h d) -> p h d", d=DH)
                    ins = nc.vector.tensor_tensor(
                        src, src, stat[:, 3, t * 8:(t + 1) * 8].unsqueeze(2).broadcast_to([P, 8, DH]), ALU.mult)
                ins.then_inc(xn_ready, 1)

            low_to(8)
            link(nc.vector.memset(scratch[:], 0.0))
            low_to(12)
            dve.wait_ge(unit_empty_act, 2)
            normed_keys(0, 1536)
            blocks(0)
            blocks_low()
            low_to(16)
            dve.wait_ge(unit_empty_act, 3)
            ada_row(2, 0)
            normed_keys(1, 2048)
            low_to(18)
            blocks(1)
            low_to(20)
            blocks_low()
            low_to(24)
            dve.wait_ge(unit_empty_act, 5)
            normed_queries(0)
            low_to(28)
            ada_columns(3)
            low_to(30)
            dve.wait_ge(unit_empty_act, 7)
            normed_queries(1)
            nc.vector.memset(k_odd[0:64], 0.0)
            dve.wait_ge(cmp_out, 1)
            kc = scratch[:, 0:DH]
            link(nc.vector.tensor_copy(kc, sc[0][:, 0:DH]))
            link(group_norm(kc.unsqueeze(1), 0, 1, DH, scratch[:, DH:2 * DH].unsqueeze(1)))
            reciprocal_roots(1, [(1, DH)])
            for u in range(2):
                ins = nc.vector.tensor_scalar(scratch[:, (2 + u) * DH:(3 + u) * DH], kc, stat[:, 3, 0:1], None,
                                              ALU.mult)
            for g in range(G):
                ins = nc.vector.tensor_copy(v_cmp[CP * g:CP * g + CP, g, :],
                                            sc[0][CP * g:CP * g + CP, DH:2 * DH])
            ins.then_inc(xn_ready, 1)
            for u in range(4):
                scaled_copy(T_Q + u, q_t[:, 2 * u:2 * u + 2, :].rearrange("p k s -> p (k s)"),
                            nsa_gains[:, 0:1])
            dve.wait_ge(tp_filled, T_KC + 1)
            for u in range(2):
                half_p = slice(64 * u, 64 * u + 64)
                ins = nc.vector.tensor_scalar(kc_t[half_p, u].rearrange("p g c -> p (g c)"),
                                              tp[T_KC % 2][half_p, 0:P], nsa_gains[half_p, 1:2], None, ALU.mult)
            ins.then_inc(tp_empty_dve, 1)
            for t in range(T):
                dve.wait_ge(cmp_scored, t + 1)
                s4 = lin[t][:].rearrange("p (h c) -> p h c", c=CP)
                mx = cstat[:, t, :]
                link(nc.vector.tensor_reduce(mx, s4, X, ALU.max))
                link(nc.vector.tensor_scalar(mx, mx, FLOOR, None, ALU.max))
                nc.vector.tensor_tensor(tfull[:, t, :].rearrange("p (h c) -> p h c", c=CP), s4,
                                        mx.unsqueeze(2).broadcast_to([P, H, CP]),
                                        ALU.subtract).then_inc(cmp_maxed, 1)
            dve.wait_ge(gate_exp, 1)
            link(nc.vector.tensor_scalar(gates[:], gates[:], 1.0, None, ALU.add))
            link(nc.vector.reciprocal(gates[:], gates[:]))
            gate_view = gates[:].rearrange("p t (g r u b) -> p t r u g b", g=G, u=2, b=3)

            def compressed_weights():
                for t in range(T):
                    dve.wait_ge(cmp_exped, t + 1)
                    cf = cstat[:, t, :]
                    link(nc.vector.tensor_reduce(cf, tfull[:, t, :].rearrange("p (h c) -> p h c", c=CP), X,
                                                 ALU.add))
                    link(nc.vector.tensor_scalar(cf, cf, TINY, None, ALU.max))
                    link(nc.vector.reciprocal(cf, cf))
                    cf4 = cf.rearrange("p (r u g) -> p r u g", r=2, u=2)
                    link(nc.vector.tensor_tensor(cf4, cf4, gate_view[:, t, :, :, :, 0], ALU.mult))

            def compressed_output(n):
                if n != 2:
                    return
                compressed_weights()
                for t in range(T):
                    o_view = o0[:, t, :].rearrange("p (g r u d) -> p r u g d", g=G, u=2, d=DH)
                    for pair in range(2):
                        bank = CMP_BANKS[2 * t + pair]
                        dve.wait_ge(cmp_pv, 2 * t + pair + 1)
                        for u in range(2):
                            j = 2 * pair + u
                            cf = cstat[:, t, j * G:(j + 1) * G]
                            ins = nc.vector.tensor_tensor(
                                o_view[:, pair, u], bank[:, u * 256:(u + 1) * 256].rearrange(
                                    "p (g d) -> p g d", g=G),
                                cf.unsqueeze(2).broadcast_to([P, G, DH]), ALU.mult)
                        ins.then_inc(cmp_added, 1)
                dve.wait_ge(cmp_added, 4)

            def nsa_step(k):
                g, b = divmod(k, 2)
                cf = coef[:, 0, :]
                dve.wait_ge(pv_done, k + 1)
                link(nc.vector.tensor_scalar(cf, sums[:, k % 4, :], TINY, None, ALU.max))
                link(nc.vector.reciprocal(cf, cf))
                gv = gates[:].rearrange("p t (h b) -> p t h b", b=3)[:, :, R * g:R * g + R, 1 + b]
                cf3 = cf.rearrange("p (t r) -> p t r", t=T)
                link(nc.vector.tensor_tensor(cf3, cf3, gv, ALU.mult))
                tmp = scratch[:, 512 * (k % 4):512 * (k % 4) + 512]
                nc.vector.tensor_tensor(tmp.rearrange("p (h d) -> p h d", d=DH),
                                        lin[k % 2][:].rearrange("p (h d) -> p h d", d=DH),
                                        cf.unsqueeze(2).broadcast_to([P, T * R, DH]),
                                        ALU.mult).then_inc(pv_empty, 1)

            def nsa_add(k):
                g = k // 2
                og = o0[:, :, 256 * g:256 * g + 256]
                tmp = scratch[:, 512 * (k % 4):512 * (k % 4) + 512]
                dve.wait_ge(pv_empty, k + 1)
                nc.vector.tensor_tensor(og, og, tmp.rearrange("p (t n) -> p t n", t=T),
                                        ALU.add).then_inc(o_steps, 1)
                dve.wait_ge(o_steps, k + 1)

            attention(2 * H, T_P0, prob_t, nsa_step, nsa_add, compressed_output)

            def odd_heads(u):
                batch = T_Q1 + 2 * u + 1
                dve.wait_ge(tp_filled, batch + 1)
                nc.vector.tensor_scalar(q1_t[0:DQ, R * u + 2:R * u + 4, :].rearrange("p h s -> p (h s)"),
                                        tp[batch % 2][0:DQ, :], qk_gain_cols[0:DQ, 0:1], None,
                                        ALU.mult).then_inc(tp_empty_dve, 1)

            def output_low(batch0):
                for m in range(4):
                    low_from_tp(batch0 + m, st_hi[:, 2 * m:2 * m + 2, :].rearrange("p k s -> p (k s)"),
                                st_lo[:, 2 * m:2 * m + 2, :].rearrange("p k s -> p (k s)"))

            output_low(T_O0)
            ada_columns(4)
            low_to(OUT0 + 8)
            modulation(1, 4)
            dve.wait_ge(slot_used, OUT0 + 4)
            update_x(U_OUT0, 0, 0)
            ada_row(5, 1)
            low_to(OUT0 + 11)
            dve.wait_ge(slot_used, OUT0 + 8)
            update_x(U_OUT0 + 1, 0, 1)
            normalise_x()
            modulated(UP0)

            def shift_and_scale():
                ada_columns(6)
                ada_columns(7)

            feed_forward(UP0, DOWN0, U_UP0, T_HID0, shift_and_scale)
            low_to(DOWN0 + 19)
            ada_row(8, 0)
            low_to(DOWN0 + FK)
            modulation(2, 7)
            dve.wait_ge(half_done, 1)
            update_x(U_DOWN0, 1, 0)
            low_to(DOWN0 + FK + 2)
            dve.wait_ge(slot_used, DOWN0 + FK)
            update_x(U_DOWN0 + 1, 1, 1)

            normalise_x()
            modulated(IN1)
            nc.vector.memset(q1_t[DQ:P], 0.0)
            low_to(KVB1)
            ada_columns(9)
            ada_columns(10)
            nc.vector.memset(k1_t[DQ:P], 0.0)
            low_to(KVB1 + 4)
            counts["squares"] += 6
            dve.wait_ge(squares, counts["squares"])
            reciprocal_roots(6, [(2, QL), (2, KVL), (2, ROT)])
            for n, (c0, w) in enumerate(((0, QL), (QL, KVL), (QL + KVL, ROT))):
                for t in range(T):
                    src = proj1[:, t, c0:c0 + w]
                    ins = nc.vector.tensor_scalar(src, src, stat[:, 3, 2 * n + t:2 * n + t + 1], None, ALU.mult)
            ins.then_inc(xn_ready, 1)
            scaled_low(3, 2)
            scaled_low(0, 2)
            scaled_low(2, 1)
            sin, cos = cs[:, 0], cs[:, 1]
            hw = ROT // 2
            dve.wait_ge(trig_done, 1)
            link(nc.vector.tensor_scalar(qk_gain_cols[:, 0:1], qk_gain_cols[:, 0:1], float(DQ ** -0.5), None,
                                         ALU.mult))
            for n, (factor, first) in enumerate(((cos, 0), (sin, hw), (sin, 0), (cos, hw))):
                ins = nc.vector.tensor_tensor(
                    cs_q[:, n], factor, q_gain_row[:, first:first + hw].unsqueeze(1).broadcast_to([P, T, hw]),
                    ALU.mult)
            link(ins)

            kr = proj1[:, :, QL + KVL:MLA_IN]
            link(nc.vector.tensor_tensor(kr, kr, k_gain_row[:].unsqueeze(1).broadcast_to([P, T, ROT]), ALU.mult))
            link(rotate(nc.vector, link, q_sq[:].rearrange("p t n -> p (t n)"), kr.unsqueeze(2), 1,
                        (cos, sin, sin, cos)))
            nc.vector.tensor_copy(k_tok[:, :, :, NOPE:DQ], kr.unsqueeze(2).broadcast_to([P, T, H, ROT]))
            sq_view = scratch[:].rearrange("p (t h d) -> p t h d", t=T, h=H)
            k_sums = stat[:, 0, :].rearrange("p (t h) -> p t h", t=T)
            k_roots = stat[:, 3, :].rearrange("p (t h) -> p t h", t=T)
            for u in range(4):
                dve.wait_ge(unit_empty_act, count_before(UNIT_EMPTIED, U_KVB1 + u + 1, "act"))
                ins = nc.vector.tensor_reduce(k_sums[:, :, R * u:R * u + R],
                                              sq_view[:, :, R * u:R * u + R, :], X, ALU.add)
                if u < 3:
                    low_to(QB1 + u + 1)
            link(ins)
            reciprocal_roots(T * H, [(T * H, NOPE)])
            low_to(QB1 + 6)
            k_nope = k_tok[:, :, :, 0:NOPE]
            nc.vector.tensor_tensor(k_nope, k_nope, k_roots.unsqueeze(3).broadcast_to([P, T, H, NOPE]),
                                    ALU.mult).then_inc(xn_ready, 1)
            for pair in range(2):
                q_sums = stat[:, 0, 0:2 * T * R].rearrange("p (u n) -> p u n", u=2)
                q_roots = stat[:, 3, 0:2 * T * R].rearrange("p (u t h) -> p u t h", u=2, t=T)
                for j in range(2):
                    u = 2 * pair + j
                    dve.wait_ge(unit_empty_act, count_before(UNIT_EMPTIED, U_QB1 + u + 1, "act"))
                    nc.vector.tensor_reduce(q_sums[:, j], q_squares[j].rearrange(
                        "p t (h d) -> p (t h) d", h=R), X, ALU.add).then_inc(q_summed, 1)
                if pair == 0:
                    low_to(QB1 + 8)
                dve.wait_ge(q_summed, 2 * pair + 2)
                reciprocal_roots(2 * T * R, [(2 * T * R, DQ)])
                for j in range(2):
                    u = 2 * pair + j
                    src = q_tok[:, :, QU * u:QU * u + QU].rearrange("p t (h d) -> p t h d", h=R)
                    nc.vector.tensor_tensor(src, src, q_roots[:, j].unsqueeze(3).broadcast_to([P, T, R, DQ]),
                                            ALU.mult).then_inc(q_scaled, 1)
                dve.wait_ge(q_scaled, 2 * pair + 2)
                rotate(nc.vector, link, scratch[:, 0:512], src[:, :, :, NOPE:DQ], R,
                       q_factors).then_inc(xn_ready, 1)
            for u in range(4):
                odd_heads(u)

            def mla_step(k):
                cf = coef[:, 0, :]
                dve.wait_ge(pv_done, 8 + k + 1)
                link(nc.vector.tensor_scalar(cf, sums[:, k % 4, :], TINY, None, ALU.max))
                link(nc.vector.reciprocal(cf, cf))
                og = o1[:, :, 256 * k:256 * k + 256].rearrange("p t (r d) -> p t r d", d=DH)
                ps = lin[k % 2][:].rearrange("p (t r d) -> p t r d", t=T, d=DH)
                for t in range(T):
                    ins = nc.vector.tensor_tensor(og[:, t], ps[:, t], cf[:, t * R:(t + 1) * R].unsqueeze(
                        2).broadcast_to([P, R, DH]), ALU.mult)
                ins.then_inc(pv_empty, 1)

            def output_weights(n):
                if n % R == 1 and n < H:
                    low_to(OUT1 + n // R + 1)

            attention(H, T_P1, prob1_t, mla_step, before=output_weights)
            output_low(T_O1)
            low_to(OUT1 + 8)
            modulation(3, 10)
            dve.wait_ge(slot_used, OUT1 + 4)
            update_x(U_OUT1, 0, 0)
            ada_row(11, 1)
            low_to(OUT1 + 11)
            dve.wait_ge(slot_used, OUT1 + 8)
            update_x(U_OUT1 + 1, 0, 1)
            normalise_x()
            modulated(UP1)
            feed_forward(UP1, DOWN1, U_UP1, T_HID1)
            low_to(END)
            dve.wait_ge(half_done, 2)
            update_x(U_DOWN1, 1, 0)
            dve.wait_ge(slot_used, END)
            update_x(U_DOWN1 + 1, 1, 1)

        @block.tensor
        def _(pe):
            xn = [0]

            def three(bank, a_h, a_l, w_h, w_l, first, last):
                nc.tensor.matmul(bank, a_h, w_h, start=first, stop=False)
                nc.tensor.matmul(bank, a_h, w_l, start=False, stop=False)
                return nc.tensor.matmul(bank, a_l, w_h, start=False, stop=last)

            def wait_unit(unit, i=None):
                if unit < 2 and i is None:
                    return
                who = UNIT_EMPTIED[unit - 2]
                pe.wait_ge(unit_empty[who], at(i, count_before(UNIT_EMPTIED, unit - 1, who), 2))

            def emptied(batch):
                who = TP_EMPTIED[batch]
                empty = {"act": tp_empty_act, "dve": tp_empty_dve, "st": st_ready}[who]
                return empty, count_before(TP_EMPTIED, batch + 1, who)

            def wait_tp(batch):
                if batch >= 2:
                    pe.wait_ge(*emptied(batch - 2))

            def transposes(batch, pieces, rows=P):
                wait_tp(batch)
                for n, src in enumerate(pieces):
                    ins = nc.tensor.transpose(tp[batch % 2][0:rows, n * P:(n + 1) * P], src, ident[:])
                ins.then_inc(tp_filled, 1)

            def unit(unit, s0, slots, n, lhs, wait_st=None):
                wait_unit(unit)
                total = sum(len(k) for k in slots)
                done = 0
                for q, kts in enumerate(slots):
                    s = s0 + q
                    pe.wait_ge(lo_ready, s + 1)
                    wh = w_hi[:, s % RING, 0:len(kts) * n].rearrange("p (k c) -> p k c", c=n)
                    wl = w_lo[:, s % RING, 0:len(kts) * n].rearrange("p (k c) -> p k c", c=n)
                    for j, k in enumerate(kts):
                        if wait_st is not None:
                            wait_st(k)
                        for t, (ah, al) in enumerate(lhs(k)):
                            ins = three(lin[2 * (unit % 2) + t][:, 0:n], ah, al, wh[:, j], wl[:, j],
                                        done == 0, done == total - 1)
                        done += 1
                    ins.then_inc(slot_used, 1)

            def stationary(k):
                return [(st_hi[:, k, t * P:(t + 1) * P], st_lo[:, k, t * P:(t + 1) * P]) for t in range(T)]

            def st_wait(first):
                def wait(k):
                    if k % 2 == 0:
                        pe.wait_ge(st_ready, first + k // 2 + 1)
                return wait

            FOUR = [[0, 1], [2, 3], [4, 5], [6, 7]]

            def transposed_x(batch0):
                xn[0] += T
                pe.wait_ge(xn_ready, xn[0])
                for m in range(4):
                    transposes(batch0 + m, [scratch[:, t * D + k * P:t * D + (k + 1) * P]
                                            for k in (2 * m, 2 * m + 1) for t in range(T)])

            def transposed_o(batch0, o):
                for m in range(4):
                    transposes(batch0 + m, [o[:, t, k * P:(k + 1) * P] for k in (2 * m, 2 * m + 1)
                                            for t in range(T)])

            def wait_acc(seg):
                if seg < 2:
                    pe.wait_ge(ada_used, KD * (seg + 1))
                else:
                    pe.wait_ge(acc_pool, seg - 1)
                if seg > 0:
                    pe.wait_ge(ada_out, seg)

            def reduce_columns(seg):
                wait_acc(seg)
                for k in range(KD):
                    ins = nc.tensor.matmul(sc[seg % 2][:, k:k + 1], ada_acc[:, seg % 2, k * P:(k + 1) * P],
                                           ones[:, 0:1], start=True, stop=True)
                ins.then_inc(ada_red, 1)

            def reduce_row(seg):
                wait_acc(seg)
                for n in range(2):
                    ins = nc.tensor.matmul(sc[n][:], ones[:], ada_acc[:, seg % 2, 512 * n:512 * n + 512],
                                           start=True, stop=True)
                ins.then_inc(ada_red, 1)

            def attention(n_items, item0, tp0, step0, q_of, k_of, v_of, prob_b, prob_tb,
                          before=lambda n: None):
                for n in range(n_items + 3):
                    before(n)
                    if n < n_items:
                        if n >= 4:
                            pe.wait_ge(exped, item0 + n - 3)
                        bank = score[n % 4]
                        for t in range(T):
                            w = (t + 1) * P
                            nc.tensor.matmul(bank[:, t * P:t * P + w], q_of(n, t), k_of(n, t + 1),
                                             start=True, stop=False)
                            ins = nc.tensor.matmul(bank[:, 2 * t * P:(2 * t + 1) * P], ident_b[:], tri[:],
                                                   start=False, stop=True)
                        ins.then_inc(scored, 1)
                    if 2 <= n < n_items + 2:
                        i = n - 2
                        pe.wait_ge(exped, item0 + i + 1)
                        transposes(tp0 + i, [prob_b[:, i % 3, j * P:(j + 1) * P] for j in range(3)])
                    if n >= 3:
                        i = n - 3
                        step, r = divmod(i, R)
                        pe.wait_ge(*emptied(tp0 + i))
                        if r == 0 and step >= 2:
                            pe.wait_ge(pv_empty, step0 + step - 1)
                        bank = lin[step % 2]
                        pt = prob_tb[:, i % 2, :]
                        nc.tensor.matmul(bank[:, r * DH:(r + 1) * DH], pt[:, 0:P], v_of(i, 0),
                                         start=True, stop=True)
                        lo = (R + r) * DH
                        nc.tensor.matmul(bank[:, lo:lo + DH], pt[:, P:2 * P], v_of(i, 0), start=True, stop=False)
                        ins = nc.tensor.matmul(bank[:, lo:lo + DH], pt[:, 2 * P:3 * P], v_of(i, 1),
                                               start=False, stop=True)
                        if r == R - 1:
                            ins.then_inc(pv_done, 1)

            def feed_forward(up, down, unit0, tp0, tp_h, up_reduce=lambda: None, down_reduce=lambda: None):
                st_h, hid0 = stationary_number(tp_h), stationary_number(tp0)

                def one(u, i=None):
                    wait_unit(unit0 + u, i)
                    for q in range(4):
                        s = up + 4 * u + q
                        pe.wait_ge(lo_ready, at(i, s + 1, 8))
                        for j in range(2):
                            k = 2 * q + j
                            if j == 0 and u == 0 and i is None:
                                pe.wait_ge(st_ready, st_h + q + 1)
                            for t, (ah, al) in enumerate(stationary(k)):
                                ins = three(lin[2 * ((unit0 + u) % 2) + t][:], ah, al,
                                            w_hi[:, s % RING, 512 * j:512 * j + 512],
                                            w_lo[:, s % RING, 512 * j:512 * j + 512], k == 0, k == KD - 1)
                        ins.then_inc(slot_used, 1)
                        if q == 1 and (u > 0 or i is not None):
                            hidden(u - 1, i)

                def hidden(u, i=None):
                    batch = tp0 + u
                    pe.wait_ge(unit_empty_dve, at(i, count_before(UNIT_EMPTIED, unit0 + u + 1, "dve"), 2))
                    empty, value = emptied(batch - 2)
                    pe.wait_ge(empty, at(i, value, 2))
                    for n in range(4):
                        k, t = divmod(n, 2)
                        ins = nc.tensor.transpose(tp[batch % 2][:, n * P:(n + 1) * P],
                                                  hid[:, u % 2, t, k * P:(k + 1) * P], ident[:])
                    ins.then_inc(tp_filled, 1)

                one(0)
                with pe.Fori(0, (FU - 3) // 2) as i:
                    one(1, i)
                    one(2, i)
                up_reduce()
                one(FU - 2)
                one(FU - 1)
                for n in range(2):
                    wait_unit(unit0 + FU + n)
                def down_product(k, ns):
                    for t in range(T):
                        c0 = k * S + t * P
                        for n in ns:
                            s = down + k
                            ins = three(lin[2 * ((unit0 + FU + n) % 2) + t][:], hid_hi[:, c0:c0 + P],
                                        hid_lo[:, c0:c0 + P], w_hi[:, s % RING, 512 * n:512 * n + 512],
                                        w_lo[:, s % RING, 512 * n:512 * n + 512], k == 0, k == FK - 1)
                    return ins

                for k in range(FK - RING):
                    pe.wait_ge(lo_ready, down + k + 1)
                    pe.wait_ge(st_ready, hid0 + k // 2 + 1)
                    down_product(k, range(2)).then_inc(slot_used, 1)
                    if k == 1:
                        hidden(FU - 1)
                    if k == 15:
                        down_reduce()
                for k in range(FK - RING, FK):
                    pe.wait_ge(lo_ready, down + k + 1)
                    pe.wait_ge(st_ready, hid0 + k // 2 + 1)
                    ins = down_product(k, [0])
                ins.then_inc(half_done, 1)
                for k in range(FK - RING, FK):
                    down_product(k, [1]).then_inc(slot_used, 1)

            pe.wait_ge(consts, 1)
            reduce_columns(0)
            reduce_columns(1)
            transposed_x(T_H0)
            KT16 = [[0, 1, 2, 3], [4, 5, 6, 7], [8, 9, 10, 11], [12, 13, 14, 15]]

            def next_tokens():
                xn[0] += 1
                pe.wait_ge(xn_ready, xn[0])

            def compress(b, u, s0):
                pe.wait_ge(a_ready, b + 1)
                unit(u, s0, KT16, CH, lambda k: [(a_hi[:, k, :], a_lo[:, k, :])])

            unit(U_KVC, KVC0, FOUR, 512, stationary, st_wait(0))
            unit(U_KVS, KVS0, FOUR, 512, stationary)
            pe.wait_ge(unit_empty_act, 1)
            for b in range(2):
                c0 = 1024 + 256 * b
                transposes(T_KVC + b, [proj[:, t, c0 + P * j:c0 + P * (j + 1)] for j in range(2) for t in range(T)])
            unit(U_KVW, KVW0, FOUR, 512, stationary)
            reduce_row(2)
            compress(0, U_CMPK, CMPK0)
            unit(U_QA, QA0, FOUR, 512, stationary)
            compress(1, U_CMPV, CMPV0)
            reduce_columns(3)
            unit(U_QB, QB0, FOUR, 512, stationary)
            pe.wait_ge(unit_empty_act, 6)
            transposes(T_SC, [tfull[:, 0, j * P:(j + 1) * P] for j in range(4)])
            unit(U_GATE, GATE0, [[0, 1, 2, 3], [4, 5, 6, 7]], 48, stationary)
            pe.wait_ge(*emptied(T_SC))
            pe.wait_ge(ada_out, 4)
            for b in range(2):
                for k in range(2):
                    ins = nc.tensor.matmul(sc[0][:, b * DH:(b + 1) * DH],
                                           sc_t[:, (2 * b + k) * P:(2 * b + k + 1) * P], w2[:, b, k, :],
                                           start=(k == 0), stop=(k == 1))
            ins.then_inc(cmp_out, 1)
            for b in range(2):
                next_tokens()
                for m in range(2):
                    transposes(T_K + 2 * b + m, [kdup_o[:, b, t * 512 + g * P:t * 512 + (g + 1) * P]
                                                 for g in (2 * m, 2 * m + 1) for t in range(T)])
            for part in range(2):
                next_tokens()
                for m in range(2 * part, 2 * part + 2):
                    transposes(T_Q + m, [proj[:, t, k * P:(k + 1) * P] for k in (2 * m, 2 * m + 1)
                                         for t in range(T)])
            next_tokens()
            transposes(T_KC, [scratch[:, 2 * DH:4 * DH]])
            pe.wait_ge(*emptied(T_KC))
            for t in range(T):
                nc.tensor.matmul(lin[t][:].rearrange("p (u c) -> p u c", u=2), ident_b[:],
                                 cmp_mask[:, t, :].unsqueeze(1).broadcast_to([P, 2, H // 2 * CP]),
                                 start=True, stop=False)
                out_view = lin[t][:].rearrange("p (r u g c) -> p r u g c", r=2, u=2, g=G)
                for pair in range(R // 2):
                    for g in range(G):
                        ins = nc.tensor.matmul(out_view[:, pair, :, g, :],
                                               q_t[:, 2 * g + pair, t * P:(t + 1) * P], kc_t[:, :, g, :],
                                               start=False, stop=(pair == 1 and g == G - 1))
                ins.then_inc(cmp_scored, 1)
            pe.wait_ge(ada_out, 4)

            def compressed_values(n):
                if n == 2:
                    for t in range(T):
                        pe.wait_ge(cmp_exped, t + 1)
                        transposes(T_PC + t, [tfull[:, t, j * P:(j + 1) * P] for j in range(4)])
                    for j in range(8):
                        t, pair, u = j // 4, j // 2 % 2, j % 2
                        if j % 4 == 0:
                            pe.wait_ge(*emptied(T_PC + t))
                        ins = nc.tensor.matmul(CMP_BANKS[j // 2][:, u * 256:(u + 1) * 256],
                                               probc_t[:, t, (j % 4) * P:(j % 4 + 1) * P],
                                               v_cmp[:].rearrange("p g d -> p (g d)"), start=True, stop=True)
                        if u == 1:
                            ins.then_inc(cmp_pv, 1)
                if n in (2, 3):
                    pe.wait_ge(cmp_added, n - 1 if n == 2 else 4)

            def item_head(n):
                step, r = divmod(n, R)
                g, b = divmod(step, 2)
                return g, b, R * g + r

            def nsa_q(n, t):
                g, b, h = item_head(n)
                return q_t[:, h // 2, t * P:(t + 1) * P]

            def nsa_k(n, tiles):
                g, b, h = item_head(n)
                return k_t[h % 2][:, b, g, 0:tiles * P]

            def nsa_v(n, t):
                g, b, h = item_head(n)
                c0 = 1792 + 512 * b + g * DH
                return proj[:, t, c0:c0 + DH]

            attention(2 * H, 0, T_P0, 0, nsa_q, nsa_k, nsa_v, prob, prob_t, compressed_values)
            pe.wait_ge(o_steps, 8)
            transposed_o(T_O0, o0)
            reduce_columns(4)
            unit(U_OUT0, OUT0, FOUR, 512, stationary, st_wait(stationary_number(T_O0)))
            reduce_row(5)
            unit(U_OUT0 + 1, OUT0 + 4, FOUR, 512, stationary)
            transposed_x(T_HF0)

            def shift_and_scale():
                reduce_columns(6)
                reduce_columns(7)

            feed_forward(UP0, DOWN0, U_UP0, T_HID0, T_HF0, shift_and_scale, lambda: reduce_row(8))

            transposed_x(T_H1)
            unit(U_IN1, IN1, FOUR, 512, stationary, st_wait(stationary_number(T_H1)))
            unit(U_IN1 + 1, INB1, [[0, 1, 2, 3], [4, 5, 6, 7]], 160, stationary)
            reduce_columns(9)
            reduce_columns(10)
            xn[0] += 1
            pe.wait_ge(xn_ready, xn[0])
            transposes(T_CQ, [proj1[:, t, k * P:(k + 1) * P] for k in (3, 4) for t in range(T)])
            transposes(T_CQ + 1, [proj1[:, t, k * P:(k + 1) * P] for k in (0, 1) for t in range(T)])
            transposes(T_CQ + 2, [proj1[:, t, 2 * P:3 * P] for t in range(T)])
            pe.wait_ge(*emptied(T_CQ))
            for u in range(4):
                unit(U_KVB1 + u, KVB1 + u, [[3, 4]], 512, stationary)
            pe.wait_ge(*emptied(T_CQ + 2))
            for u in range(4):
                unit(U_QB1 + u, QB1 + 2 * u, [[0, 1], [2]], QU, stationary)
                if u == 3:
                    next_tokens()
                    for j in range(8):
                        transposes(T_K1 + j, [k_tok[:, t, h, :] for h in (2 * j, 2 * j + 1)
                                              for t in range(T)], DQ)
            for u in range(4):
                if u % 2 == 0:
                    pe.wait_ge(q_rotated, u // 2 + 1)
                else:
                    next_tokens()
                for j in (2 * u, 2 * u + 1):
                    transposes(T_Q1 + j, [q_tok[:, t, h * DQ:(h + 1) * DQ] for h in (2 * j, 2 * j + 1)
                                          for t in range(T)], DQ)
            pe.wait_ge(*emptied(T_P1 - 2))
            pe.wait_ge(*emptied(T_P1 - 1))
            pe.wait_ge(ada_out, 11)
            attention(H, 2 * H, T_P1, 8,
                      lambda n, t: q1_t[:, n, t * P:(t + 1) * P],
                      lambda n, tiles: k1_t[:, n, 0:tiles * P],
                      lambda n, t: v_tok[:, t, n, :], prob1, prob1_t)
            pe.wait_ge(pv_empty, 8 + 4)
            transposed_o(T_O1, o1)
            unit(U_OUT1, OUT1, FOUR, 512, stationary, st_wait(stationary_number(T_O1)))
            reduce_row(11)
            unit(U_OUT1 + 1, OUT1 + 4, FOUR, 512, stationary)
            transposed_x(T_HF1)
            feed_forward(UP1, DOWN1, U_UP1, T_HID1, T_HF1)


_INS = ['x', 'c', 'positions', 'ada_w', 'ada_b', 'norm_mix', 'norm_ffn', 'ffn_w_in', 'ffn_w_out',
        'nsa_w_in', 'nsa_q_norm', 'nsa_k_norm', 'nsa_cmp_pe', 'nsa_cmp_w1', 'nsa_cmp_w2', 'nsa_w_out',
        'mla_w_in', 'mla_q_a_norm', 'mla_kv_a_norm', 'mla_w_q_b', 'mla_w_kv_b', 'mla_q_norm',
        'mla_k_norm', 'mla_w_out']


def kernel(**inputs):
    import concourse.bacc as bacc
    from concourse.bass_utils import run_bass_kernel_spmd

    nc = bacc.Bacc("TRN2", target_bir_lowering=False, num_devices=1)
    arrays, args = {}, []
    for name in _INS:
        a = np.ascontiguousarray(inputs[name])
        arrays[f"in_{name}_dram"] = a
        args.append(nc.dram_tensor(f"in_{name}_dram", a.shape, mybir.dt.from_np(a.dtype),
                                   kind="ExternalInput").ap())
    args.append(nc.dram_tensor("out_0_dram", (1, S, D), F32, kind="ExternalOutput").ap())
    trunk(nc, *args)
    r = run_bass_kernel_spmd(nc, [arrays], core_ids=[0])
    return r.results[0]["out_0_dram"]
```

```python
from contextlib import ExitStack

import numpy as np

import concourse.bass as bass
from concourse import mybir

F32 = mybir.dt.float32
F32R = mybir.dt.float32r
BF16 = mybir.dt.bfloat16
I32 = mybir.dt.int32
ACT = mybir.ActivationFunctionType
ALU = mybir.AluOpType
X = mybir.AxisListType.X

P = 128
S = 256
T = S // P
D = 1024
KD = D // P
EPS = 1e-6
MASKED = -1e30
FLOOR = -1e29
TINY = 1e-30
H = 16
DH = 64
G = 4
R = H // G
STRIDE = 16
CLEN = 32
NCMP = S // STRIDE - 1
CP = 32
CM = CLEN * DH // P
CH = 256
QKV = H * DH + 6 * G * DH
NG = 3 * H
QL, KVL, ROT, NOPE = 384, 256, 32, 64
DQ = NOPE + ROT
QU = R * DQ
MLA_IN = QL + KVL + ROT
FH = 2816
HU = 256
FU = FH // HU
FK = FH // P
NSEG = 12
RING = 4
DOWN_AHEAD = 3
ARING = 3
HALF = 1024

KVC0 = 0
KVS0 = KVC0 + 4
KVW0 = KVS0 + 4
QA0 = KVW0 + 4
GATE0 = QA0 + 4
CMPK0 = GATE0 + 2
QB0 = CMPK0 + 4
CMPV0 = QB0 + 4
OUT0 = CMPV0 + 4
UP0 = OUT0 + 8
DOWN0 = UP0 + 4 * FU
IN1 = DOWN0 + FK
INB1 = IN1 + 4
KVB1 = INB1 + 4
QB1 = KVB1 + 4
OUT1 = QB1 + 8
UP1 = OUT1 + 8
DOWN1 = UP1 + 4 * FU
END = DOWN1 + FK
NSA_UNITS = {KVC0: 1024, KVS0: 1536, KVW0: 2048, QA0: 0, QB0: 512}

UNIT_EMPTIED = ["act"] * 8 + ["dve"] * (2 + FU + 2) + ["act"] * 10 + ["dve"] * (2 + FU + 2)
U_KVC, U_KVS, U_KVW, U_QA, U_GATE, U_CMPK, U_QB, U_CMPV = range(8)
U_OUT0, U_UP0 = 8, 10
U_DOWN0 = U_UP0 + FU
U_IN1 = U_DOWN0 + 2
U_KVB1 = U_IN1 + 2
U_QB1 = U_KVB1 + 4
U_OUT1 = U_QB1 + 4
U_UP1 = U_OUT1 + 2
U_DOWN1 = U_UP1 + FU

TP_EMPTIED = []
PIECES = ((0, 1), (1, 1), (2, 2), (4, 2), (6, 2))


def _batches(n, *who):
    TP_EMPTIED.extend(who[i % len(who)] for i in range(n))
    return len(TP_EMPTIED) - n


T_H0 = _batches(len(PIECES), "st")
T_KVC = _batches(2, "act")
T_K = _batches(4, "act")
T_G = _batches(1, "act")
T_QA = _batches(2, "dve")
T_SCK = _batches(1, "act")
T_CK = _batches(1, "dve")
T_QB = _batches(2, "act")
T_SCV = _batches(1, "act")
T_KC = _batches(1, "dve")
T_CV = _batches(1, "dve")
T_PC = _batches(2, "act")
T_P0 = _batches(2 * H, "act", "dve")
T_O0 = _batches(len(PIECES), "st")
T_HF0 = _batches(len(PIECES), "st")
T_HID0 = _batches(FU, "st")
T_H1 = _batches(len(PIECES), "st")
LATENTS = ((3, 2), (0, 2), (2, 1))
T_CQ = _batches(len(LATENTS), "st")
T_K1 = _batches(8, "act")
T_Q1 = _batches(4, "act")
T_Q1B = _batches(4, "act", "dve")
T_P1 = _batches(H, "act", "dve")
T_O1 = _batches(len(PIECES), "st")
T_HF1 = _batches(len(PIECES), "st")
T_HID1 = _batches(FU, "st")


def count_before(owners, n, who):
    return sum(o == who for o in owners[:n])


def stationary_number(batch):
    return count_before(TP_EMPTIED, batch, "st")


def trunk(nc, x_in, c_in, positions, ada_w, ada_b, norm_mix, norm_ffn, ffn_w_in, ffn_w_out,
          nsa_w_in, nsa_q_norm, nsa_k_norm, nsa_cmp_pe, nsa_cmp_w1, nsa_cmp_w2, nsa_w_out,
          mla_w_in, mla_q_a_norm, mla_kv_a_norm, mla_w_q_b, mla_w_kv_b, mla_q_norm, mla_k_norm,
          mla_w_out, out):
    ctx = ExitStack()
    with ctx:
        def sb(name, shape, dt, stack=ctx):
            return stack.enter_context(nc.sbuf_tensor(name, shape, dt))

        def sem(name):
            return ctx.enter_context(nc.semaphore(name))

        raw = sb("raw", [P, RING, 2 * HALF], F32)
        w_hi = sb("w_hi", [P, RING, HALF], F32R)
        w_lo = sb("w_lo", [P, RING, HALF], F32R)
        ada_ring = sb("ada_ring", [P, ARING, D], F32)
        ada_acc = sb("ada_acc", [P, 2, D], F32)
        x = sb("x", [P, T, D], F32)
        st_hi = sb("st_hi", [P, KD, S], F32R)
        st_lo = sb("st_lo", [P, KD, S], F32R)
        compression = ExitStack()
        with compression:
            a_hi = sb("a_hi", [P, CM, G * CP], F32R, compression)
        gate_rows = sb("gate_rows", [P, 2, D], F32)
        scratch = sb("scratch", [P, 2 * D], F32)
        tfull = sb("tfull", [P, 2, 512], F32)
        ident = sb("ident", [P, P], F32)
        ident_b = sb("ident_b", [P, P], BF16)
        ones = sb("ones", [P, P], F32)
        tri = sb("tri", [P, P], BF16)
        cmp_mask = sb("cmp_mask", [P, T, H // 2 * CP], BF16)
        cond = sb("cond", [P, KD], F32)
        gain_cols = sb("gain_cols", [P, 4, KD], F32)
        ada_cols = sb("ada_cols", [P, NSEG, KD], F32)
        scale_cols = sb("scale_cols", [P, 4, KD], F32)
        nsa_gains = sb("nsa_gains", [P, 4], F32)
        pe_cols = sb("pe_cols", [P, 2, CM], F32)
        w2 = sb("w2", [P, 2, CH // P, DH], F32)
        lat_gains = sb("lat_gains", [P, 5], F32)
        q_gain_row = sb("q_gain_row", [P, ROT], F32)
        k_gain_row = sb("k_gain_row", [P, ROT], F32)
        qk_gain_cols = sb("qk_gain_cols", [P, 2], F32)
        pos_i = sb("pos_i", [P, T], I32)
        inv = sb("inv", [P, ROT // 2], F32)
        cs = sb("cs", [P, 2, T, ROT // 2], F32)
        trig = sb("trig", [P, 3, T * ROT // 2], F32)
        stat = sb("stat", [P, 8, 32], F32)
        table_exp = sb("table_exp", [P, 1], F32)
        nmax = sb("nmax", [P, 4, 2], F32)
        sums = sb("sums", [P, 4, T * R], F32)
        coef = sb("coef", [P, 3, T * R], F32)

        lin = [ctx.enter_context(nc.psum_tensor(f"lin{n}", [P, 512], F32)) for n in range(4)]
        tp = [ctx.enter_context(nc.psum_tensor(f"tp{n}", [P, 512], F32)) for n in range(2)]
        sc = [ctx.enter_context(nc.psum_tensor(f"sc{n}", [P, 512], F32)) for n in range(2)]
        score = [sc[0], sc[1], lin[2], lin[3]]
        CMP_BANKS = [lin[2], lin[3], lin[0], lin[1]]

        nsa = ExitStack()
        with nsa:
            proj = sb("proj", [P, T, QKV], F32, nsa)
            kdup_o = sb("kdup_o", [P, 2, T * G * 2 * DH], F32, nsa)
            q_t = sb("q_t", [P, H // 2, S], F32, nsa)
            k_even = sb("k_even", [P, 2, G, S], F32, nsa)
            z = sb("z", [P, 2, G, S], F32, nsa)
            a_lo = sb("a_lo", [P, CM, G * CP], F32R, nsa)
            kc_t = sb("kc_t", [P, 2, G, CP], F32, nsa)
            gates = sb("gates", [P, T, NG], F32, nsa)
            gates_t = sb("gates_t", [NG, S], F32, nsa)
            v_cmp = sb("v_cmp", [P, G, DH], F32, nsa)
            cstat = sb("cstat", [P, 3, H], F32, nsa)
            k_odd = sb("k_odd", [P, 2, G, S], F32, nsa)
            k_t = [k_even, k_odd]
        z_flat = z[:].rearrange("p b g s -> p (b g s)")
        prob = z_flat[:, 0:9 * P].rearrange("p (b n) -> p b n", b=3)
        prob_t = z_flat[:, 9 * P:15 * P].rearrange("p (b n) -> p b n", b=2)
        probc_t = scratch[:, 0:2 * 512].rearrange("p (b n) -> p b n", b=2)
        sc_t = z_flat[:, 3 * 512:4 * 512]
        ffn = ExitStack()
        with ffn:
            hid_hi = sb("hid_hi", [P, FK * S], F32R, ffn)
            hid_lo = sb("hid_lo", [P, FK * S], F32R, ffn)
            silu_a = sb("silu_a", [P, 2, T, HU], F32, ffn)
            hid = sb("hid", [P, 2, T, HU], F32, ffn)
        mla = ExitStack()
        with mla:
            proj1 = sb("proj1", [P, T, MLA_IN], F32, mla)
            q_tok = sb("q_tok", [P, T, H * DQ], F32, mla)
            k_tok = sb("k_tok", [P, T, H, DQ], F32, mla)
            v_tok = sb("v_tok", [P, T, H, DH], F32, mla)
            q_sq = sb("q_sq", [P, T, QU], F32, mla)
            cs_q = sb("cs_q", [P, 4, T, ROT // 2], F32, mla)
            q1_t = sb("q1_t", [P, H, S], F32, mla)
            k1_t = sb("k1_t", [P, H, S], F32, mla)
        q_flat = q_t[:].rearrange("p k s -> p (k s)")
        sq_keys = [q_flat[:, 1024:1536], q_flat[:, 1536:2048]]
        sq_queries = [q_flat[:, 0:1024], q_flat[:, 1024:2048]]
        q_squares = [tfull[:].rearrange("p b n -> p (b n)")[:, 0:T * QU].rearrange("p (t n) -> p t n", t=T),
                     q_sq[:]]
        kv_t = q_flat[:, 0:1024].rearrange("p (b n) -> p b n", b=2)
        o0 = kdup_o[:, :, :].rearrange("p t n -> p (t n)").rearrange("p (t n) -> p t n", t=T)
        q_tok_flat = q_tok[:, :, :].rearrange("p t n -> p (t n)")
        k_tok_flat = k_tok[:, :, :, :].rearrange("p t h d -> p (t h d)")
        o1 = q_tok_flat[:, 0:T * D].rearrange("p (t n) -> p t n", t=T)
        prob1 = k_tok_flat[:, 0:9 * P].rearrange("p (b n) -> p b n", b=3)
        prob1_t = k_tok_flat[:, 9 * P:15 * P].rearrange("p (b n) -> p b n", b=2)

        small_in = sem("small_in")
        x_in_done = sem("x_in_done")
        landed = [sem(f"landed{n}") for n in range(RING)]
        hi_ready = sem("hi_ready")
        lo_ready = sem("lo_ready")
        slot_used = sem("slot_used")
        unit_empty_act = sem("unit_empty_act")
        unit_empty_dve = sem("unit_empty_dve")
        unit_empty = {"act": unit_empty_act, "dve": unit_empty_dve}
        tp_filled = sem("tp_filled")
        tp_empty_act = sem("tp_empty_act")
        tp_empty_dve = sem("tp_empty_dve")
        tp_empty = {"act": tp_empty_act, "dve": tp_empty_dve}
        st_high = sem("st_high")
        st_ready = sem("st_ready")
        ada_landed = [sem(f"ada_landed{n}") for n in range(ARING)]
        ada_bias = [sem(f"ada_bias{n}") for n in range(2)]
        ada_used = sem("ada_used")
        acc_pool = sem("acc_pool")
        ada_red = sem("ada_red")
        ada_out = sem("ada_out")
        consts = sem("consts")
        inv_ready = sem("inv_ready")
        part_done = sem("part_done")
        scales_ready = sem("scales_ready")
        squares = sem("squares")
        xn_ready = sem("xn_ready")
        cond_landed = sem("cond_landed")
        first_bias = sem("first_bias")
        first_gain = sem("first_gain")
        cond_ready = sem("cond_ready")
        q_summed = sem("q_summed")
        scale_in_gain = sem("scale_in_gain")
        pads_zero = sem("pads_zero")
        q_scaled = sem("q_scaled")
        q_rotated = sem("q_rotated")
        trig_arg = sem("trig_arg")
        trig_done = sem("trig_done")
        resid = sem("resid")
        z_done = sem("z_done")
        a_full = sem("a_full")
        a_high = sem("a_high")
        a_ready = sem("a_ready")
        gate_exp = sem("gate_exp")
        scored = sem("scored")
        maxed = sem("maxed")
        cmp_scored = sem("cmp_scored")
        cmp_maxed = sem("cmp_maxed")
        cmp_exped = sem("cmp_exped")
        cmp_pv = sem("cmp_pv")
        cmp_added = sem("cmp_added")
        exped = sem("exped")
        pv_done = sem("pv_done")
        pv_empty = sem("pv_empty")
        o_steps = sem("o_steps")
        silu_ready = sem("silu_ready")
        act_step = sem("act_step")
        dve_step = sem("dve_step")
        pool_step = sem("pool_step")
        stored = sem("stored")

        block = ctx.enter_context(nc.Block())

        def at(i, first, stride):
            return first if i is None else i * stride + first

        def split_sizes(s):
            if GATE0 <= s < CMPK0:
                return 4 * NG
            if IN1 <= s < KVB1:
                return 2 * (KVL + ROT if s < INB1 else QL)
            if QB1 <= s < OUT1:
                return (2 if (s - QB1) % 2 == 0 else 1) * QU
            return HALF

        def raw_part(s):
            n = split_sizes(s)
            slot = raw[:, (s // 2) % RING, :]
            if KVB1 <= s < QB1:
                v = slot.rearrange("p (k c) -> p k c", k=2)
                return v[:, :, (s % 2) * 512:(s % 2 + 1) * 512]
            first = 0 if s % 2 == 0 else (split_sizes(s - 1))
            return slot[:, first:first + n]

        def part_of(buf, s):
            n = split_sizes(s)
            v = buf[:, s % RING, 0:n]
            if KVB1 <= s < QB1:
                return v.rearrange("p (k c) -> p k c", k=2)
            return v

        q_factors = [cs_q[:, n] for n in range(4)]

        def rotate(engine, link, temp, v, heads, factors):
            hw = ROT // 2
            n = T * heads * hw
            p = [temp[:, j * n:j * n + n].rearrange("p (t h d) -> p t h d", t=T, h=heads) for j in range(4)]
            x1, x2 = v[:, :, :, 0:hw], v[:, :, :, hw:ROT]
            for j, x12 in enumerate((x1, x2, x1, x2)):
                ins = engine.tensor_tensor(
                    p[j], x12, factors[j].unsqueeze(2).broadcast_to([P, T, heads, hw]), ALU.mult)
                if j == 3 or engine is nc.gpsimd:
                    link(ins)
            ins = engine.tensor_tensor(x1, p[0], p[1], ALU.subtract)
            if engine is nc.gpsimd:
                link(ins)
            return engine.tensor_tensor(x2, p[2], p[3], ALU.add)

        up_view = ffn_w_in.rearrange("l (k p) (two c) -> l p k two c", p=P, two=2)

        def weight_slot(b):
            s = 2 * b
            slot = raw[:, b % RING, :]

            def cut(k, c):
                return slot[:, 0:k * c].rearrange("p (k c) -> p k c", k=k)

            def columns(w, k0, k, c0, c):
                return w.rearrange("(k p) n -> p k n", p=P)[:, k0:k0 + k, c0:c0 + c]

            for which, first in ((0, CMPK0), (1, CMPV0)):
                if first <= s < first + 4:
                    return columns(nsa_cmp_w1[0, which], 4 * (s - first), 8, 0, CH), cut(8, CH)
            for first, c0 in NSA_UNITS.items():
                if first <= s < first + 4:
                    return columns(nsa_w_in[0], 2 * (s - first), 4, c0, 512), cut(4, 512)
            if s < OUT0:
                return columns(nsa_w_in[0], 0, KD, QKV, NG), cut(KD, NG)
            for first, w in ((OUT0, nsa_w_out), (OUT1, mla_w_out)):
                if first <= s < first + 8:
                    u, h = divmod(s - first, 4)
                    return columns(w[0], 2 * h, 4, 512 * u, 512), cut(4, 512)
            for layer, first in ((0, DOWN0), (1, DOWN1)):
                if first <= s < first + FK:
                    return columns(ffn_w_out[layer], s - first, 2, 0, D), cut(2, D)
            if s < INB1:
                return columns(mla_w_in[0], 2 * (s - IN1), 4, QL, KVL + ROT), cut(4, KVL + ROT)
            if s < KVB1:
                return columns(mla_w_in[0], 2 * (s - INB1), 4, 0, QL), cut(4, QL)
            if s < QB1:
                return columns(mla_w_kv_b[0], 0, 2, 512 * (s - KVB1), D), cut(2, D)
            return columns(mla_w_q_b[0], 0, 3, QU * ((s - QB1) // 2), QU), cut(3, QU)

        LANDED = []
        count = [32] * RING
        for b in range(END // 2):
            is_up = UP0 <= 2 * b < DOWN0 or UP1 <= 2 * b < DOWN1
            count[b % RING] += 32 if is_up else 16
            LANDED.append(count[b % RING])

        smalls = [(gain_cols[:, 2 * layer + j, :], g[layer].rearrange("(k p) -> p k", p=P))
                  for layer in range(2) for j, g in enumerate((norm_mix, norm_ffn))]
        smalls += [(pe_cols[:, b, :], nsa_cmp_pe[0, b].rearrange("(m u) d -> (u d) m", u=2))
                   for b in range(2)]
        smalls += [
            (nsa_gains[0:64, 0:1], nsa_q_norm.rearrange("l p -> p l")),
            (nsa_gains[64:128, 0:1], nsa_q_norm.rearrange("l p -> p l")),
            (nsa_gains[0:64, 1:4], nsa_k_norm[0].rearrange("b p -> p b")),
            (nsa_gains[64:128, 1:4], nsa_k_norm[0].rearrange("b p -> p b")),
            (lat_gains[:, 0:3], mla_q_a_norm[0].rearrange("(k p) -> p k", p=P)),
            (lat_gains[:, 3:5], mla_kv_a_norm[0].rearrange("(k p) -> p k", p=P)),
            (qk_gain_cols[0:NOPE, 0:1], mla_q_norm[0:1, 0:NOPE].rearrange("l p -> p l")),
            (qk_gain_cols[0:NOPE, 1:2], mla_k_norm[0:1, 0:NOPE].rearrange("l p -> p l")),
            (q_gain_row[:], mla_q_norm[0, NOPE:DQ].partition_broadcast(P)),
            (k_gain_row[:], mla_k_norm[0, NOPE:DQ].partition_broadcast(P)),
        ]
        smalls += [(w2[:, b], nsa_cmp_w2[0, b].rearrange("(k p) d -> p k d", p=P)) for b in range(2)]
        smalls += [(pos_i[:], positions[0].rearrange("(t p) -> p t", p=P))]
        N_SMALL = 16 * (len(smalls) - 1)

        @block.sync
        def _(sp):
            for a in range(KD):
                pair, seg = divmod(a, 2)
                if a >= RING:
                    sp.wait_ge(ada_used, 4 * (pair - 1))
                src = ada_w[0].rearrange("(k p) n -> p k n", p=P)[:, 2 * pair:2 * pair + 2,
                                                                  seg * D:(seg + 1) * D]
                sp.dma_start(raw[:, a % RING, :].rearrange("p (k n) -> p k n", k=2),
                             src).then_inc(landed[a % RING], 16)
                if a == 4:
                    sp.dma_start(x[:], x_in[0].rearrange("(t p) n -> p t n", p=P)).then_inc(x_in_done, 16)

            def load(b, i=None):
                if b >= RING or i is not None:
                    sp.wait_ge(lo_ready, at(i, 2 * (b - RING) + 2, 8))
                else:
                    sp.wait_ge(ada_used, 4 * ((b + RING) // 2 + 1))

            def load_up(layer, first, b, i):
                load(b, i)
                j = b - first
                k0 = 4 * (j % 2)
                slot = raw[:, b % RING, :].rearrange("p (k two c) -> p k two c", k=4, two=2)
                for side in range(2):
                    c0 = at(i, HU * (j // 2), 2 * HU)
                    src = up_view[layer][:, k0:k0 + 4, side, bass.ds(c0, HU)]
                    sp.dma_start(slot[:, :, side, :], src).then_inc(landed[b % RING], 16)

            b = 0
            while b < END // 2:
                layer = 0 if b < UP1 // 2 else 1
                first = (UP0, UP1)[layer] // 2
                if b == first:
                    for q in range(2):
                        load_up(layer, first, first + q, None)
                    with sp.Fori(0, (FU - 1) // 2) as i:
                        for q in range(4):
                            load_up(layer, first, first + 2 + q, i)
                    b = first + 2 * FU
                    continue
                src, dst = weight_slot(b)
                load(b)
                sp.dma_start(dst, src).then_inc(landed[b % RING], 16)
                b += 1
            y = out[0].rearrange("(t p) n -> p t n", p=P)
            for n in range(2):
                for t in range(T):
                    sp.wait_ge(resid, 12 + 2 * n + t + 1)
                    sp.dma_start(y[:, t, 512 * n:512 * n + 512],
                                 x[:, t, 512 * n:512 * n + 512]).then_inc(stored, 16)
            sp.wait_ge(stored, 16 * 2 * T)

        def ada_source(a):
            seg, kt = divmod(a, KD)
            layer, s6 = divmod(seg, 6)
            return ada_w[layer, kt * P:(kt + 1) * P, s6 * D:(s6 + 1) * D]

        @block.gpsimd
        def _(pool):
            steps = [0]

            def link(ins):
                steps[0] += 1
                ins.then_inc(pool_step, 1)
                pool.wait_ge(pool_step, steps[0])

            def issue(a):
                n = a - 2 * KD
                pool.dma_start(ada_ring[:, n % ARING, :], ada_source(a)).then_inc(ada_landed[n % ARING], 16)

            def issue_bias(seg):
                layer, s6 = divmod(seg, 6)
                pool.dma_start(ada_acc[0:1, seg % 2, :],
                               ada_b[layer:layer + 1, s6 * D:(s6 + 1) * D]).then_inc(ada_bias[seg % 2], 16)

            for n in range(ROT // 2):
                f = float(np.float32(np.float64(10000.0) ** (-2.0 * n / ROT)))
                ins = nc.gpsimd.memset(inv[:, n:n + 1], f)
            ins.then_inc(inv_ready, 1)
            nc.gpsimd.memset(ones[:], 1.0)
            nc.gpsimd.memset(ident[:], 0.0)
            nc.gpsimd.memset(ident_b[:], 0.0)
            nc.gpsimd.memset(tri[:], 0.0)
            nc.gpsimd.memset(v_cmp[:], 0.0)
            link(nc.gpsimd.memset(cmp_mask[:], 0.0))
            for t in (ident, ident_b):
                nc.gpsimd.affine_select(out=t[:], in_=t[:], compare_op=ALU.not_equal, fill=1.0, base=0,
                                        pattern=[[-1, P]], channel_multiplier=1)
            nc.gpsimd.affine_select(out=tri[:], in_=tri[:], compare_op=ALU.is_ge, fill=MASKED,
                                    base=0, pattern=[[-1, P]], channel_multiplier=1)
            for t in range(T):
                last = nc.gpsimd.affine_select(
                    out=cmp_mask[:, t, :], in_=cmp_mask[:, t, :], compare_op=ALU.is_ge, fill=MASKED,
                    base=t * P - CLEN + 1, pattern=[[0, H // 2], [-STRIDE, CP]], channel_multiplier=1)
            last.then_inc(consts, 1)
            pool.wait_ge(ada_used, 2 * KD - 4)
            for a in range(2 * KD, 2 * KD + ARING):
                issue(a)
            for seg in range(2, NSEG):
                if seg == NSEG - 1:
                    pool.wait_ge(slot_used, DOWN0 + FK)
                    link(nc.gpsimd.memset(q1_t[DQ:P], 0.0))
                    nc.gpsimd.memset(k1_t[DQ:P], 0.0).then_inc(pads_zero, 1)
                    pool.wait_ge(pads_zero, 1)
                    for u in (0, 2):
                        pool.wait_ge(q_scaled, u + 1)
                        v = q_tok[:, :, QU * u:QU * u + QU].rearrange("p t (h d) -> p t h d", h=R)
                        link(rotate(nc.gpsimd, link, scratch[:, 512:1024], v[:, :, :, NOPE:DQ], R, q_factors))
                        pool.sem_inc(q_rotated, 1)
                acc = ada_acc[:, seg % 2, :]
                pool.wait_ge(ada_red, seg - 1)
                link(nc.gpsimd.memset(acc, 0.0))
                issue_bias(seg)
                pool.wait_ge(ada_bias[seg % 2], 16 * (seg // 2))
                for kt in range(KD):
                    a = seg * KD + kt
                    n = a - 2 * KD
                    chunk = ada_ring[:, n % ARING, :]
                    pool.wait_ge(ada_landed[n % ARING], 16 * (n // ARING + 1))
                    link(nc.gpsimd.tensor_scalar(chunk, chunk, cond[:, kt:kt + 1], 0.0, ALU.mult, ALU.add))
                    add = nc.gpsimd.tensor_tensor(acc, acc, chunk, ALU.add)
                    link(add)
                    if a + ARING < NSEG * KD:
                        issue(a + ARING)
                pool.sem_inc(acc_pool, 1)

        @block.scalar
        def _(act):
            steps = [0]
            made = [0]
            scaled_count = [0]

            def link(ins):
                steps[0] += 1
                ins.then_inc(act_step, 1)
                act.wait_ge(act_step, steps[0])

            def high(s, i=None, landed_at=None):
                if s % 2 == 0:
                    b = s // 2
                    act.wait_ge(landed[b % RING], LANDED[b] if landed_at is None else landed_at)
                if s >= RING or i is not None:
                    act.wait_ge(slot_used, at(i, s - RING + 1, 8))
                nc.scalar.activation(part_of(w_hi, s), raw_part(s), ACT.Copy).then_inc(hi_ready, 1)

            def high_to(n):
                while made[0] < n:
                    high(made[0])
                    made[0] += 1

            def unit_done(s_end):
                act.wait_ge(slot_used, s_end)

            def squares_of_x(k, n, tiles=range(T)):
                for t in tiles:
                    if k == 0:
                        act.wait_ge(x_in_done, 16)
                    else:
                        act.wait_ge(resid, 4 * (k - 1) + 2 * n + t + 1)
                    nc.scalar.activation(scratch[:, (2 * n + t) * 512:(2 * n + t + 1) * 512],
                                         x[:, t, 512 * n:512 * n + 512], ACT.Square,
                                         accum_out=stat[:, 0, 2 * n + t:2 * n + t + 1]).then_inc(squares, 1)

            def scaled_high(batch, k0, nk, scale, shift=None):
                m = stationary_number(batch)
                parity = scaled_count[0] % 2
                scaled_count[0] += 1
                act.wait_ge(tp_filled, batch + 1)
                if m >= 2:
                    act.wait_ge(st_ready, m - 1)
                for k in range(nk):
                    src = tp[batch % 2][:, k * S:(k + 1) * S]
                    dst = tfull[:, parity, k * S:(k + 1) * S]
                    if shift is None:
                        ins = nc.scalar.activation(dst, src, ACT.Copy, scale=scale[:, k:k + 1])
                    else:
                        ins = nc.scalar.activation(dst, src, ACT.Identity, scale=scale[:, k:k + 1],
                                                   bias=shift[:, k:k + 1])
                link(ins)
                nc.scalar.activation(st_hi[:, k0:k0 + nk, :], tfull[:, parity, 0:nk * S].rearrange(
                    "p (k s) -> p k s", k=nk), ACT.Copy).then_inc(st_high, 1)

            def modulated(norm, batch0, shift_seg):
                act.wait_ge(scales_ready, norm + 1)
                for m, (k0, nk) in enumerate(PIECES):
                    scaled_high(batch0 + m, k0, nk, scale_cols[:, norm, k0:k0 + nk],
                                ada_cols[:, shift_seg, k0:k0 + nk])

            def high_from_tp(batch, dst):
                act.wait_ge(tp_filled, batch + 1)
                nc.scalar.activation(dst, tp[batch % 2][:], ACT.Copy).then_inc(st_high, 1)

            def output_high(batch0):
                for m, (k0, nk) in enumerate(PIECES):
                    act.wait_ge(tp_filled, batch0 + m + 1)
                    nc.scalar.activation(st_hi[:, k0:k0 + nk, :].rearrange("p k s -> p (k s)"),
                                         tp[(batch0 + m) % 2][:, 0:nk * S], ACT.Copy).then_inc(st_high, 1)

            def attention(n_items, item0, tp0, prob_b, prob_tb):
                for n in range(n_items + 2):
                    if n < n_items:
                        m = item0 + n
                        step, r = divmod(n, R)
                        act.wait_ge(maxed, m + 1)
                        if n >= 3:
                            act.wait_ge(tp_filled, tp0 + n - 2)
                        for t in range(T):
                            w = (t + 1) * P
                            c0 = t * P
                            e = nc.scalar.activation(
                                prob_b[:, n % 3, c0:c0 + w], score[n % 4][:, c0:c0 + w], ACT.Exp,
                                bias=nmax[:, n % 4, t:t + 1],
                                accum_out=sums[:, step % 4, t * R + r:t * R + r + 1])
                        e.then_inc(exped, 1)
                    if n >= 2 and TP_EMPTIED[tp0 + n - 2] == "act":
                        b = tp0 + n - 2
                        act.wait_ge(tp_filled, b + 1)
                        nc.scalar.activation(prob_tb[:, (n - 2) % 2, 0:3 * P], tp[b % 2][:, 0:3 * P],
                                             ACT.Copy).then_inc(tp_empty_act, 1)

            def feed_forward(up, down, unit0, tp0):
                def unit(u, i=None):
                    for q in range(4):
                        s = up + 4 * u + 4 + q
                        b = s // 2
                        if q == 2 and (u > 0 or i is not None):
                            batch = tp0 + u - 1
                            act.wait_ge(tp_filled, at(i, batch + 1, 2))
                            nc.scalar.activation(hid_hi[:, bass.ds(at(i, (u - 1) * 512, 1024), 512)],
                                                 tp[batch % 2][:], ACT.Copy).then_inc(st_high, 1)
                        stride = 32
                        if i is not None or s < down:
                            lv = at(i, LANDED[b], stride)
                        else:
                            lv = LANDED[b]
                        high(s, i, lv)
                    act.wait_ge(slot_used, at(i, up + 4 * u + 4, 8))
                    for t in range(T):
                        nc.scalar.activation(silu_a[:, u % 2, t, :], lin[2 * ((unit0 + u) % 2) + t][:, 0:HU],
                                             ACT.Silu).then_inc(silu_ready, 1)

                unit(0)
                with act.Fori(0, (FU - 3) // 2) as i:
                    unit(1, i)
                    unit(2, i)
                unit(FU - 2)
                unit(FU - 1)
                made[0] = down + 4
                high_to(down + 5)
                high_from_tp(tp0 + FU - 1, hid_hi[:, (FU - 1) * 512:FU * 512])
                high_to(down + FK)

            with nc.allow_non_contiguous_dma(reason="vectors laid out over partitions"):
                act.dma_start(cond[:], c_in[0].rearrange("(k p) -> p k", p=P)).then_inc(cond_landed, 16)
                act.dma_start(gate_rows[0:1].rearrange("p s n -> p (s n)"),
                              ada_b[0:1, 0:2 * D]).then_inc(first_bias, 16)
            act.wait_ge(cond_landed, 16)
            nc.scalar.activation(cond[:], cond[:], ACT.Silu).then_inc(cond_ready, 1)
            with nc.allow_non_contiguous_dma(reason="vectors laid out over partitions"):
                for dst, src in smalls[:1]:
                    act.dma_start(dst, src).then_inc(first_gain, 16)
            squares_of_x(0, 0)
            squares_of_x(0, 1)
            with nc.allow_non_contiguous_dma(reason="vectors laid out over partitions"):
                for dst, src in smalls[1:]:
                    act.dma_start(dst, src).then_inc(small_in, 16)
            high_to(4)
            modulated(0, T_H0, 0)

            def empty_unit(unit, s_end, dst, c0, n, sq=None):
                high_to(s_end + 4)
                unit_done(s_end)
                for t in range(T):
                    bank = lin[2 * (unit % 2) + t]
                    if sq is not None:
                        w = sq.shape[1] // T
                        nc.scalar.activation(sq[:, t * w:(t + 1) * w], bank[:, 0:w], ACT.Square)
                    ev = nc.scalar.activation(dst[:, t, c0:c0 + n], bank[:, 0:n], ACT.Copy)
                ev.then_inc(unit_empty_act, 1)

            def blocks_high(b):
                act.wait_ge(a_full, b + 1)
                nc.scalar.activation(a_hi[:].rearrange("p m c -> p (m c)"), scratch[:],
                                     ACT.Copy).then_inc(a_high, 1)

            def compressed_hidden(b, unit, s_end):
                high_to(s_end + 4)
                unit_done(s_end)
                nc.scalar.activation(tfull[:, 0, b * CH:(b + 1) * CH], lin[2 * (unit % 2)][:, 0:CH],
                                     ACT.Silu).then_inc(unit_empty_act, 1)

            def before_norm(s, k, column_halves=False):
                if not column_halves:
                    high_to(s + 2)
                squares_of_x(k, 0)
                squares_of_x(k, 1, [0])
                high_to(s + 2)
                squares_of_x(k, 1, [1])
                high_to(s + 4)

            empty_unit(U_KVC, KVC0 + 4, proj, 1024, 512)
            empty_unit(U_KVS, KVS0 + 4, proj, 1536, 512, sq_keys[0])
            for b in range(2):
                act.wait_ge(tp_filled, T_KVC + b + 1)
                nc.scalar.activation(kv_t[:, b, :], tp[(T_KVC + b) % 2][:], ACT.Copy).then_inc(tp_empty_act, 1)
                act.wait_ge(tp_empty_act, b + 1)
                for odd in range(2):
                    src = kv_t[64 * odd:64 * odd + 64, b, :].rearrange("p (j s) -> p j s", j=2)
                    act.dma_start(z[0:64, b, odd::2, :], src).then_inc(z_done, 16)
                    act.dma_start(z[64:128, b, odd::2, 0:S - 1], src[:, :, 1:S]).then_inc(z_done, 16)

            def keys_copied(b):
                for m in range(2):
                    batch = T_K + 2 * b + m
                    act.wait_ge(tp_filled, batch + 1)
                    for u in range(2):
                        half_p = slice(64 * u, 64 * u + 64)
                        ev = nc.scalar.activation(
                            k_t[u][half_p, b, 2 * m:2 * m + 2, :].rearrange("p g s -> p (g s)"),
                            tp[batch % 2][half_p, :], ACT.Copy, scale=nsa_gains[half_p, 2 + b:3 + b])
                    ev.then_inc(tp_empty_act, 1)

            def hidden_copied(b):
                batch = (T_SCK, T_SCV)[b]
                act.wait_ge(tp_filled, batch + 1)
                nc.scalar.activation(sc_t[:, b * 256:(b + 1) * 256], tp[batch % 2][:, 0:256],
                                     ACT.Copy).then_inc(tp_empty_act, 1)

            empty_unit(U_KVW, KVW0 + 4, proj, 2048, 512, sq_keys[1])
            keys_copied(0)
            blocks_high(0)
            act.wait_ge(z_done, 16 * 4 * 2)
            empty_unit(U_QA, QA0 + 4, proj, 0, 512, sq_queries[0])
            high_to(GATE0 + 2 + 4)
            unit_done(GATE0 + 2)
            nc.scalar.activation(gates_t[:], lin[2 * (U_GATE % 2)][0:NG, 0:S], ACT.Copy).then_inc(
                unit_empty_act, 1)
            high_to(QB0 + 2)
            keys_copied(1)
            compressed_hidden(0, U_CMPK, CMPK0 + 4)
            act.wait_ge(tp_filled, T_G + 1)
            nc.scalar.activation(gates[:].rearrange("p t n -> p (t n)"), tp[T_G % 2][:, 0:T * NG],
                                 ACT.Copy).then_inc(tp_empty_act, 1)
            blocks_high(1)
            act.wait_ge(xn_ready, T + 2)
            empty_unit(U_QB, QB0 + 4, proj, 512, 512, sq_queries[1])
            hidden_copied(0)
            compressed_hidden(1, U_CMPV, CMPV0 + 4)
            act.wait_ge(scale_in_gain, 1)
            for u in range(2):
                act.wait_ge(tp_filled, T_QB + u + 1)
                nc.scalar.activation(q_t[:, 4 + 2 * u:6 + 2 * u, :].rearrange("p k s -> p (k s)"),
                                     tp[(T_QB + u) % 2][:], ACT.Copy,
                                     scale=nsa_gains[:, 0:1]).then_inc(tp_empty_act, 1)
            hidden_copied(1)
            act.wait_ge(tp_empty_act, count_before(TP_EMPTIED, T_G + 1, "act"))
            nc.scalar.activation(gates[:], gates[:], ACT.Exp, scale=-1.0).then_inc(gate_exp, 1)
            for t in range(T):
                act.wait_ge(cmp_maxed, t + 1)
                nc.scalar.activation(tfull[:, t, :], tfull[:, t, :], ACT.Exp).then_inc(cmp_exped, 1)
            for t in range(T):
                act.wait_ge(tp_filled, T_PC + t + 1)
                nc.scalar.activation(probc_t[:, t, :], tp[(T_PC + t) % 2][:], ACT.Copy).then_inc(tp_empty_act, 1)
            attention(2 * H, 0, T_P0, prob, prob_t)
            output_high(T_O0)
            before_norm(OUT0 + 8, 1)
            modulated(1, T_HF0, 3)
            feed_forward(UP0, DOWN0, U_UP0, T_HID0)

            before_norm(DOWN0 + FK, 2, True)
            modulated(2, T_H1, 6)

            def latents(u, s_end, parts):
                high_to(KVB1 + (0, 3)[u])
                unit_done(s_end)
                n = parts[-1][1]
                c0 = (QL, 0)[u]
                for t in range(T):
                    bank = lin[2 * ((U_IN1 + u) % 2) + t]
                    for first, last, col in parts:
                        junk = (2 * u + t) * 512 + first
                        nc.scalar.activation(scratch[:, junk:junk + last - first], bank[:, first:last],
                                             ACT.Square, accum_out=stat[:, 0, col + t:col + t + 1])
                    ev = nc.scalar.activation(proj1[:, t, c0:c0 + n], bank[:, 0:n], ACT.Copy)
                ev.then_inc(unit_empty_act, 1)

            def latent_high(m):
                k0, nk = LATENTS[m]
                scaled_high(T_CQ + m, k0, nk, lat_gains[:, k0:k0 + nk])

            latents(0, INB1, ((0, KVL, 2), (KVL, KVL + ROT, 4)))
            high_to(KVB1 + 2)
            latent_high(0)
            latents(1, KVB1, ((0, QL, 0),))
            act.wait_ge(unit_empty_act, count_before(UNIT_EMPTIED, U_IN1 + 2, "act"))
            sq_view = scratch[:].rearrange("p (t h d) -> p t h d", t=T, h=H)
            for u in range(4):
                high_to(KVB1 + u + 1 + 4)
                unit_done(KVB1 + u + 1)
                for t in range(T):
                    kv = lin[2 * ((U_KVB1 + u) % 2) + t][:].rearrange("p (h d) -> p h d", d=2 * DH)
                    heads = slice(R * u, R * u + R)
                    nc.scalar.activation(k_tok[:, t, heads, 0:NOPE], kv[:, :, 0:NOPE], ACT.Copy)
                    nc.scalar.activation(sq_view[:, t, heads, :], kv[:, :, 0:NOPE], ACT.Square)
                    ev = nc.scalar.activation(v_tok[:, t, heads, :], kv[:, :, NOPE:], ACT.Copy)
                ev.then_inc(unit_empty_act, 1)
                if u == 1:
                    latent_high(1)
                    latent_high(2)
                    act.wait_ge(trig_arg, 2)
                    nc.scalar.activation(cs[:].rearrange("p a t n -> p (a t n)"),
                                         trig[:, 0:2, :].rearrange("p a n -> p (a n)"),
                                         ACT.Sin).then_inc(trig_done, 1)

            def heads_copied(batch, j, dst, which):
                act.wait_ge(tp_filled, batch + 1)
                nc.scalar.activation(dst[0:DQ, 2 * j:2 * j + 2, :].rearrange("p h s -> p (h s)"),
                                     tp[batch % 2][0:DQ, :], ACT.Copy,
                                     scale=qk_gain_cols[0:DQ, which:which + 1]).then_inc(tp_empty_act, 1)

            for u in range(4):
                high_to(QB1 + 2 * u + 2 + 4)
                if u == 3:
                    for j in range(2):
                        heads_copied(T_K1 + j, j, k1_t, 1)
                unit_done(QB1 + 2 * u + 2)
                for t in range(T):
                    bank = lin[2 * ((U_QB1 + u) % 2) + t][:, 0:QU]
                    if u >= 2 and t == 0:
                        act.wait_ge(q_summed, u - 1)
                    nc.scalar.activation(q_squares[u % 2][:, t, :], bank, ACT.Square)
                    ev = nc.scalar.activation(q_tok[:, t, QU * u:QU * u + QU], bank, ACT.Copy)
                ev.then_inc(unit_empty_act, 1)
                if u == 3:
                    for j in range(2, 8):
                        heads_copied(T_K1 + j, j, k1_t, 1)
            for j in (0, 1, 2, 3, 4, 6):
                heads_copied(T_Q1 + j, j, q1_t, 0)
            nc.scalar.activation(table_exp[:], ones[:, 0:1], ACT.Exp)
            act.wait_ge(tp_filled, T_P1)
            attention(H, 2 * H, T_P1, prob1, prob1_t)
            output_high(T_O1)
            before_norm(OUT1 + 8, 3)
            modulated(3, T_HF1, 9)
            feed_forward(UP1, DOWN1, U_UP1, T_HID1)

        @block.vector
        def _(dve):
            steps = [0]
            made = [0]
            counts = {"scaled": 0, "st": 0, "squares": 0, "item": 0, "blocks": 0, "silu": 0}

            def link(ins):
                steps[0] += 1
                ins.then_inc(dve_step, 1)
                dve.wait_ge(dve_step, steps[0])

            def low(s, i=None):
                dve.wait_ge(hi_ready, at(i, s + 1, 8))
                nc.vector.tensor_tensor(part_of(w_lo, s), raw_part(s), part_of(w_hi, s).bitcast(F32),
                                        ALU.subtract).then_inc(lo_ready, 1)

            def low_to(n):
                while made[0] < n:
                    low(made[0])
                    made[0] += 1

            def reciprocal_roots(n, widths, c0=0):
                first = c0
                for cnt, width in widths:
                    ins = nc.vector.tensor_scalar(stat[:, 1, c0:c0 + cnt], stat[:, 0, c0:c0 + cnt],
                                                  1.0 / width, EPS, ALU.mult, ALU.add)
                    c0 += cnt
                link(ins)
                v, y, a = (stat[:, j, first:first + n] for j in (1, 3, 4))
                link(nc.vector.tensor_scalar(y.bitcast(I32), v.bitcast(I32), 1, None,
                                             ALU.logical_shift_right))
                link(nc.vector.tensor_scalar(y.bitcast(I32), y.bitcast(I32), -1.0, float(0x5F3759DF),
                                             ALU.mult, ALU.add))
                link(nc.vector.tensor_tensor(a, y, y, ALU.mult))
                link(nc.vector.tensor_tensor(a, a, v, ALU.mult))
                link(nc.vector.scalar_tensor_tensor(a, a, -10 / 3, a, ALU.add, ALU.mult))
                link(nc.vector.scalar_tensor_tensor(y, a, 5.0, y, ALU.add, ALU.mult))
                c = 3 / 8
                link(nc.vector.scalar_tensor_tensor(a, y, -0.5 * c ** 3, y, ALU.mult, ALU.mult))
                link(nc.vector.tensor_tensor(a, a, v, ALU.mult))
                link(nc.vector.scalar_tensor_tensor(y, a, 1.5 * c, y, ALU.add, ALU.mult))

            def normalise_x():
                counts["squares"] += 2 * T
                dve.wait_ge(squares, counts["squares"])
                link(nc.vector.tensor_tensor(stat[:, 0, 0:T], stat[:, 0, 0:T], stat[:, 0, T:2 * T], ALU.add))
                reciprocal_roots(T, [(T, D)])
                for n in range(2):
                    for t in range(T):
                        ins = nc.vector.tensor_scalar(
                            scratch[:, t * D + 512 * n:t * D + 512 * n + 512], x[:, t, 512 * n:512 * n + 512],
                            stat[:, 3, t:t + 1], None, ALU.mult)
                    ins.then_inc(xn_ready, 1)

            def scaled_low(k0, nk):
                m = counts["scaled"]
                counts["scaled"] += 1
                counts["st"] += 1
                dve.wait_ge(st_high, counts["st"])
                nc.vector.tensor_tensor(
                    st_lo[:, k0:k0 + nk, :], tfull[:, m % 2, 0:nk * S].rearrange("p (k s) -> p k s", k=nk),
                    st_hi[:, k0:k0 + nk, :].bitcast(F32), ALU.subtract).then_inc(st_ready, 1)

            def modulated(s):
                low_to(s + 2)
                for m, (k0, nk) in enumerate(PIECES):
                    scaled_low(k0, nk)
                    if 1 <= m < 3:
                        low_to(s + 2 + m)

            def low_from_tp(batch, hi, lo, i=None):
                counts["st"] += 1
                dve.wait_ge(st_high, at(i, counts["st"], 2))
                nc.vector.tensor_tensor(lo, tp[batch % 2][:], hi.bitcast(F32), ALU.subtract).then_inc(st_ready, 1)

            def ada_columns(seg):
                dve.wait_ge(ada_red, seg + 1)
                nc.vector.tensor_copy(ada_cols[:, seg, :], sc[seg % 2][:, 0:KD]).then_inc(ada_out, 1)

            def ada_row(seg, row):
                dve.wait_ge(ada_red, seg + 1)
                nc.vector.tensor_copy(gate_rows[:, row, 0:512], sc[0][:])
                nc.vector.tensor_copy(gate_rows[:, row, 512:D], sc[1][:]).then_inc(ada_out, 1)

            def modulation(norm, scale_seg):
                dve.wait_ge(ada_out, scale_seg + 1)
                link(nc.vector.tensor_scalar(scale_cols[:, norm, :], ada_cols[:, scale_seg, :], 1.0, None,
                                             ALU.add))
                nc.vector.tensor_tensor(scale_cols[:, norm, :], scale_cols[:, norm, :],
                                        gain_cols[:, norm, :], ALU.mult).then_inc(scales_ready, 1)

            def update_x(unit, row, n, done, first_tile=None):
                for t in range(T):
                    if t == 0 and first_tile is not None:
                        dve.wait_ge(part_done, first_tile)
                    else:
                        dve.wait_ge(*done)
                    tmp = scratch[:, (2 * n + t) * 512:(2 * n + t + 1) * 512]
                    ins = nc.vector.tensor_tensor(tmp, lin[2 * (unit % 2) + t][:],
                                                  gate_rows[:, row, 512 * n:512 * n + 512], ALU.mult)
                    if t == T - 1:
                        ins.then_inc(unit_empty_dve, 1)
                        dve.wait_ge(unit_empty_dve, count_before(UNIT_EMPTIED, unit + 1, "dve"))
                    else:
                        link(ins)
                    xs = x[:, t, 512 * n:512 * n + 512]
                    nc.vector.tensor_tensor(xs, xs, tmp, ALU.add).then_inc(resid, 1)

            def group_norm(src, n_cols, groups, width, squares_buf):
                link(nc.vector.tensor_tensor(squares_buf, src, src, ALU.mult))
                return nc.vector.tensor_reduce(stat[:, 0, n_cols:n_cols + groups], squares_buf, X, ALU.add)

            def attention(n_items, tp0, prob_tb, emit_step, finish_step=lambda k: None,
                          before=lambda n: None):
                for n in range(n_items + R + 3):
                    before(n)
                    if n < n_items:
                        m = counts["item"]
                        counts["item"] += 1
                        dve.wait_ge(scored, m + 1)
                        bank = score[n % 4]
                        nc.vector.tensor_reduce(nmax[:, n % 4, 0:1], bank[:, 0:P], X, ALU.max, negate=True)
                        nc.vector.tensor_reduce(nmax[:, n % 4, 1:2], bank[:, P:3 * P], X, ALU.max,
                                                negate=True).then_inc(maxed, 1)
                    if 2 <= n < n_items + 2 and TP_EMPTIED[tp0 + n - 2] == "dve":
                        b = tp0 + n - 2
                        dve.wait_ge(tp_filled, b + 1)
                        nc.vector.tensor_copy(prob_tb[:, (n - 2) % 2, 0:3 * P],
                                              tp[b % 2][:, 0:3 * P]).then_inc(tp_empty_dve, 1)
                    if n >= 2 * R and n % R == 0:
                        emit_step(n // R - 2)
                    if n >= 2 * R + 2 and n % R == 2:
                        finish_step(n // R - 2)

            def feed_forward(up, down, unit0, tp0, at_start=lambda: None, at_end=lambda: None):
                st0 = counts["st"]

                def unit(u, i=None):
                    for q in range(4):
                        s = up + 4 * u + 4 + q
                        if q == 2 and (u > 0 or i is not None):
                            batch = tp0 + u - 1
                            dve.wait_ge(st_high, at(i, st0 + u, 2))
                            cols = bass.ds(at(i, (u - 1) * 512, 1024), 512)
                            nc.vector.tensor_tensor(hid_lo[:, cols], tp[batch % 2][:],
                                                    hid_hi[:, cols].bitcast(F32),
                                                    ALU.subtract).then_inc(st_ready, 1)
                        low(s, i)
                    for t in range(T):
                        dve.wait_ge(silu_ready, at(i, silu0 + T * u + t + 1, 2 * T))
                        ins = nc.vector.tensor_tensor(hid[:, u % 2, t, :], silu_a[:, u % 2, t, :],
                                                      lin[2 * ((unit0 + u) % 2) + t][:, HU:2 * HU], ALU.mult)
                    ins.then_inc(unit_empty_dve, 1)

                silu0 = counts["silu"]
                for u in range(3):
                    unit(u)
                at_start()
                with dve.Fori(0, (FU - 5) // 2) as i:
                    unit(3, i)
                    unit(4, i)
                at_end()
                unit(FU - 2)
                unit(FU - 1)
                counts["silu"] = silu0 + T * FU
                made[0] = down + 4
                low_to(down + 5)
                counts["st"] = st0 + FU - 1
                low_from_tp(tp0 + FU - 1, hid_hi[:, (FU - 1) * 512:FU * 512], hid_lo[:, (FU - 1) * 512:FU * 512])

            nc.vector.memset(qk_gain_cols[NOPE:P], 1.0)
            nc.vector.memset(k_even[64:128], 0.0)
            nc.vector.memset(k_odd[0:64], 0.0)
            nc.vector.memset(kc_t[64:128, 0], 0.0)
            nc.vector.memset(kc_t[0:64, 1], 0.0)
            dve.wait_ge(cond_ready, 1)
            for a in range(2 * KD):
                pair, j = divmod(a, 4)
                part, seg = divmod(j, 2)
                slot, kt = 2 * pair + seg, 2 * pair + part
                dve.wait_ge(landed[slot % RING], 16 * (slot // RING + 1))
                chunk = raw[:, slot % RING, part * HALF:(part + 1) * HALF]
                acc = ada_acc[:, seg, :]
                if a < 2:
                    ins = nc.vector.tensor_scalar(acc, chunk, cond[:, kt:kt + 1], None, ALU.mult)
                else:
                    dve.wait_ge(ada_used, a - 1)
                    ins = nc.vector.scalar_tensor_tensor(acc, chunk, cond[:, kt:kt + 1], acc, ALU.mult,
                                                         ALU.add)
                ins.then_inc(ada_used, 1)
                if a == 2 * KD - 5:
                    normalise_x()
            ada_columns(0)
            ada_columns(1)
            dve.wait_ge(first_gain, 16)
            modulation(0, 1)
            modulated(0)
            dve.wait_ge(small_in, N_SMALL)
            nc.vector.tensor_scalar(nsa_gains[:, 0:1], nsa_gains[:, 0:1], float(DH ** -0.5), None,
                                    ALU.mult).then_inc(scale_in_gain, 1)
            dve.wait_ge(scale_in_gain, 1)

            def normed_keys(b, c0):
                link(nc.vector.tensor_reduce(stat[:, 0, 0:T * G], sq_keys[b].rearrange(
                    "p (n d) -> p n d", d=DH), X, ALU.add))
                reciprocal_roots(T * G, [(T * G, DH)])
                src = proj[:, :, c0:c0 + G * DH].rearrange("p t (g d) -> p t g d", g=G)
                dst = kdup_o[:, b, :].rearrange("p (t g u d) -> p t g u d", t=T, g=G, u=2)
                root = stat[:, 3, 0:T * G].rearrange("p (t g) -> p t g", t=T).unsqueeze(3).broadcast_to(
                    [P, T, G, DH])
                for u in range(2):
                    ins = nc.vector.tensor_tensor(dst[:, :, :, u, :], src, root, ALU.mult)
                ins.then_inc(xn_ready, 1)

            def blocks(b):
                a_view = scratch[:].rearrange("p (m g c) -> p m g c", m=CM, g=G)
                dve.wait_ge(z_done, 16 * 4 * 2)
                if b == 1:
                    dve.wait_ge(a_ready, 1)
                for g in range(G):
                    zg = z[:, b, g, :].rearrange("p (c m u) -> p u m c", u=2, m=CM // 2)
                    for hm in range(2):
                        src = zg[:, 0, :, hm:hm + NCMP]
                        pe = pe_cols[:, b, hm * 8:hm * 8 + 8].unsqueeze(2).broadcast_to([P, 8, NCMP])
                        ins = nc.vector.tensor_tensor(a_view[:, hm * 8:hm * 8 + 8, g, 0:NCMP], src, pe, ALU.add)
                ins.then_inc(a_full, 1)

            def blocks_low():
                counts["blocks"] += 1
                dve.wait_ge(a_high, counts["blocks"])
                nc.vector.tensor_tensor(a_lo[:].rearrange("p m c -> p (m c)"), scratch[:],
                                        a_hi[:].rearrange("p m c -> p (m c)").bitcast(F32),
                                        ALU.subtract).then_inc(a_ready, 1)

            def scaled_copy(batch, dst, gain):
                dve.wait_ge(tp_filled, batch + 1)
                nc.vector.tensor_scalar(dst, tp[batch % 2][:], gain, None, ALU.mult).then_inc(tp_empty_dve, 1)

            def normed_queries(half_of):
                c0 = half_of * D // 2
                link(nc.vector.tensor_reduce(stat[:, 0, 0:T * 8], sq_queries[half_of].rearrange(
                    "p (n d) -> p n d", d=DH), X, ALU.add))
                reciprocal_roots(T * 8, [(T * 8, DH)])
                src = proj[:, :, c0:c0 + D // 2].rearrange("p t (h d) -> p t h d", d=DH)
                nc.vector.tensor_tensor(src, src, stat[:, 3, 0:T * 8].rearrange(
                    "p (t h) -> p t h", t=T).unsqueeze(3).broadcast_to([P, T, 8, DH]),
                    ALU.mult).then_inc(xn_ready, 1)

            low_to(8)
            link(nc.vector.memset(scratch[:], 0.0))
            low_to(12)
            dve.wait_ge(unit_empty_act, 2)
            normed_keys(0, 1536)
            low_to(16)
            blocks(0)
            dve.wait_ge(unit_empty_act, 3)
            normed_keys(1, 2048)
            low_to(CMPK0)
            blocks_low()
            low_to(QB0)
            low_to(QB0 + 2)
            blocks(1)
            low_to(QB0 + 4)
            dve.wait_ge(unit_empty_act, U_QA + 1)
            normed_queries(0)
            blocks_low()
            low_to(CMPV0 + 3)
            for u in range(2):
                scaled_copy(T_QA + u, q_t[:, 2 * u:2 * u + 2, :].rearrange("p k s -> p (k s)"),
                            nsa_gains[:, 0:1])
            low_to(CMPV0 + 4)
            dve.wait_ge(unit_empty_act, U_QB + 1)
            normed_queries(1)
            dve.wait_ge(tp_filled, T_CK + 1)
            kc = scratch[:, 0:DH]
            nc.vector.tensor_copy(kc, tp[T_CK % 2][:, 0:DH]).then_inc(tp_empty_dve, 1)
            dve.wait_ge(tp_empty_dve, count_before(TP_EMPTIED, T_CK + 1, "dve"))
            link(group_norm(kc.unsqueeze(1), 0, 1, DH, scratch[:, DH:2 * DH].unsqueeze(1)))
            reciprocal_roots(1, [(1, DH)])
            for u in range(2):
                ins = nc.vector.tensor_scalar(scratch[:, (2 + u) * DH:(3 + u) * DH], kc, stat[:, 3, 0:1], None,
                                              ALU.mult)
            ins.then_inc(xn_ready, 1)
            dve.wait_ge(tp_filled, T_KC + 1)
            for u in range(2):
                half_p = slice(64 * u, 64 * u + 64)
                ins = nc.vector.tensor_scalar(kc_t[half_p, u].rearrange("p g c -> p (g c)"),
                                              tp[T_KC % 2][half_p, 0:P], nsa_gains[half_p, 1:2], None, ALU.mult)
            ins.then_inc(tp_empty_dve, 1)
            dve.wait_ge(tp_filled, T_CV + 1)
            for g in range(G):
                ins = nc.vector.tensor_copy(v_cmp[CP * g:CP * g + CP, g, :],
                                            tp[T_CV % 2][CP * g:CP * g + CP, 0:DH])
            ins.then_inc(tp_empty_dve, 1)
            dve.wait_ge(slot_used, CMPV0 + 4)
            ada_row(2, 0)
            ada_columns(3)
            for t in range(T):
                dve.wait_ge(cmp_scored, t + 1)
                s4 = lin[t][:].rearrange("p (h c) -> p h c", c=CP)
                mx = cstat[:, t, :]
                link(nc.vector.tensor_reduce(mx, s4, X, ALU.max))
                link(nc.vector.tensor_scalar(mx, mx, FLOOR, None, ALU.max))
                nc.vector.tensor_tensor(tfull[:, t, :].rearrange("p (h c) -> p h c", c=CP), s4,
                                        mx.unsqueeze(2).broadcast_to([P, H, CP]),
                                        ALU.subtract).then_inc(cmp_maxed, 1)
            dve.wait_ge(gate_exp, 1)
            link(nc.vector.tensor_scalar(gates[:], gates[:], 1.0, None, ALU.add))
            link(nc.vector.reciprocal(gates[:], gates[:]))
            gate_view = gates[:].rearrange("p t (g r u b) -> p t r u g b", g=G, u=2, b=3)

            def compressed_weights():
                for t in range(T):
                    dve.wait_ge(cmp_exped, t + 1)
                    cf = cstat[:, t, :]
                    link(nc.vector.tensor_reduce(cf, tfull[:, t, :].rearrange("p (h c) -> p h c", c=CP), X,
                                                 ALU.add))
                    link(nc.vector.tensor_scalar(cf, cf, TINY, None, ALU.max))
                    link(nc.vector.reciprocal(cf, cf))
                    cf4 = cf.rearrange("p (r u g) -> p r u g", r=2, u=2)
                    link(nc.vector.tensor_tensor(cf4, cf4, gate_view[:, t, :, :, :, 0], ALU.mult))

            def compressed_output(n):
                if n != 2:
                    return
                compressed_weights()
                for t in range(T):
                    o_view = o0[:, t, :].rearrange("p (g r u d) -> p r u g d", g=G, u=2, d=DH)
                    for pair in range(2):
                        bank = CMP_BANKS[2 * t + pair]
                        dve.wait_ge(cmp_pv, 2 * t + pair + 1)
                        for u in range(2):
                            j = 2 * pair + u
                            cf = cstat[:, t, j * G:(j + 1) * G]
                            ins = nc.vector.tensor_tensor(
                                o_view[:, pair, u], bank[:, u * 256:(u + 1) * 256].rearrange(
                                    "p (g d) -> p g d", g=G),
                                cf.unsqueeze(2).broadcast_to([P, G, DH]), ALU.mult)
                        ins.then_inc(cmp_added, 1)
                dve.wait_ge(cmp_added, 4)

            def nsa_step(k):
                g, b = divmod(k, 2)
                cf = coef[:, 0, :]
                dve.wait_ge(pv_done, k + 1)
                link(nc.vector.tensor_scalar(cf, sums[:, k % 4, :], TINY, None, ALU.max))
                link(nc.vector.reciprocal(cf, cf))
                gv = gates[:].rearrange("p t (h b) -> p t h b", b=3)[:, :, R * g:R * g + R, 1 + b]
                cf3 = cf.rearrange("p (t r) -> p t r", t=T)
                link(nc.vector.tensor_tensor(cf3, cf3, gv, ALU.mult))
                tmp = scratch[:, 512 * (k % 4):512 * (k % 4) + 512]
                nc.vector.tensor_tensor(tmp.rearrange("p (h d) -> p h d", d=DH),
                                        lin[k % 2][:].rearrange("p (h d) -> p h d", d=DH),
                                        cf.unsqueeze(2).broadcast_to([P, T * R, DH]),
                                        ALU.mult).then_inc(pv_empty, 1)

            def nsa_add(k):
                g = k // 2
                og = o0[:, :, 256 * g:256 * g + 256]
                tmp = scratch[:, 512 * (k % 4):512 * (k % 4) + 512]
                dve.wait_ge(pv_empty, k + 1)
                nc.vector.tensor_tensor(og, og, tmp.rearrange("p (t n) -> p t n", t=T),
                                        ALU.add).then_inc(o_steps, 1)
                dve.wait_ge(o_steps, k + 1)

            def between_items(n):
                compressed_output(n)
                if n % R == 1 and R <= n < 5 * R:
                    low_to(OUT0 + n // R)

            attention(2 * H, T_P0, prob_t, nsa_step, nsa_add, between_items)

            def odd_heads(u):
                batch = T_Q1 + 2 * u + 1
                dve.wait_ge(tp_filled, batch + 1)
                nc.vector.tensor_scalar(q1_t[0:DQ, R * u + 2:R * u + 4, :].rearrange("p h s -> p (h s)"),
                                        tp[batch % 2][0:DQ, :], qk_gain_cols[0:DQ, 0:1], None,
                                        ALU.mult).then_inc(tp_empty_dve, 1)

            def output_low(batch0):
                for m, (k0, nk) in enumerate(PIECES):
                    counts["st"] += 1
                    dve.wait_ge(st_high, counts["st"])
                    nc.vector.tensor_tensor(
                        st_lo[:, k0:k0 + nk, :].rearrange("p k s -> p (k s)"), tp[(batch0 + m) % 2][:, 0:nk * S],
                        st_hi[:, k0:k0 + nk, :].rearrange("p k s -> p (k s)").bitcast(F32),
                        ALU.subtract).then_inc(st_ready, 1)

            output_low(T_O0)
            low_to(OUT0 + 8)
            ada_columns(4)
            modulation(1, 4)
            update_x(U_OUT0, 0, 0, (slot_used, OUT0 + 4))
            low_to(OUT0 + 10)
            update_x(U_OUT0 + 1, 0, 1, (slot_used, OUT0 + 8), 1)
            normalise_x()
            modulated(UP0)
            ada_row(5, 1)

            feed_forward(UP0, DOWN0, U_UP0, T_HID0, lambda: ada_columns(6), lambda: ada_columns(7))
            low_to(DOWN0 + 19)
            ada_row(8, 0)
            low_to(DOWN0 + FK)
            modulation(2, 7)
            update_x(U_DOWN0, 1, 0, (part_done, 2))
            update_x(U_DOWN0 + 1, 1, 1, (slot_used, DOWN0 + FK), 3)
            low_to(DOWN0 + FK + 1)

            normalise_x()
            modulated(IN1)
            dve.wait_ge(inv_ready, 1)
            two_pi = 2 * np.pi
            pieces, left = [], two_pi
            for bits in (7, 8, 8):
                scale = 2.0 ** (bits - 1 - np.floor(np.log2(left)))
                piece = float(np.floor(left * scale) / scale)
                pieces.append(piece)
                left -= piece
            pieces.append(float(np.float32(left)))
            ang = trig[:, 2, :]
            pos_f = stat[:, 5, 0:T]
            link(nc.vector.tensor_copy(pos_f, pos_i[:]))
            half_w = ROT // 2
            for t in range(T):
                ins = nc.vector.tensor_scalar(ang[:, t * half_w:(t + 1) * half_w], inv[:], pos_f[:, t:t + 1],
                                              None, ALU.mult)
            link(ins)
            magic = float(1.5 * 2 ** 23)

            def reduced_angle(j):
                turns = stat[:, 6, :]
                arg = trig[:, j, :]
                link(nc.vector.tensor_scalar(turns, ang, 1.0 / two_pi, 0.25 * j, ALU.mult, ALU.add))
                link(nc.vector.tensor_scalar(turns, turns, magic, None, ALU.add))
                link(nc.vector.tensor_scalar(turns, turns, -magic, None, ALU.add))
                src = ang
                for piece in pieces:
                    link(nc.vector.scalar_tensor_tensor(arg, turns, -piece, src, ALU.mult, ALU.add))
                    src = arg
                link(nc.vector.tensor_scalar(arg, arg, float(j * np.pi / 2), None, ALU.add))
                nc.vector.tensor_scalar(arg, arg, -3.1415925, 3.1415925, ALU.max, ALU.min).then_inc(trig_arg, 1)

            def scaled_latent(c0, w, col):
                for t in range(T):
                    src = proj1[:, t, c0:c0 + w]
                    ins = nc.vector.tensor_scalar(src, src, stat[:, 3, col + t:col + t + 1], None, ALU.mult)
                return ins

            low_to(KVB1)
            ada_columns(9)
            dve.wait_ge(unit_empty_act, count_before(UNIT_EMPTIED, U_IN1 + 1, "act"))
            reciprocal_roots(2 * T, [(T, KVL), (T, ROT)], 2)
            scaled_latent(QL, KVL, 2).then_inc(xn_ready, 1)
            scaled_latent(QL + KVL, ROT, 4)
            low_to(KVB1 + 2)
            scaled_low(*LATENTS[0])
            reduced_angle(0)
            reduced_angle(1)
            dve.wait_ge(unit_empty_act, count_before(UNIT_EMPTIED, U_IN1 + 2, "act"))
            reciprocal_roots(T, [(T, QL)])
            scaled_latent(0, QL, 0).then_inc(xn_ready, 1)
            low_to(KVB1 + 4)
            scaled_low(*LATENTS[1])
            scaled_low(*LATENTS[2])
            ada_columns(10)
            low_to(QB1 + 1)
            sin, cos = cs[:, 0], cs[:, 1]
            hw = ROT // 2
            dve.wait_ge(trig_done, 1)
            link(nc.vector.tensor_scalar(qk_gain_cols[:, 0:1], qk_gain_cols[:, 0:1], float(DQ ** -0.5), None,
                                         ALU.mult))
            for n, (factor, first) in enumerate(((cos, 0), (sin, hw), (sin, 0), (cos, hw))):
                ins = nc.vector.tensor_tensor(
                    cs_q[:, n], factor, q_gain_row[:, first:first + hw].unsqueeze(1).broadcast_to([P, T, hw]),
                    ALU.mult)
            link(ins)

            kr = proj1[:, :, QL + KVL:MLA_IN]
            link(nc.vector.tensor_tensor(kr, kr, k_gain_row[:].unsqueeze(1).broadcast_to([P, T, ROT]), ALU.mult))
            link(rotate(nc.vector, link, q_sq[:].rearrange("p t n -> p (t n)"), kr.unsqueeze(2), 1,
                        (cos, sin, sin, cos)))
            nc.vector.tensor_copy(k_tok[:, :, :, NOPE:DQ], kr.unsqueeze(2).broadcast_to([P, T, H, ROT]))
            sq_view = scratch[:].rearrange("p (t h d) -> p t h d", t=T, h=H)
            k_sums = stat[:, 0, :].rearrange("p (t h) -> p t h", t=T)
            k_roots = stat[:, 3, :].rearrange("p (t h) -> p t h", t=T)
            for u in range(4):
                dve.wait_ge(unit_empty_act, count_before(UNIT_EMPTIED, U_KVB1 + u + 1, "act"))
                ins = nc.vector.tensor_reduce(k_sums[:, :, R * u:R * u + R],
                                              sq_view[:, :, R * u:R * u + R, :], X, ALU.add)
                if u < 3:
                    low_to(QB1 + u + 1)
            link(ins)
            reciprocal_roots(T * H, [(T * H, NOPE)])
            low_to(QB1 + 6)
            k_nope = k_tok[:, :, :, 0:NOPE]
            nc.vector.tensor_tensor(k_nope, k_nope, k_roots.unsqueeze(3).broadcast_to([P, T, H, NOPE]),
                                    ALU.mult).then_inc(xn_ready, 1)
            for pair in range(2):
                q_sums = stat[:, 0, 0:2 * T * R].rearrange("p (u n) -> p u n", u=2)
                q_roots = stat[:, 3, 0:2 * T * R].rearrange("p (u t h) -> p u t h", u=2, t=T)
                for j in range(2):
                    u = 2 * pair + j
                    dve.wait_ge(unit_empty_act, count_before(UNIT_EMPTIED, U_QB1 + u + 1, "act"))
                    nc.vector.tensor_reduce(q_sums[:, j], q_squares[j].rearrange(
                        "p t (h d) -> p (t h) d", h=R), X, ALU.add).then_inc(q_summed, 1)
                if pair == 0:
                    low_to(QB1 + 8)
                dve.wait_ge(q_summed, 2 * pair + 2)
                reciprocal_roots(2 * T * R, [(2 * T * R, DQ)])
                for j in range(2):
                    u = 2 * pair + j
                    src = q_tok[:, :, QU * u:QU * u + QU].rearrange("p t (h d) -> p t h d", h=R)
                    nc.vector.tensor_tensor(src, src, q_roots[:, j].unsqueeze(3).broadcast_to([P, T, R, DQ]),
                                            ALU.mult).then_inc(q_scaled, 1)
                dve.wait_ge(q_scaled, 2 * pair + 2)
                rotate(nc.vector, link, scratch[:, 0:512], src[:, :, :, NOPE:DQ], R,
                       q_factors).then_inc(xn_ready, 1)
            for u in (2, 3):
                odd_heads(u)

            def mla_step(k):
                cf = coef[:, 0, :]
                dve.wait_ge(pv_done, 8 + k + 1)
                link(nc.vector.tensor_scalar(cf, sums[:, k % 4, :], TINY, None, ALU.max))
                link(nc.vector.reciprocal(cf, cf))
                og = o1[:, :, 256 * k:256 * k + 256].rearrange("p t (r d) -> p t r d", d=DH)
                ps = lin[k % 2][:].rearrange("p (t r d) -> p t r d", t=T, d=DH)
                for t in range(T):
                    ins = nc.vector.tensor_tensor(og[:, t], ps[:, t], cf[:, t * R:(t + 1) * R].unsqueeze(
                        2).broadcast_to([P, R, DH]), ALU.mult)
                ins.then_inc(pv_empty, 1)

            def output_weights(n):
                if n % R == 1 and n < H:
                    low_to(OUT1 + n // R + 1)

            attention(H, T_P1, prob1_t, mla_step, before=output_weights)
            output_low(T_O1)
            low_to(OUT1 + 8)
            modulation(3, 10)
            update_x(U_OUT1, 0, 0, (slot_used, OUT1 + 4))
            low_to(OUT1 + 10)
            update_x(U_OUT1 + 1, 0, 1, (slot_used, OUT1 + 8), 4)
            normalise_x()
            modulated(UP1)
            ada_row(11, 1)
            feed_forward(UP1, DOWN1, U_UP1, T_HID1)
            low_to(END)
            update_x(U_DOWN1, 1, 0, (part_done, 5))
            update_x(U_DOWN1 + 1, 1, 1, (slot_used, END), 6)

        @block.tensor
        def _(pe):
            xn = [0]

            def three(bank, a_h, a_l, w_h, w_l, first, last):
                nc.tensor.matmul(bank, a_h, w_h, start=first, stop=False)
                nc.tensor.matmul(bank, a_h, w_l, start=False, stop=False)
                return nc.tensor.matmul(bank, a_l, w_h, start=False, stop=last)

            def wait_unit(unit, i=None):
                if unit < 2 and i is None:
                    return
                who = UNIT_EMPTIED[unit - 2]
                pe.wait_ge(unit_empty[who], at(i, count_before(UNIT_EMPTIED, unit - 1, who), 2))

            def emptied(batch):
                who = TP_EMPTIED[batch]
                empty = {"act": tp_empty_act, "dve": tp_empty_dve, "st": st_ready}[who]
                return empty, count_before(TP_EMPTIED, batch + 1, who)

            def wait_tp(batch):
                if batch >= 2:
                    pe.wait_ge(*emptied(batch - 2))

            def transposes(batch, pieces, rows=P):
                wait_tp(batch)
                for n, src in enumerate(pieces):
                    ins = nc.tensor.transpose(tp[batch % 2][0:rows, n * P:(n + 1) * P], src, ident[:])
                ins.then_inc(tp_filled, 1)

            def last_unit(unit, s0):
                wait_unit(unit)
                for tiles, slots in ((range(T), (0, 1)), ((0,), (2, 3)), ((1,), (2, 3))):
                    for q in slots:
                        s = s0 + q
                        pe.wait_ge(lo_ready, s + 1)
                        for j, k in enumerate(FOUR[q]):
                            for t in tiles:
                                ah, al = stationary(k)[t]
                                ins = three(lin[2 * (unit % 2) + t][:], ah, al,
                                            w_hi[:, s % RING, 512 * j:512 * j + 512],
                                            w_lo[:, s % RING, 512 * j:512 * j + 512], k == 0, k == KD - 1)
                        if tiles != (0,):
                            ins.then_inc(slot_used, 1)
                    if tiles == (0,):
                        ins.then_inc(part_done, 1)

            def unit(unit, s0, slots, n, lhs, wait_st=None):
                wait_unit(unit)
                total = sum(len(k) for k in slots)
                done = 0
                for q, kts in enumerate(slots):
                    s = s0 + q
                    pe.wait_ge(lo_ready, s + 1)
                    wh = w_hi[:, s % RING, 0:len(kts) * n].rearrange("p (k c) -> p k c", c=n)
                    wl = w_lo[:, s % RING, 0:len(kts) * n].rearrange("p (k c) -> p k c", c=n)
                    for j, k in enumerate(kts):
                        if wait_st is not None:
                            wait_st(k)
                        for t, (ah, al) in enumerate(lhs(k)):
                            ins = three(lin[2 * (unit % 2) + t][:, 0:n], ah, al, wh[:, j], wl[:, j],
                                        done == 0, done == total - 1)
                        done += 1
                    ins.then_inc(slot_used, 1)

            def stationary(k):
                return [(st_hi[:, k, t * P:(t + 1) * P], st_lo[:, k, t * P:(t + 1) * P]) for t in range(T)]

            FOUR = [[0, 1], [2, 3], [4, 5], [6, 7]]

            def next_tokens():
                xn[0] += 1
                pe.wait_ge(xn_ready, xn[0])

            def x_batch(batch0, m):
                k0, nk = PIECES[m]
                if k0 in (0, KD // 2):
                    next_tokens()
                transposes(batch0 + m, [scratch[:, t * D + k * P:t * D + (k + 1) * P]
                                        for k in range(k0, k0 + nk) for t in range(T)])

            def o_batch(o):
                def batch(batch0, m):
                    k0, nk = PIECES[m]
                    transposes(batch0 + m, [o[:, t, k * P:(k + 1) * P] for k in range(k0, k0 + nk)
                                            for t in range(T)])
                return batch

            def st_wait(batch0, batch):
                def wait(k):
                    for m, (k0, nk) in enumerate(PIECES):
                        if k == k0:
                            pe.wait_ge(st_ready, stationary_number(batch0) + m + 1)
                            if m + 2 < len(PIECES):
                                batch(batch0, m + 2)
                return wait

            def wait_acc(seg):
                pe.wait_ge(acc_pool, seg - 1)
                pe.wait_ge(ada_out, seg)

            def reduce_columns(seg):
                if seg >= 2:
                    wait_acc(seg)
                for k in range(KD):
                    ins = nc.tensor.matmul(sc[seg % 2][:, k:k + 1], ada_acc[:, seg % 2, k * P:(k + 1) * P],
                                           ones[:, 0:1], start=(seg >= 2), stop=(seg >= 2 or k == KD - 1))
                ins.then_inc(ada_red, 1)

            def reduce_row(seg):
                wait_acc(seg)
                for n in range(2):
                    ins = nc.tensor.matmul(sc[n][:], ones[:], ada_acc[:, seg % 2, 512 * n:512 * n + 512],
                                           start=True, stop=True)
                ins.then_inc(ada_red, 1)

            def attention(n_items, item0, tp0, step0, q_of, k_of, v_of, prob_b, prob_tb,
                          before=lambda n: None):
                for n in range(n_items + 3):
                    before(n)
                    if n < n_items:
                        if n >= 4:
                            pe.wait_ge(exped, item0 + n - 3)
                        bank = score[n % 4]
                        for t in range(T):
                            w = (t + 1) * P
                            nc.tensor.matmul(bank[:, t * P:t * P + w], q_of(n, t), k_of(n, t + 1),
                                             start=True, stop=False)
                            ins = nc.tensor.matmul(bank[:, 2 * t * P:(2 * t + 1) * P], ident_b[:], tri[:],
                                                   start=False, stop=True)
                        ins.then_inc(scored, 1)
                    if 2 <= n < n_items + 2:
                        i = n - 2
                        pe.wait_ge(exped, item0 + i + 1)
                        transposes(tp0 + i, [prob_b[:, i % 3, j * P:(j + 1) * P] for j in range(3)])
                    if n >= 3:
                        i = n - 3
                        step, r = divmod(i, R)
                        pe.wait_ge(*emptied(tp0 + i))
                        if r == 0 and step >= 2:
                            pe.wait_ge(pv_empty, step0 + step - 1)
                        bank = lin[step % 2]
                        pt = prob_tb[:, i % 2, :]
                        nc.tensor.matmul(bank[:, r * DH:(r + 1) * DH], pt[:, 0:P], v_of(i, 0),
                                         start=True, stop=True)
                        lo = (R + r) * DH
                        nc.tensor.matmul(bank[:, lo:lo + DH], pt[:, P:2 * P], v_of(i, 0), start=True, stop=False)
                        ins = nc.tensor.matmul(bank[:, lo:lo + DH], pt[:, 2 * P:3 * P], v_of(i, 1),
                                               start=False, stop=True)
                        if r == R - 1:
                            ins.then_inc(pv_done, 1)

            def feed_forward(up, down, unit0, tp0, tp_h, at_start=lambda: None, at_end=lambda: None,
                             in_down=lambda: None):
                hid0 = stationary_number(tp0)
                wait_st = st_wait(tp_h, x_batch)

                def one(u, i=None):
                    wait_unit(unit0 + u, i)
                    for q in range(4):
                        s = up + 4 * u + q
                        pe.wait_ge(lo_ready, at(i, s + 1, 8))
                        for j in range(2):
                            k = 2 * q + j
                            if u == 0 and i is None:
                                wait_st(k)
                            for t, (ah, al) in enumerate(stationary(k)):
                                ins = three(lin[2 * ((unit0 + u) % 2) + t][:], ah, al,
                                            w_hi[:, s % RING, 512 * j:512 * j + 512],
                                            w_lo[:, s % RING, 512 * j:512 * j + 512], k == 0, k == KD - 1)
                        ins.then_inc(slot_used, 1)
                        if q == 1 and (u > 0 or i is not None):
                            hidden(u - 1, i)

                def hidden(u, i=None):
                    batch = tp0 + u
                    pe.wait_ge(unit_empty_dve, at(i, count_before(UNIT_EMPTIED, unit0 + u + 1, "dve"), 2))
                    empty, value = emptied(batch - 2)
                    pe.wait_ge(empty, at(i, value, 2))
                    for n in range(4):
                        k, t = divmod(n, 2)
                        ins = nc.tensor.transpose(tp[batch % 2][:, n * P:(n + 1) * P],
                                                  hid[:, u % 2, t, k * P:(k + 1) * P], ident[:])
                    ins.then_inc(tp_filled, 1)

                for u in range(3):
                    one(u)
                at_start()
                with pe.Fori(0, (FU - 5) // 2) as i:
                    one(3, i)
                    one(4, i)
                at_end()
                one(FU - 2)
                one(FU - 1)
                def down_product(k, ns, tiles=range(T)):
                    for t in tiles:
                        c0 = k * S + t * P
                        for n in ns:
                            s = down + k
                            ins = three(lin[2 * ((unit0 + FU + n) % 2) + t][:], hid_hi[:, c0:c0 + P],
                                        hid_lo[:, c0:c0 + P], w_hi[:, s % RING, 512 * n:512 * n + 512],
                                        w_lo[:, s % RING, 512 * n:512 * n + 512], k == 0, k == FK - 1)
                    return ins

                wait_unit(unit0 + FU)
                for k in range(DOWN_AHEAD):
                    pe.wait_ge(lo_ready, down + k + 1)
                    pe.wait_ge(st_ready, hid0 + k // 2 + 1)
                    down_product(k, [0])
                wait_unit(unit0 + FU + 1)
                for k in range(FK - RING):
                    if k < DOWN_AHEAD:
                        down_product(k, [1]).then_inc(slot_used, 1)
                    else:
                        pe.wait_ge(lo_ready, down + k + 1)
                        pe.wait_ge(st_ready, hid0 + k // 2 + 1)
                        down_product(k, range(2)).then_inc(slot_used, 1)
                    if k == 1:
                        hidden(FU - 1)
                    if k == 15:
                        in_down()
                for k in range(FK - RING, FK):
                    pe.wait_ge(lo_ready, down + k + 1)
                    pe.wait_ge(st_ready, hid0 + k // 2 + 1)
                    ins = down_product(k, [0])
                ins.then_inc(part_done, 1)
                for k in range(FK - RING, FK):
                    ins = down_product(k, [1], [0])
                ins.then_inc(part_done, 1)
                for k in range(FK - RING, FK):
                    down_product(k, [1], [1]).then_inc(slot_used, 1)

            pe.wait_ge(consts, 1)
            pe.wait_ge(first_bias, 16)
            for seg in range(2):
                for k in range(KD):
                    nc.tensor.matmul(sc[seg][:, k:k + 1], gate_rows[0:1, seg, k * P:(k + 1) * P],
                                     ones[0:1, 0:1], start=(k == 0), stop=False)

            x_batch(T_H0, 0)
            x_batch(T_H0, 1)
            pe.wait_ge(ada_used, 2 * KD)
            reduce_columns(0)
            reduce_columns(1)
            KT16 = [[0, 1, 2, 3], [4, 5, 6, 7], [8, 9, 10, 11], [12, 13, 14, 15]]

            def compress(b, u, s0, among=None):
                pe.wait_ge(a_ready, b + 1)
                unit(u, s0, KT16, CH, lambda k: [(a_hi[:, k, :], a_lo[:, k, :])], among)

            unit(U_KVC, KVC0, FOUR, 512, stationary, st_wait(T_H0, x_batch))
            unit(U_KVS, KVS0, FOUR, 512, stationary)
            pe.wait_ge(unit_empty_act, 1)
            for b in range(2):
                c0 = 1024 + 256 * b
                transposes(T_KVC + b, [proj[:, t, c0 + P * j:c0 + P * (j + 1)]
                                       for j in range(2) for t in range(T)])
            unit(U_KVW, KVW0, FOUR, 512, stationary)

            def transposed_keys(b):
                next_tokens()
                for m in range(2):
                    transposes(T_K + 2 * b + m, [kdup_o[:, b, t * 512 + g * P:t * 512 + (g + 1) * P]
                                                 for g in (2 * m, 2 * m + 1) for t in range(T)])

            def transposed_queries(part, batch0):
                next_tokens()
                for m in range(2):
                    transposes(batch0 + m, [proj[:, t, k * P:(k + 1) * P]
                                            for k in (4 * part + 2 * m, 4 * part + 2 * m + 1) for t in range(T)])

            def transposed_hidden(b, batch):
                pe.wait_ge(unit_empty_act, (U_CMPK, U_CMPV)[b] + 1)
                transposes(batch, [tfull[:, 0, (2 * b + j) * P:(2 * b + j + 1) * P] for j in range(2)])

            def compressed(b, batch, hidden_batch):
                pe.wait_ge(*emptied(hidden_batch))
                wait_tp(batch)
                for k in range(2):
                    ins = nc.tensor.matmul(tp[batch % 2][:, 0:DH], sc_t[:, (2 * b + k) * P:(2 * b + k + 1) * P],
                                           w2[:, b, k, :], start=(k == 0), stop=(k == 1))
                ins.then_inc(tp_filled, 1)

            transposed_keys(0)
            unit(U_QA, QA0, FOUR, 512, stationary)
            transposed_keys(1)
            wait_unit(U_GATE)
            for k in range(KD):
                q, j = divmod(k, 4)
                s = GATE0 + q
                if j == 0:
                    pe.wait_ge(lo_ready, s + 1)
                wh, wl = (w[:, s % RING, j * NG:(j + 1) * NG] for w in (w_hi, w_lo))
                bank = lin[2 * (U_GATE % 2)][0:NG, 0:S]
                nc.tensor.matmul(bank, wh, st_hi[:, k, :], start=(k == 0), stop=False)
                nc.tensor.matmul(bank, wl, st_hi[:, k, :], start=False, stop=False)
                ins = nc.tensor.matmul(bank, wh, st_lo[:, k, :], start=False, stop=(k == KD - 1))
                if j == 3:
                    ins.then_inc(slot_used, 1)
            compress(0, U_CMPK, CMPK0)
            wait_tp(T_G)
            pe.wait_ge(unit_empty_act, U_GATE + 1)
            for t in range(T):
                ins = nc.tensor.transpose(tp[T_G % 2][:, t * NG:(t + 1) * NG], gates_t[:, t * P:(t + 1) * P],
                                          ident[0:NG, 0:NG])
            ins.then_inc(tp_filled, 1)
            unit(U_QB, QB0, FOUR, 512, stationary)
            transposed_queries(0, T_QA)

            def keys_of_hidden(k):
                if k == 8:
                    transposed_hidden(0, T_SCK)
                elif k == 12:
                    compressed(0, T_CK, T_SCK)

            compress(1, U_CMPV, CMPV0, keys_of_hidden)
            transposed_queries(1, T_QB)
            reduce_row(2)
            transposed_hidden(1, T_SCV)
            next_tokens()
            transposes(T_KC, [scratch[:, 2 * DH:4 * DH]])
            compressed(1, T_CV, T_SCV)
            pe.wait_ge(*emptied(T_KC))
            for t in range(T):
                nc.tensor.matmul(lin[t][:].rearrange("p (u c) -> p u c", u=2), ident_b[:],
                                 cmp_mask[:, t, :].unsqueeze(1).broadcast_to([P, 2, H // 2 * CP]),
                                 start=True, stop=False)
                out_view = lin[t][:].rearrange("p (r u g c) -> p r u g c", r=2, u=2, g=G)
                for pair in range(R // 2):
                    for g in range(G):
                        ins = nc.tensor.matmul(out_view[:, pair, :, g, :],
                                               q_t[:, 2 * g + pair, t * P:(t + 1) * P], kc_t[:, :, g, :],
                                               start=False, stop=(pair == 1 and g == G - 1))
                ins.then_inc(cmp_scored, 1)
                if t == 0:
                    reduce_columns(3)
            pe.wait_ge(ada_out, 4)

            def compressed_values(n):
                if n == 2:
                    for t in range(T):
                        pe.wait_ge(cmp_exped, t + 1)
                        transposes(T_PC + t, [tfull[:, t, j * P:(j + 1) * P] for j in range(4)])
                    for j in range(8):
                        t, pair, u = j // 4, j // 2 % 2, j % 2
                        if j % 4 == 0:
                            pe.wait_ge(*emptied(T_PC + t))
                        ins = nc.tensor.matmul(CMP_BANKS[j // 2][:, u * 256:(u + 1) * 256],
                                               probc_t[:, t, (j % 4) * P:(j % 4 + 1) * P],
                                               v_cmp[:].rearrange("p g d -> p (g d)"), start=True, stop=True)
                        if u == 1:
                            ins.then_inc(cmp_pv, 1)
                if n in (2, 3):
                    pe.wait_ge(cmp_added, n - 1 if n == 2 else 4)

            def item_head(n):
                step, r = divmod(n, R)
                g, b = divmod(step, 2)
                return g, b, R * g + r

            def nsa_q(n, t):
                g, b, h = item_head(n)
                return q_t[:, h // 2, t * P:(t + 1) * P]

            def nsa_k(n, tiles):
                g, b, h = item_head(n)
                return k_t[h % 2][:, b, g, 0:tiles * P]

            def nsa_v(n, t):
                g, b, h = item_head(n)
                c0 = 1792 + 512 * b + g * DH
                return proj[:, t, c0:c0 + DH]

            attention(2 * H, 0, T_P0, 0, nsa_q, nsa_k, nsa_v, prob, prob_t, compressed_values)
            pe.wait_ge(o_steps, 8)
            for m in range(2):
                o_batch(o0)(T_O0, m)
            unit(U_OUT0, OUT0, FOUR, 512, stationary, st_wait(T_O0, o_batch(o0)))
            reduce_columns(4)
            last_unit(U_OUT0 + 1, OUT0 + 4)
            reduce_row(5)
            for m in range(2):
                x_batch(T_HF0, m)

            feed_forward(UP0, DOWN0, U_UP0, T_HID0, T_HF0, lambda: reduce_columns(6),
                         lambda: reduce_columns(7), lambda: reduce_row(8))

            reduce_columns(9)
            for m in range(2):
                x_batch(T_H1, m)
            unit(U_IN1, IN1, FOUR, KVL + ROT, stationary, st_wait(T_H1, x_batch))

            def latent_transposes(m):
                k0, nk = LATENTS[m]
                transposes(T_CQ + m, [proj1[:, t, k * P:(k + 1) * P] for k in range(k0, k0 + nk)
                                      for t in range(T)])

            def key_value_latent(k):
                if k == 6:
                    next_tokens()
                    latent_transposes(0)

            unit(U_IN1 + 1, INB1, FOUR, QL, stationary, key_value_latent)
            reduce_columns(10)
            pe.wait_ge(*emptied(T_CQ))
            for u in range(4):
                if u == 2:
                    next_tokens()
                    latent_transposes(1)
                    latent_transposes(2)
                unit(U_KVB1 + u, KVB1 + u, [[3, 4]], 512, stationary)

            def key_transposes(first, last):
                for j in range(first, last):
                    transposes(T_K1 + j, [k_tok[:, t, h, :] for h in (2 * j, 2 * j + 1)
                                          for t in range(T)], DQ)

            pe.wait_ge(*emptied(T_CQ + 2))
            for u in range(4):
                if u == 3:
                    next_tokens()
                    key_transposes(0, 2)
                unit(U_QB1 + u, QB1 + 2 * u, [[0, 1], [2]], QU, stationary)
            key_transposes(2, 8)
            for u in range(4):
                if u % 2 == 0:
                    pe.wait_ge(q_rotated, u // 2 + 1)
                else:
                    next_tokens()
                for j in (2 * u, 2 * u + 1):
                    transposes(T_Q1 + j, [q_tok[:, t, h * DQ:(h + 1) * DQ] for h in (2 * j, 2 * j + 1)
                                          for t in range(T)], DQ)
            pe.wait_ge(*emptied(T_P1 - 2))
            pe.wait_ge(pads_zero, 1)
            pe.wait_ge(*emptied(T_P1 - 1))
            pe.wait_ge(ada_out, 11)
            attention(H, 2 * H, T_P1, 8,
                      lambda n, t: q1_t[:, n, t * P:(t + 1) * P],
                      lambda n, tiles: k1_t[:, n, 0:tiles * P],
                      lambda n, t: v_tok[:, t, n, :], prob1, prob1_t)
            pe.wait_ge(pv_empty, 8 + 4)
            for m in range(2):
                o_batch(o1)(T_O1, m)
            unit(U_OUT1, OUT1, FOUR, 512, stationary, st_wait(T_O1, o_batch(o1)))
            last_unit(U_OUT1 + 1, OUT1 + 4)
            reduce_row(11)
            for m in range(2):
                x_batch(T_HF1, m)
            feed_forward(UP1, DOWN1, U_UP1, T_HID1, T_HF1)


_INS = ['x', 'c', 'positions', 'ada_w', 'ada_b', 'norm_mix', 'norm_ffn', 'ffn_w_in', 'ffn_w_out',
        'nsa_w_in', 'nsa_q_norm', 'nsa_k_norm', 'nsa_cmp_pe', 'nsa_cmp_w1', 'nsa_cmp_w2', 'nsa_w_out',
        'mla_w_in', 'mla_q_a_norm', 'mla_kv_a_norm', 'mla_w_q_b', 'mla_w_kv_b', 'mla_q_norm',
        'mla_k_norm', 'mla_w_out']


def kernel(**inputs):
    import concourse.bacc as bacc
    from concourse.bass_utils import run_bass_kernel_spmd

    nc = bacc.Bacc("TRN2", target_bir_lowering=False, num_devices=1)
    arrays, args = {}, []
    for name in _INS:
        a = np.ascontiguousarray(inputs[name])
        arrays[f"in_{name}_dram"] = a
        args.append(nc.dram_tensor(f"in_{name}_dram", a.shape, mybir.dt.from_np(a.dtype),
                                   kind="ExternalInput").ap())
    args.append(nc.dram_tensor("out_0_dram", (1, S, D), F32, kind="ExternalOutput").ap())
    trunk(nc, *args)
    r = run_bass_kernel_spmd(nc, [arrays], core_ids=[0])
    return r.results[0]["out_0_dram"]
```
